# Optimizing a Trainium2 kernel written in Bass

```python
import math
import jax
import jax.numpy as jnp
from jax import lax
import numpy as np

D_MODEL = 1024
BATCH = 1
SEQ = 256
DEPTH = 1

SSM_WIDTH = D_MODEL // 2
SSM_GROUP = 16
SSM_GROUPS = SSM_WIDTH // SSM_GROUP
SSM_STATE = 64
DT_MIN = 1e-3
DT_MAX = 1e-1
ATTN_HEADS = 8
HEAD_DIM = 64
ATTN_WIDTH = ATTN_HEADS * HEAD_DIM
MOBA_BLOCK = 256
MOBA_TOPK = 3
Q_CHUNK = 64
ROPE_THETA = 500000.0
ROT_DIM = HEAD_DIM // 4
IN_WIDTH = SSM_WIDTH + 3 * ATTN_WIDTH + 2 * D_MODEL
N_EXPERTS = 32
TOP_K = 4
D_FF = D_MODEL
SWIGLU_LIMIT = 7.0
SWIGLU_ALPHA = 1.702
EXPERT_ROWS = 256
RMS_EPS = 1e-5

kernel_name = 'hybrid_s5_moba_moe_block'

def rms_norm(x, g):
    xf = x.astype(jnp.float32)
    r = lax.rsqrt(jnp.mean(xf * xf, axis=-1, keepdims=True) + RMS_EPS)
    return (xf * r * g.astype(jnp.float32)).astype(x.dtype)

def modulate(h, shift, scale):
    return h * (1.0 + scale[:, None, :]) + shift[:, None, :]

def rotary_tables(seq):
    inv_freq = 1.0 / (ROPE_THETA ** (jnp.arange(0, ROT_DIM, 2, dtype=jnp.float32) / ROT_DIM))
    ang = jnp.arange(seq, dtype=jnp.float32)[:, None] * inv_freq[None, :]
    return jnp.cos(ang), jnp.sin(ang)

def partial_rotary(t, cos, sin):
    half = ROT_DIM // 2
    t1 = t[..., :half].astype(jnp.float32)
    t2 = t[..., half:ROT_DIM].astype(jnp.float32)
    r1 = (t1 * cos - t2 * sin).astype(t.dtype)
    r2 = (t2 * cos + t1 * sin).astype(t.dtype)
    return jnp.concatenate([r1, r2, t[..., ROT_DIM:]], axis=-1)

def to_heads(t):
    b, s, _ = t.shape
    return t.reshape(b, s, ATTN_HEADS, HEAD_DIM).transpose(0, 2, 1, 3)

def s5_mixer(u, a_re, a_im, log_dt, b_re, b_im, c_re, c_im, d_skip):
    bsz, s, _ = u.shape
    f32 = jnp.float32
    uf = u.astype(f32).reshape(bsz, s, SSM_GROUPS, SSM_GROUP)
    dt = jnp.exp(log_dt.astype(f32))[:, None]
    lr = a_re.astype(f32)
    li = a_im.astype(f32)
    mag = jnp.exp(lr * dt)
    abar_r = mag * jnp.cos(li * dt)
    abar_i = mag * jnp.sin(li * dt)
    den = lr * lr + li * li
    coef_r = ((abar_r - 1.0) * lr + abar_i * li) / den
    coef_i = (abar_i * lr - (abar_r - 1.0) * li) / den
    br = b_re.astype(f32)
    bi = b_im.astype(f32)
    bbar_r = coef_r[..., None] * br - coef_i[..., None] * bi
    bbar_i = coef_r[..., None] * bi + coef_i[..., None] * br
    bu_r = jnp.einsum('bsgc,gpc->bsgp', uf, bbar_r)
    bu_i = jnp.einsum('bsgc,gpc->bsgp', uf, bbar_i)
    a_r = jnp.broadcast_to(abar_r[None, None], (1, s, SSM_GROUPS, SSM_STATE))
    a_i = jnp.broadcast_to(abar_i[None, None], (1, s, SSM_GROUPS, SSM_STATE))

    def combine(e1, e2):
        a1r, a1i, b1r, b1i = e1
        a2r, a2i, b2r, b2i = e2
        return (a2r * a1r - a2i * a1i,
                a2r * a1i + a2i * a1r,
                a2r * b1r - a2i * b1i + b2r,
                a2r * b1i + a2i * b1r + b2i)

    _, _, xr, xi = lax.associative_scan(combine, (a_r, a_i, bu_r, bu_i), axis=1)
    y = (jnp.einsum('gcp,bsgp->bsgc', c_re.astype(f32), xr)
         - jnp.einsum('gcp,bsgp->bsgc', c_im.astype(f32), xi))
    y = y.reshape(bsz, s, SSM_WIDTH) + d_skip.astype(f32) * uf.reshape(bsz, s, SSM_WIDTH)
    return y.astype(u.dtype)

def moba_attention(q, k, v):
    bsz, nh, s, dh = q.shape
    f32 = jnp.float32
    nb = -(-s // MOBA_BLOCK)
    pad = nb * MOBA_BLOCK - s
    kb = jnp.pad(k, ((0, 0), (0, 0), (0, pad), (0, 0))).reshape(bsz, nh, nb, MOBA_BLOCK, dh)
    vb = jnp.pad(v, ((0, 0), (0, 0), (0, pad), (0, 0))).reshape(bsz, nh, nb, MOBA_BLOCK, dh)
    k_mean = jnp.mean(kb.astype(f32), axis=3)
    pos = jnp.arange(s)
    n_past = pos // MOBA_BLOCK
    gate = jnp.einsum('bhsd,bhnd->bhsn', q.astype(f32), k_mean)
    past = jnp.arange(nb)[None, :] < n_past[:, None]
    gate = jnp.where(past, gate, -jnp.inf)
    n_sel = min(MOBA_TOPK, nb)
    _, sel = lax.top_k(gate, n_sel)
    sel_ok = sel < n_past[:, None]
    n_chunks = s // Q_CHUNK

    def to_chunks(t):
        return jnp.moveaxis(t.reshape(bsz, nh, n_chunks, Q_CHUNK, t.shape[-1]), 2, 0)

    b_ix = jnp.arange(bsz)[:, None, None, None]
    h_ix = jnp.arange(nh)[None, :, None, None]
    scale = dh ** -0.5
    n_sel_keys = n_sel * MOBA_BLOCK

    def chunk(args):
        ci, qc, selc, okc = args
        q0 = ci * Q_CHUNK
        own = q0 // MOBA_BLOCK
        k_own = lax.dynamic_index_in_dim(kb, own, axis=2, keepdims=False)
        v_own = lax.dynamic_index_in_dim(vb, own, axis=2, keepdims=False)
        k_sel = kb[b_ix, h_ix, selc]
        v_sel = vb[b_ix, h_ix, selc]
        s_sel = jnp.einsum('bhqd,bhqnkd->bhqnk', qc, k_sel).astype(f32) * scale
        s_sel = jnp.where(okc[..., None], s_sel, -jnp.inf)
        s_own = jnp.einsum('bhqd,bhkd->bhqk', qc, k_own).astype(f32) * scale
        qpos = q0 + jnp.arange(Q_CHUNK)
        kpos = own * MOBA_BLOCK + jnp.arange(MOBA_BLOCK)
        s_own = jnp.where(kpos[None, :] <= qpos[:, None], s_own, -jnp.inf)
        sc = jnp.concatenate([s_sel.reshape(bsz, nh, Q_CHUNK, n_sel_keys), s_own], axis=-1)
        p = jax.nn.softmax(sc, axis=-1).astype(v.dtype)
        p_sel = p[..., :n_sel_keys].reshape(bsz, nh, Q_CHUNK, n_sel, MOBA_BLOCK)
        p_own = p[..., n_sel_keys:]
        return (jnp.einsum('bhqnk,bhqnkd->bhqd', p_sel, v_sel)
                + jnp.einsum('bhqk,bhkd->bhqd', p_own, v_own))

    out = lax.map(chunk, (jnp.arange(n_chunks), to_chunks(q), to_chunks(sel), to_chunks(sel_ok)))
    return jnp.moveaxis(out, 0, 2).reshape(bsz, nh, s, dh)

def moe_ffn(h, w_router, b_router, w_gu, b_gu, w_down, b_down):
    bsz, s, dm = h.shape
    n = bsz * s
    hf = h.reshape(n, dm)
    logits = (hf @ w_router + b_router).astype(jnp.float32)
    top_vals, top_idx = lax.top_k(logits, TOP_K)
    top_w = jax.nn.softmax(top_vals, axis=-1)
    nk = n * TOP_K
    flat_e = top_idx.reshape(nk)
    flat_t = jnp.arange(nk, dtype=jnp.int32) // TOP_K
    flat_w = top_w.reshape(nk)
    order = jnp.argsort(flat_e)
    sorted_e = flat_e[order]
    counts = jnp.bincount(flat_e, length=N_EXPERTS)
    group_start = jnp.cumsum(counts) - counts
    padded = (counts + EXPERT_ROWS - 1) // EXPERT_ROWS * EXPERT_ROWS
    padded_end = jnp.cumsum(padded)
    padded_start = padded_end - padded
    n_blocks = -(-nk // EXPERT_ROWS) + N_EXPERTS
    rows_total = n_blocks * EXPERT_ROWS
    dest = padded_start[sorted_e] + jnp.arange(nk, dtype=jnp.int32) - group_start[sorted_e]
    row_tok = jnp.full((rows_total,), n, dtype=jnp.int32).at[dest].set(flat_t[order])
    row_w = jnp.zeros((rows_total,), jnp.float32).at[dest].set(flat_w[order])
    blk_e = jnp.minimum(jnp.searchsorted(padded_end, jnp.arange(n_blocks) * EXPERT_ROWS, side='right'),
                        N_EXPERTS - 1)
    h_pad = jnp.concatenate([hf, jnp.zeros((1, dm), hf.dtype)], axis=0)

    def expert_block(args):
        e, tok, wt = args
        xb = h_pad[tok]
        gu = xb @ w_gu[e] + b_gu[e]
        gate = jnp.minimum(gu[:, :D_FF], SWIGLU_LIMIT)
        up = jnp.clip(gu[:, D_FF:], -SWIGLU_LIMIT, SWIGLU_LIMIT)
        act = (up + 1.0) * gate * jax.nn.sigmoid(SWIGLU_ALPHA * gate)
        y = act @ w_down[e] + b_down[e]
        return y * wt[:, None].astype(y.dtype)

    rows = lax.map(expert_block, (blk_e, row_tok.reshape(n_blocks, EXPERT_ROWS),
                                  row_w.reshape(n_blocks, EXPERT_ROWS)))
    out = jnp.zeros((n + 1, dm), rows.dtype).at[row_tok].add(rows.reshape(rows_total, dm))[:n]
    return out.reshape(bsz, s, dm).astype(h.dtype)

def setup_inputs(seed: int = 0) -> dict:
    key = jax.random.key(seed)
    ks = jax.random.split(key, 32)
    f32 = jnp.float32
    L, D, G, P, C = DEPTH, D_MODEL, SSM_GROUPS, SSM_STATE, SSM_GROUP

    def nrm(k, shape, scale):
        return jax.random.normal(k, shape, f32) * scale

    u01 = jax.random.uniform(ks[8], (L, G), f32)
    return {
        'x': nrm(ks[0], (BATCH, SEQ, D), 1.0),
        'c': nrm(ks[1], (BATCH, D), 1.0),
        'w_ada': nrm(ks[2], (L, D, 6 * D), D ** -0.5),
        'b_ada': nrm(ks[3], (L, 6 * D), 0.01),
        'g_mix': 1.0 + nrm(ks[4], (L, D), 0.01),
        'w_in': nrm(ks[5], (L, D, IN_WIDTH), D ** -0.5),
        'ssm_a_re': -0.5 + nrm(ks[6], (L, G, P), 0.01),
        'ssm_a_im': math.pi * jnp.arange(P, dtype=f32) + nrm(ks[7], (L, G, P), 0.01),
        'ssm_log_dt': math.log(DT_MIN) + u01 * (math.log(DT_MAX) - math.log(DT_MIN)),
        'ssm_b_re': nrm(ks[9], (L, G, P, C), (2 * C) ** -0.5),
        'ssm_b_im': nrm(ks[10], (L, G, P, C), (2 * C) ** -0.5),
        'ssm_c_re': nrm(ks[11], (L, G, C, P), (2 * P) ** -0.5),
        'ssm_c_im': nrm(ks[12], (L, G, C, P), (2 * P) ** -0.5),
        'ssm_d': nrm(ks[13], (L, SSM_WIDTH), 1.0),
        'w_glu': nrm(ks[14], (L, SSM_WIDTH, 2 * D), SSM_WIDTH ** -0.5),
        'w_attn_o': nrm(ks[15], (L, ATTN_WIDTH, D), ATTN_WIDTH ** -0.5),
        'w_out': nrm(ks[16], (L, D, D), D ** -0.5),
        'g_ffn': 1.0 + nrm(ks[17], (L, D), 0.01),
        'w_router': nrm(ks[18], (L, D, N_EXPERTS), D ** -0.5),
        'b_router': nrm(ks[19], (L, N_EXPERTS), 0.01),
        'w_gu': nrm(ks[20], (L, N_EXPERTS, D, 2 * D_FF), D ** -0.5),
        'b_gu': nrm(ks[21], (L, N_EXPERTS, 2 * D_FF), 0.01),
        'w_down': nrm(ks[22], (L, N_EXPERTS, D_FF, D), D_FF ** -0.5),
        'b_down': nrm(ks[23], (L, N_EXPERTS, D), 0.01),
        'g_final': 1.0 + nrm(ks[24], (D,), 0.01),
    }

def reference(x, c, w_ada, b_ada, g_mix, w_in, ssm_a_re, ssm_a_im, ssm_log_dt, ssm_b_re, ssm_b_im,
              ssm_c_re, ssm_c_im, ssm_d, w_glu, w_attn_o, w_out, g_ffn, w_router, b_router,
              w_gu, b_gu, w_down, b_down, g_final):
    s = x.shape[1]
    cos, sin = rotary_tables(s)
    cond = jax.nn.silu(c)
    splits = [SSM_WIDTH, SSM_WIDTH + ATTN_WIDTH, SSM_WIDTH + 2 * ATTN_WIDTH,
              SSM_WIDTH + 3 * ATTN_WIDTH, SSM_WIDTH + 3 * ATTN_WIDTH + D_MODEL]
    for l in range(DEPTH):
        mod = cond @ w_ada[l] + b_ada[l]
        sh1, sc1, gt1, sh2, sc2, gt2 = jnp.split(mod, 6, axis=-1)
        h = modulate(rms_norm(x, g_mix[l]), sh1, sc1)
        proj = h @ w_in[l]
        u, q, k, v, ga, gb = jnp.split(proj, splits, axis=-1)
        y_ssm = s5_mixer(u, ssm_a_re[l], ssm_a_im[l], ssm_log_dt[l], ssm_b_re[l], ssm_b_im[l],
                         ssm_c_re[l], ssm_c_im[l], ssm_d[l])
        glu = jax.nn.gelu(y_ssm) @ w_glu[l]
        y_a = glu[..., :D_MODEL] * jax.nn.sigmoid(glu[..., D_MODEL:])
        qh = partial_rotary(to_heads(q), cos, sin)
        kh = partial_rotary(to_heads(k), cos, sin)
        o = moba_attention(qh, kh, to_heads(v))
        o = o.transpose(0, 2, 1, 3).reshape(x.shape[0], s, ATTN_WIDTH)
        y_b = o @ w_attn_o[l]
        merged = jax.nn.sigmoid(ga) * y_a + jax.nn.sigmoid(gb) * y_b
        x = x + gt1[:, None, :] * (merged @ w_out[l])
        h2 = modulate(rms_norm(x, g_ffn[l]), sh2, sc2)
        x = x + gt2[:, None, :] * moe_ffn(h2, w_router[l], b_router[l], w_gu[l], b_gu[l],
                                          w_down[l], b_down[l])
    return rms_norm(x, g_final)


_drawn_inputs = setup_inputs


def setup_inputs(seed=0):
    import zlib

    import numpy as np

    out = dict(_drawn_inputs(seed))
    spreads = {}
    factors = {'g_mix': 6.193,
     'ssm_a_re': 64.0,
     'ssm_log_dt': 20.947,
     'ssm_b_re': 22.472,
     'ssm_b_im': 32.195,
     'ssm_c_re': 25.152,
     'ssm_c_im': 22.018,
     'b_gu': 40.565,
     'b_down': 56.534,
     'g_final': 33.396,
     'ssm_a_im': 5.989,
     'g_ffn': 6.719,
     'b_router': 6.316}
    for name, (base, spread) in spreads.items():
        noise = np.random.default_rng([zlib.crc32(name.encode()), seed]).standard_normal(out[name].shape)
        drawn = base * np.exp(spread * noise) if base else spread * noise
        out[name] = jnp.asarray(drawn.astype(out[name].dtype))
    for name, factor in factors.items():
        out[name] = (out[name] * factor).astype(out[name].dtype)
    return out
```

```python
from contextlib import ExitStack

import numpy as np

import concourse.bass as bass
from concourse import mybir

F32 = mybir.dt.float32
I32 = mybir.dt.int32
ALU = mybir.AluOpType
ACT = mybir.ActivationFunctionType
AX = mybir.AxisListType

P = 128
D = 1024
T = 256
TT = T // P
KD = D // P
W = D // 2
KW = W // P
HEADS, HD = 8, 64
G, N, C = 32, 64, 16
ST = G * N // P
EXPERTS, TOPK = 32, 4
CAP = 64
OVER = 15
ITEMS = EXPERTS + OVER
COLS = ITEMS + 2
SLOTS = 12
SLOT = 2048
EPS = 1e-5
LIMIT, ALPHA = 7.0, 1.702
THETA = 500000.0
HALF = HD // 8
TWO_PI = 2.0 * np.pi
ROUND = 1.5 * 2.0 ** 23

C_ID, C_COS, C_SIN, C_ROT, C_TRI, C_CAUSAL = 0, 128, 384, 640, 768, 896
C_SLOT, C_TRI32, C_ID32, C_Q, C_E, C_MB, C_MC = 1280, 1344, 1376, 1408, 1424, 1425, 1427
C_ALL = 1429
BF16 = mybir.dt.bfloat16
R_C, R_GMIX, R_GFFN, R_ADA, R_D, R_ALL = 0, 8, 16, 24, 72, 76
SH1, SC1, GT1, SH2, SC2, GT2 = (8 * j for j in range(6))


def constants():
    c = np.zeros((P, C_ALL), np.float32)
    p = np.arange(P)
    c[:, C_ID:C_ID + P] = np.eye(P)
    inv = (1.0 / THETA ** (np.arange(0, 2 * HALF, 2, dtype=np.float32) / (2 * HALF))).astype(np.float32)
    ang = np.arange(T, dtype=np.float32)[None, :] * inv[p % HALF][:, None]
    turned = (p % HD < 2 * HALF)[:, None]
    c[:, C_COS:C_COS + T] = np.where(turned, np.cos(ang), 1.0)
    c[:, C_SIN:C_SIN + T] = np.where(turned, np.sin(ang), 0.0)
    for j in range(P):
        if j % HD < HALF:
            c[j + HALF, C_ROT + j] = -1.0
        elif j % HD < 2 * HALF:
            c[j - HALF, C_ROT + j] = 1.0
    c[:, C_TRI:C_TRI + P] = p[:, None] < p[None, :]
    past = np.where(p[None, :] <= p[:, None], 0.0, -1e30)
    c[:, C_CAUSAL:C_CAUSAL + P] = past
    c[:, C_CAUSAL + 2 * P:C_CAUSAL + 3 * P] = past
    c[:, C_SLOT:C_SLOT + CAP] = np.arange(1, CAP + 1)
    e = np.arange(EXPERTS)
    c[:EXPERTS, C_TRI32:C_TRI32 + EXPERTS] = e[:, None] <= e[None, :]
    c[:EXPERTS, C_ID32:C_ID32 + EXPERTS] = np.eye(EXPERTS)
    c[:, C_Q:C_Q + OVER + 1] = np.arange(OVER + 1)
    c[:EXPERTS, C_E] = e
    c[:, C_MB:C_MB + 2] = (p // N)[:, None] == np.arange(2)
    c[:, C_MC:C_MC + 2] = (p % (2 * C) // C)[:, None] == np.arange(2)
    return c


def build(nc, x, c, w_ada, b_ada, g_mix, w_in, a_re, a_im, log_dt, b_re, b_im, c_re, c_im, ssm_d,
          w_glu, w_attn_o, w_out, g_ffn, w_router, b_router, w_gu, b_gu, w_down, b_down, g_final,
          const, out):
    ctx = ExitStack()

    def sb(name, shape, dt=F32):
        return ctx.enter_context(nc.sbuf_tensor(name, shape, dt))

    def sem(name):
        return ctx.enter_context(nc.semaphore(name))

    ring = sb("ring", [P, SLOTS, SLOT])
    x_tok = sb("x_tok", [P, TT, D])
    xn_tok = sb("xn_tok", [P, TT, D])
    hT = sb("hT", [P, KD, T])
    cst = sb("cst", [P, C_ALL])
    ones = sb("ones", [P, P])
    cols = sb("cols", [P, R_ALL])
    mod = sb("mod", [P, 6 * KD])
    scale1 = sb("scale1", [P, KD])
    scale2 = sb("scale2", [P, KD])
    cond = sb("cond", [P, KD])
    condb = sb("condb", [P, KD, 32])
    stat = sb("stat", [P, 4, TT])
    ident = cst[:, C_ID:C_ID + P]

    zone = sb("zone", [P, 19456])
    at = [0]

    def cut(n):
        at[0] += n
        assert at[0] <= zone.shape[1]
        return zone[:, at[0] - n:at[0]]

    ecos = cut(ST * T).rearrange("p (s t) -> p s t", s=ST)
    esin = cut(ST * T).rearrange("p (s t) -> p s t", s=ST)
    uT = cut(KW * T).rearrange("p (m t) -> p m t", m=KW)
    qT = cut(KW * T).rearrange("p (m t) -> p m t", m=KW)
    kT = cut(KW * T).rearrange("p (m t) -> p m t", m=KW)
    oT = cut(KW * T).rearrange("p (m t) -> p m t", m=KW)
    v_tok = cut(TT * W).rearrange("p (i n) -> p i n", i=TT)
    gaT = xn_tok[:, :, :].rearrange("p i d -> p (i d)").rearrange("p (m t) -> p m t", m=KD)
    gbT = cut(KD * T).rearrange("p (m t) -> p m t", m=KD)
    z = cut(4 * 512).rearrange("p (b r n) -> p b r n", b=2, r=2)
    BT = cut(2 * KW * P).rearrange("p (r m n) -> p r m n", r=2, m=KW)
    CT = cut(2 * KW * P).rearrange("p (r m n) -> p r m n", r=2, m=KW)
    gates = z.rearrange("p b r n -> p (b r n)")
    gate_mix, gate_ffn = gates[:, 0:D], gates[:, D:2 * D]
    xs = sb("xs", [P, 2, 2, 512])
    tmp = sb("tmp", [P, 2, 512])
    ptmp = sb("ptmp", [P, 512])
    modrow = ptmp
    gluT = ecos.rearrange("p s t -> p (s t)")[:, 0:KW * T].rearrange("p (m t) -> p m t", m=KW)
    yaT = ecos.rearrange("p s t -> p (s t)")[:, 1024:3072].rearrange("p (m t) -> p m t", m=KD)
    sigb = ecos.rearrange("p s t -> p (s t)")[:, 3072:4096].rearrange("p (m t) -> p m t", m=KW)
    mergedT = esin.rearrange("p s t -> p (s t)")[:, 0:2048].rearrange("p (m t) -> p m t", m=KD)
    ybT = esin.rearrange("p s t -> p (s t)")[:, 2048:4096].rearrange("p (m t) -> p m t", m=KD)
    prob = tmp[:, :, 0:3 * P]
    probT = xs[:, :, 0, 0:3 * P]
    mx = sb("mx", [P, 2, 4])
    raw = v_tok.rearrange("p i n -> p (i n)")
    are, aim, ldt = raw[0:ST, 0:P], raw[0:ST, P:2 * P], raw[0:ST, 2 * P:2 * P + 2]
    rows = raw[0:R_ALL, 3 * P:4 * P]
    b_in = kT.rearrange("p m t -> p (m t)")[:, 0:512].rearrange("p (r s c) -> p r s c", r=2, s=ST)
    c_in = oT.rearrange("p m t -> p (m t)")[:, 0:512].rearrange("p (r m n) -> p r m n", r=2, m=KW)
    sprow = gbT.rearrange("p m t -> p (m t)")[0:ST, :].rearrange("p (j n) -> p j n", n=P)
    sprm = sb("sprm", [P, 5, ST])
    blk = z.rearrange("p b r n -> p (b r n)")
    Bblk = blk[:, 0:1024].rearrange("p (r s q c) -> p r s q c", r=2, s=ST, q=2)
    Cblk = blk[:, 1024:2048].rearrange("p (r m q n) -> p r m q n", r=2, m=KW, q=2)
    at[0] = 0
    acc = cut(TT * D).rearrange("p (i n) -> p i n", i=TT)
    hg = cut(KD * CAP).rearrange("p (f s) -> p f s", f=KD)
    gate, up, sig = cut(D // 2), cut(D // 2), cut(D // 2)
    act_ = cut(D // 2)
    actT = cut(D // 2).rearrange("p (j h s) -> p j h s", j=4, h=2)
    ysb = cut(D // 2)
    pickw = cut(2 * TT * P).rearrange("p (i h n) -> p i h n", i=TT, h=2)
    pickwT = cut(2 * T).rearrange("p (h t) -> p h t", h=2)
    pick = cut(TT * CAP // 2).bitcast(BF16).rearrange("p (i s) -> p i s", i=TT)
    hotb = cut(CAP)
    bgu_rows = cut(2 * D)
    bdn_rows = cut(D)
    gfin = cut(D)
    xpart = cut(3 * TT * D // 2).bitcast(BF16).rearrange("p (c i d) -> p c i d", c=3, i=TT)
    wr = cut(KD * EXPERTS).rearrange("p (k e) -> p k e", k=KD)
    rowT = cut(2 * T).rearrange("p (j t) -> p j t", j=2)
    assert at[0] <= 4096 * 2 + 1024 * 5 + 2048
    brt = sb("brt", [P, EXPERTS])
    lg = sb("lg", [P, TT, EXPERTS])
    rt = sb("rt", [P, 6, TT, EXPERTS])
    top = sb("top", [P, TT, 8])
    rs = sb("rs", [P, TT, 4])
    chunk = sb("chunk", [EXPERTS, 8])
    gate_rest = zone[:, 0:TT * D].rearrange("p (i d) -> p i d", i=TT)
    hot = sb("hot", [P, 3, 48])
    posI = sb("posI", [P, TT, COLS])
    wI = sb("wI", [P, TT, COLS])
    itab = sb("itab", [1, 48], I32)
    icnt = sb("icnt", [1, 2], I32)
    ps = ctx.enter_context(nc.psum_tensor("ps", [P, 8, 512], F32))

    arrived = [sem(f"arrived{s}") for s in range(SLOTS)]
    w_used = sem("w_used")
    names = """x_in const_in rows_in ssm_in bc_in late_in out_stored
        ones_set cols_up cols_sb cond_set ssm_rows sprm_up sprm_sb Bblk_set Cblk0_set Cblk1_set
        BT_up CT0_up CT1_up BT_sb CT0_sb CT1_sb phases mod_up modrow_sb modT_up mod1_sb sq1 xn1 xT_up h_sb
        proj_up proj_sb bu_up bu_read scanned z_read xs_set xs_read rot_up rot_read rope_set
        sc_up sc_read negmax expd probs probsT_up probsT_sb o_up o_sb mod2_up mod2_sb row_up row_sb y_up y_skip gelu
        sig_ga sig_gb a_up sigb_set ya_set yb_up yb_used merged out_up x1 sq2 xn2 x2T_up h2_sb logit_up
        logit_sb top_set ex_set sel_set pos_up pos_sb rT_up rT_sb extra_set cum_up hot_set item_up item_sb zeroed
        hotb_set bias_up acc_set pick_set hg_up hg_sb gu_up gated sig_set act_set y_dn y_sb pickw_set pwT_up
        pwT_sb actT_up actT_sb comb_up comb_add ysb_zero exp_end fin sq3 fin_out
        dt_set mag_set trig_set lrdt_set angle_set phase_lo pick_half pickw_half hg_half gates_up up_c gate_s xh_set xr_set xm_set x_split
        lnD lnA lnP cond_half""".split()
    S = {n: sem(n) for n in names}

    def linker(eng, s):
        count = [0]

        def link(ins):
            count[0] += 1
            ins.then_inc(s, 1)
            eng.wait_ge(s, count[0])
        return link

    def square(eng, link, n):
        a, b = ecos[:, :, n // 2:n // 2 + 1], esin[:, :, n // 2:n // 2 + 1]
        c1, s1 = ecos[:, :, n + 1:n + 2], esin[:, :, n + 1:n + 2]
        link(eng.tensor_tensor(c1, a, a, ALU.mult))
        link(eng.tensor_tensor(s1, b, b, ALU.mult))
        link(eng.tensor_tensor(ecos[:, :, n:n + 1], c1, s1, ALU.subtract))
        link(eng.tensor_tensor(c1, a, b, ALU.mult))
        link(eng.tensor_tensor(esin[:, :, n:n + 1], c1, c1, ALU.add))

    def double(eng, link, n, scratch):
        w = min(ST, 512 // n)
        for s in range(0, ST, w):
            shape = [P, w, n - 1]
            cn, sn = (e[:, s:s + w, n:n + 1].to_broadcast(shape) for e in (ecos, esin))
            ct, st = ecos[:, s:s + w, 1:n], esin[:, s:s + w, 1:n]
            t0, t1 = (scratch[:, r, 0:w * (n - 1)].rearrange("p (s t) -> p s t", s=w) for r in range(2))
            link(eng.tensor_tensor(t0, ct, cn, ALU.mult))
            link(eng.tensor_tensor(t1, st, sn, ALU.mult))
            link(eng.tensor_tensor(ecos[:, s:s + w, n + 1:2 * n], t0, t1, ALU.subtract))
            link(eng.tensor_tensor(t0, ct, sn, ALU.mult))
            link(eng.tensor_tensor(t1, st, cn, ALU.mult))
            link(eng.tensor_tensor(esin[:, s:s + w, n + 1:2 * n], t0, t1, ALU.add))

    def kp(w):
        return w.rearrange("(k p) n -> p k n", p=P)

    ada, win, glu, wao, wo = kp(w_ada[0]), kp(w_in[0]), kp(w_glu[0]), kp(w_attn_o[0]), kp(w_out[0])
    pieces = [ada[:, k:k + 1, 0:2 * D] for k in range(KD)]
    pieces += [win[:, 4 * h:4 * h + 4, W * g:W * g + W] for g in range(8) for h in range(2)]
    pieces += [ada[:, k:k + 1, 2 * D * j:2 * D * (j + 1)] for j in (1, 2) for k in range(KD)]
    pieces += [glu[:, :, W * j:W * j + W] for j in (0, 2, 1, 3)]
    pieces += [wao[:, :, W * j:W * j + W] for j in range(2)]
    pieces += [wo[:, 2 * j:2 * j + 2, :] for j in range(4)]
    PRE = len(pieces)
    PIECE_ADA1, PIECE_IN, PIECE_ADA2, PIECE_GLU, PIECE_AO, PIECE_OUT = 0, 8, 24, 40, 44, 46
    GU_PIECES, DN_PIECES = 8, 4
    slot_of = [(PRE + j) % SLOTS for j in range(SLOTS)]
    round_of = [(PRE + j) // SLOTS for j in range(SLOTS)]

    def slot(n, k):
        return ring[:, n % SLOTS, :].rearrange("p (k n) -> p k n", k=k)

    with nc.Block() as block:

        @block.sync
        def _(sp):
            sp.dma_start(rows[R_C:R_C + KD, :], c.rearrange("a (k p) -> (a k) p", p=P)).then_inc(S["rows_in"], 16)
            sp.dma_start(rows[R_GMIX:R_GMIX + KD, :], g_mix.rearrange("a (k p) -> (a k) p", p=P)).then_inc(S["rows_in"], 16)
            sp.dma_start(rows[R_GFFN:R_GFFN + KD, :], g_ffn.rearrange("a (k p) -> (a k) p", p=P)).then_inc(S["rows_in"], 16)
            sp.dma_start(rows[R_ADA:R_ADA + 6 * KD, :], b_ada.rearrange("a (k p) -> (a k) p", p=P)).then_inc(S["rows_in"], 16)
            sp.dma_start(rows[R_D:R_D + KW, :], ssm_d.rearrange("a (k p) -> (a k) p", p=P)).then_inc(S["rows_in"], 16)
            sp.dma_start(cst[:, :], const).then_inc(S["const_in"], 16)
            for n, src in enumerate(pieces):
                if n >= SLOTS:
                    sp.wait_ge(w_used, n - SLOTS + 1)
                sp.dma_start(slot(n, src.shape[1]), src).then_inc(arrived[n % SLOTS], 16)
                if n == 1:
                    sp.dma_start(x_tok[:, :, :], x[0].rearrange("(i p) d -> p i d", p=P)).then_inc(S["x_in"], 16)

            def expert_load(item, e):
                gu = w_gu[0, bass.ds(e, 1)].rearrange("e (k p) n -> p (e k) n", p=P)
                dn = w_down[0, bass.ds(e, 1)].rearrange("e (k p) n -> p (e k) n", p=P)
                for j in range(SLOTS):
                    sp.wait_ge(w_used, item * SLOTS + (PRE + j - SLOTS + 1))
                    src = gu[:, j:j + 1, :] if j < GU_PIECES else dn[:, 2 * (j - GU_PIECES):2 * (j - GU_PIECES) + 2, :]
                    sp.dma_start(slot(PRE + j, src.shape[1]), src).then_inc(arrived[slot_of[j]], 16)

            with sp.Fori(0, EXPERTS) as i:
                expert_load(i, i)
            sp.wait_ge(S["item_sb"], 4)
            count = sp.value_load(icnt[0:1, 0:1], min_val=EXPERTS, max_val=ITEMS)
            with sp.Fori(EXPERTS, ITEMS) as i:
                with sp.If(i < count):
                    expert_load(i, sp.value_load(itab[0:1, bass.ds(i, 1)], min_val=0, max_val=EXPERTS - 1))
            sp.wait_ge(S["fin_out"], TT)
            sp.dma_start(out[0].rearrange("(i p) d -> p i d", p=P), x_tok[:, :, :]).then_inc(S["out_stored"], 16)
            sp.wait_ge(S["out_stored"], 16)

        @block.tensor
        def _(pe):
            mm = nc.tensor.matmul

            def take(n):
                pe.wait_ge(arrived[n % SLOTS], 16 * (n // SLOTS + 1))

            pe.wait_ge(S["rows_in"], 80)
            pe.wait_ge(S["const_in"], 16)
            nc.tensor.transpose(ps[:, 7, 0:R_ALL], rows[:, :], cst[0:R_ALL, C_ID:C_ID + R_ALL]).then_inc(S["cols_up"], 1)
            pe.wait_ge(S["ssm_rows"], 1)
            for j in range(5):
                last = nc.tensor.transpose(ps[:, 6, ST * j:ST * j + ST], sprow[:, j, :], cst[0:ST, C_ID:C_ID + ST])
            last.then_inc(S["sprm_up"], 1)

            pe.wait_ge(S["cond_set"], 1)

            def modulation(first, bank, n):
                for k in range(KD):
                    take(first + k)
                    w = slot(first + k, 1)
                    for j in range(4):
                        last = mm(ps[32 * j:32 * j + 32, bank, :], condb[:, k, :], w[:, 0, 512 * j:512 * j + 512],
                                  start=(k == 0), stop=(k == KD - 1), skip_group_check=True)
                    last.then_inc(w_used, 1)
                pe.wait_ge(S["modrow_sb"], n + 1)
                for cb in range(4):
                    last = nc.tensor.transpose(ps[:, bank, P * cb:P * cb + P], modrow[:, P * cb:P * cb + P], ident)
                last.then_inc(S["modT_up"], 1)

            modulation(PIECE_ADA1, 5, 0)
            pe.wait_ge(S["xn1"], TT)
            for k in range(KD):
                for i in range(TT):
                    last = nc.tensor.transpose(ps[:, k // 2, (k % 2) * T + P * i:(k % 2) * T + P * i + P],
                                               xn_tok[:, i, P * k:P * k + P], ident)
            last.then_inc(S["xT_up"], 1)
            pe.wait_ge(S["Bblk_set"], 1)
            pe.wait_ge(S["sprm_sb"], 1)
            for r in range(2):
                for m in range(KW):
                    last = nc.tensor.transpose(ps[:, 6 + r, P * m:P * m + P],
                                               Bblk[:, r, 4 * m:4 * m + 4].rearrange("p s q c -> p (s q c)"), ident)
            last.then_inc(S["BT_up"], 1)
            for r in range(2):
                pe.wait_ge(S[f"Cblk{r}_set"], 1)
                if r == 0:
                    pe.wait_ge(S["mod1_sb"], 1)
                for m in range(KW):
                    last = nc.tensor.transpose(ps[:, 4 + r, P * m:P * m + P],
                                               Cblk[:, r, m].rearrange("p q n -> p (q n)"), ident)
                last.then_inc(S[f"CT{r}_up"], 1)

            def proj(g, h):
                n = PIECE_IN + 2 * g + h
                take(n)
                w = slot(n, 4)
                b = 2 * (g % 2)
                if h == 0:
                    if g < 2:
                        pe.wait_ge(S["h_sb"], KD)
                    else:
                        pe.wait_ge(S["proj_sb"], g - 1)
                for kk in range(4):
                    k = 4 * h + kk
                    if g == 3:
                        for i in range(TT):
                            last = mm(ps[:, b + i, :], hT[:, k, P * i:P * i + P], w[:, kk, :], start=(k == 0), stop=(k == KD - 1))
                    else:
                        for m in range(4):
                            last = mm(ps[:, b + m // 2, (m % 2) * T:(m % 2) * T + T], w[:, kk, P * m:P * m + P], hT[:, k, :],
                                      start=(k == 0 and m % 2 == 0), stop=(k == KD - 1), skip_group_check=True)
                last.then_inc(w_used, 1)

            def b_u(j):
                if j == 0:
                    pe.wait_ge(S["proj_sb"], 1)
                    pe.wait_ge(S["BT_sb"], 1)
                    pe.wait_ge(S["CT0_sb"], 1)
                    pe.wait_ge(S["CT1_sb"], 1)
                else:
                    pe.wait_ge(S["bu_read"], j)
                for q in range(2):
                    s = 2 * j + q
                    a = 32 * (s % 4)
                    for r in range(2):
                        last = mm(ps[:, 4 + q, T * r:T * r + T], BT[a:a + 32, r, s // 4, :], uT[a:a + 32, s // 4, :],
                                  start=True, stop=True, skip_group_check=True)
                last.then_inc(S["bu_up"], 1)

            def c_x(j):
                pe.wait_ge(S["xs_set"], j + 1)
                if j == 0:
                    pe.wait_ge(S["BT_sb"], 1)
                for q in range(2):
                    s = 2 * j + q
                    m, a = s // 4, 32 * (s % 4)
                    for r in range(2):
                        last = mm(ps[a:a + 32, 6 + m // 2, (m % 2) * T:(m % 2) * T + T], CT[:, r, m, a:a + 32],
                                  xs[:, j % 2, r, T * q:T * q + T], start=(r == 0), stop=(r == 1), skip_group_check=True)
                last.then_inc(S["xs_read"], 1)

            def rotate(src, n):
                pe.wait_ge(S["proj_sb"], 2 + n)
                pe.wait_ge(*((S["bu_read"], 8) if n == 0 else (S["rot_read"], 1)))
                for m in range(KW):
                    last = mm(ps[:, 4 + m // 2, (m % 2) * T:(m % 2) * T + T], cst[:, C_ROT:C_ROT + P], src[:, m, :],
                              start=True, stop=True, skip_group_check=True)
                last.then_inc(S["rot_up"], 1)

            def scores(h):
                if h == 0:
                    pe.wait_ge(S["rope_set"], 2)
                if h >= 2:
                    pe.wait_ge(S["o_sb"], h - 1)
                a, m, b = HD * (h % 2), h // 2, 4 + h % 2
                mm(ps[:, b, 0:P], qT[a:a + HD, m, 0:P], kT[a:a + HD, m, 0:P], start=True, stop=True, skip_group_check=True)
                mm(ps[:, b, P:3 * P], qT[a:a + HD, m, P:T], kT[a:a + HD, m, :], start=True, stop=True,
                   skip_group_check=True).then_inc(S["sc_up"], 1)

            def weigh(h):
                a, m, b = HD * (h % 2), h // 2, 4 + h % 2
                pe.wait_ge(S["probs"], h + 1)
                for j in range(3):
                    last = nc.tensor.transpose(ps[:, b, P * j:P * j + P], prob[:, h % 2, P * j:P * j + P], ident)
                last.then_inc(S["probsT_up"], 1)
                pe.wait_ge(S["probsT_sb"], h + 1)
                mm(ps[a:a + HD, b, 0:T], v_tok[:, 0, HD * h:HD * h + HD], probT[:, h % 2, 0:T], start=True, stop=False,
                   skip_group_check=True)
                mm(ps[a:a + HD, b, P:T], v_tok[:, 1, HD * h:HD * h + HD], probT[:, h % 2, T:3 * P], start=False, stop=True,
                   skip_group_check=True).then_inc(S["o_up"], 1)

            steps = [(g, h) for g in range(8) for h in range(2)]
            fill = {(0, 1): [("b", 0)], (1, 0): [("b", 1)], (1, 1): [("b", 2), ("c", 0)], (2, 0): [("b", 3), ("c", 1)],
                    (2, 1): [("b", 4), ("c", 2)], (3, 0): [("b", 5), ("c", 3)], (3, 1): [("b", 6), ("c", 4)],
                    (4, 0): [("b", 7), ("c", 5)], (4, 1): [("r", 0), ("c", 6)], (5, 0): [("r", 1), ("c", 7)],
                    (5, 1): [("s", 0)], (6, 0): [("w", 0), ("s", 1)], (6, 1): [("w", 1), ("s", 2)], (7, 0): [("w", 2), ("s", 3)],
                    (7, 1): [("w", 3), ("s", 4)]}
            for g, h in steps:
                proj(g, h)
                for what, j in fill.get((g, h), []):
                    if what == "b":
                        b_u(j)
                    elif what == "c":
                        c_x(j)
                    elif what == "r":
                        rotate(qT if j == 0 else kT, j)
                    elif what == "s":
                        scores(j)
                    else:
                        weigh(j)
            pe.wait_ge(S["proj_sb"], 7)
            modulation(PIECE_ADA2, 0, 1)
            weigh(4), scores(5)
            modulation(PIECE_ADA2 + KD, 1, 2)
            weigh(5), scores(6)
            weigh(6), scores(7)
            pe.wait_ge(S["mod2_sb"], 1)
            pe.wait_ge(S["proj_sb"], 8)
            for j, t in enumerate((GT1, GT2)):
                for k in range(KD):
                    b = (2, 0)[j] + k // 4
                    last = mm(ps[:, b, P * (k % 4):P * (k % 4) + P], mod[:, t + k:t + k + 1].to_broadcast([P, P]), ident,
                              start=True, stop=True, skip_group_check=True)
                last.then_inc(S["row_up"], 1)
            weigh(7)
            for n, b in enumerate((0, 2, 4, 6)):
                take(PIECE_GLU + n)
                w = slot(PIECE_GLU + n, 4)
                if n == 0:
                    pe.wait_ge(S["row_sb"], 2)
                    pe.wait_ge(S["gelu"], 1)
                    pe.wait_ge(S["o_sb"], HEADS)
                for kk in range(KW):
                    for m in range(4):
                        last = mm(ps[:, b + m // 2, (m % 2) * T:(m % 2) * T + T], w[:, kk, P * m:P * m + P], gluT[:, kk, :],
                                  start=(kk == 0 and m % 2 == 0), stop=(kk == KW - 1), skip_group_check=True)
                last.then_inc(w_used, 1)
            for n in range(2):
                take(PIECE_AO + n)
                w = slot(PIECE_AO + n, 4)
                pe.wait_ge(S["ya_set"], 1)
                for kk in range(KW):
                    for m in range(4):
                        last = mm(ps[:, 2 * n + m // 2, (m % 2) * T:(m % 2) * T + T], w[:, kk, P * m:P * m + P], oT[:, kk, :],
                                  start=(kk == 0 and m % 2 == 0), stop=(kk == KW - 1), skip_group_check=True)
                last.then_inc(w_used, 1)
            for n in range(4):
                take(PIECE_OUT + n)
                w = slot(PIECE_OUT + n, 2)
                if n == 0:
                    pe.wait_ge(S["ya_set"], 2)
                pe.wait_ge(S["merged"], 1 if n < 2 else 2)
                for kk in range(2):
                    k = 2 * n + kk
                    for i in range(TT):
                        for h in range(2):
                            last = mm(ps[:, 4 + 2 * i + h, :], mergedT[:, k, P * i:P * i + P], w[:, kk, 512 * h:512 * h + 512],
                                      start=(k == 0), stop=(k == KD - 1))
                last.then_inc(w_used, 1)
            pe.wait_ge(S["xn2"], TT)
            pe.wait_ge(S["yb_used"], 2)
            for k in range(KD):
                for i in range(TT):
                    last = nc.tensor.transpose(ps[:, k // 2, (k % 2) * T + P * i:(k % 2) * T + P * i + P],
                                               xn_tok[:, i, P * k:P * k + P], ident)
            last.then_inc(S["x2T_up"], 1)
            pe.wait_ge(S["h2_sb"], KD)
            pe.wait_ge(S["late_in"], 80)
            for i in range(TT):
                for k in range(KD):
                    last = mm(ps[:, 4, EXPERTS * i:EXPERTS * i + EXPERTS], hT[:, k, P * i:P * i + P], wr[:, k, :],
                              start=(k == 0), stop=(k == KD - 1), skip_group_check=True)
            last.then_inc(S["logit_up"], 1)
            sel = rt[:, 0]
            tri = cst[:, C_TRI:C_TRI + P]
            pe.wait_ge(S["sel_set"], 1)
            pe.wait_ge(S["ones_set"], 1)
            mm(ps[:, 5, 0:EXPERTS], tri, sel[:, 0, :], start=True, stop=True, skip_group_check=True)
            mm(ps[:, 5, EXPERTS:2 * EXPERTS], ones[:, :], sel[:, 0, :], start=True, stop=False, skip_group_check=True)
            mm(ps[:, 5, EXPERTS:2 * EXPERTS], tri, sel[:, 1, :], start=False, stop=True, skip_group_check=True)
            mm(ps[0:EXPERTS, 6, 0:1], sel[:, 0, :], ones[:, 0:1], start=True, stop=False, skip_group_check=True)
            mm(ps[0:EXPERTS, 6, 0:1], sel[:, 1, :], ones[:, 0:1], start=False, stop=True, skip_group_check=True).then_inc(S["pos_up"], 1)
            pe.wait_ge(S["pos_sb"], 1)
            for j, src in enumerate((rt[:, 1], rt[:, 2])):
                for i in range(TT):
                    last = nc.tensor.transpose(ps[0:EXPERTS, 7, T * j + P * i:T * j + P * i + P], src[:, i, :], ident)
            last.then_inc(S["rT_up"], 1)
            pe.wait_ge(S["extra_set"], 1)
            mm(ps[0:EXPERTS, 6, 1:2], cst[0:EXPERTS, C_TRI32:C_TRI32 + EXPERTS], chunk[:, 3:4], start=True, stop=True,
               skip_group_check=True)
            mm(ps[0:1, 6, 2:3], ones[0:EXPERTS, 0:1], chunk[:, 3:4], start=True, stop=True,
               skip_group_check=True).then_inc(S["cum_up"], 1)
            pe.wait_ge(S["hot_set"], 1)
            pe.wait_ge(S["rT_sb"], 1)
            for i in range(TT):
                mm(ps[:, 4, 48 * i:48 * i + ITEMS], rowT[:, 0, P * i:P * i + P], hot[:, 0, 0:ITEMS], start=True, stop=False,
                   skip_group_check=True)
                mm(ps[:, 4, 48 * i:48 * i + ITEMS], ones[:, :], hot[:, 1, 0:ITEMS], start=False, stop=True,
                   skip_group_check=True)
                mm(ps[:, 5, 48 * i:48 * i + ITEMS], rowT[:, 1, P * i:P * i + P], hot[:, 0, 0:ITEMS], start=True, stop=True,
                   skip_group_check=True)
            mm(ps[0:1, 6, 8:8 + ITEMS], cst[:, C_E:C_E + 1], hot[:, 0, 0:ITEMS], start=True, stop=True,
               skip_group_check=True).then_inc(S["item_up"], 1)

            def gather():
                for f in range(KD):
                    for i in range(TT):
                        for c in range(3):
                            last = mm(ps[:, 2, CAP * f:CAP * f + CAP], xpart[:, c, i, P * f:P * f + P], pick[:, i, :],
                                      start=(i == 0 and c == 0), stop=(i == TT - 1 and c == 2), skip_group_check=True)
                last.then_inc(S["hg_up"], 1)

            pe.wait_ge(S["pick_set"], 1)
            pe.wait_ge(S["x_split"], 1)
            gather()
            pe.wait_ge(S["item_sb"], 4)
            for i in range(TT):
                if i == 1:
                    pe.wait_ge(S["acc_set"], 1)
                for h in range(2):
                    last = mm(ps[:, 6 + h, :], rowT[:, 1, P * i:P * i + P], bdn_rows[:, 512 * h:512 * h + 512],
                              start=True, stop=True)
                last.then_inc(S["bias_up"], 1)
            pe.wait_ge(S["ysb_zero"], 1)
            pe.wait_ge(S["acc_set"], 2)
            count = pe.value_load(icnt[0:1, 0:1], min_val=EXPERTS, max_val=ITEMS)

            def combine(i):
                pe.wait_ge(S["pickw_set"], i + 1)
                for t in range(TT):
                    for h in range(2):
                        last = nc.tensor.transpose(ps[:, 5, T * h + P * t:T * h + P * t + P], pickw[:, t, h, :], ident)
                last.then_inc(S["pwT_up"], 1)
                pe.wait_ge(S["y_sb"], i)
                pe.wait_ge(S["pwT_sb"], i + 1)
                for t in range(TT):
                    for h in range(2):
                        if t + h:
                            pe.wait_ge(S["comb_add"], i * 4 + (2 * t + h - 1))
                        else:
                            pe.wait_ge(S["comb_add"], i * 4)
                        mm(ps[:, 6 + h, :], pickwT[:, h, P * t:P * t + P], ysb, start=True, stop=True).then_inc(S["comb_up"], 1)

            with pe.Fori(0, ITEMS) as i:
                with pe.If(i < count):
                    pe.wait_ge(S["hotb_set"], i + 1)
                    for b in range(2):
                        for h in range(2):
                            mm(ps[CAP * h:CAP * h + CAP, b, :], hotb, bgu_rows[:, D * b + 512 * h:D * b + 512 * h + 512],
                               start=True, stop=False, skip_group_check=True)
                    pe.wait_ge(S["hg_sb"], i + 1)
                    for j in range(GU_PIECES):
                        pe.wait_ge(arrived[slot_of[j]], i * 16 + 16 * (round_of[j] + 1))
                        w = slot(PRE + j, 1)
                        for b in range(2):
                            for h in range(2):
                                last = mm(ps[CAP * h:CAP * h + CAP, b, :], hg[:, j, :],
                                          w[:, 0, D * b + 512 * h:D * b + 512 * h + 512],
                                          start=False, stop=(j == GU_PIECES - 1), skip_group_check=True)
                        last.then_inc(w_used, 1)
                    pe.wait_ge(S["pick_set"], i + 2)
                    gather()
                    combine(i)
                    pe.wait_ge(S["act_set"], i + 1)
                    for j in range(4):
                        last = nc.tensor.transpose(ps[:, 4, P * j:P * j + P], act_[:, P * j:P * j + P], ident)
                    last.then_inc(S["actT_up"], 1)
                    pe.wait_ge(S["actT_sb"], i + 1)
                    for j in range(DN_PIECES):
                        pe.wait_ge(arrived[slot_of[GU_PIECES + j]], i * 16 + 16 * (round_of[GU_PIECES + j] + 1))
                        w = slot(PRE + GU_PIECES + j, 2)
                        for kk in range(2):
                            k = 2 * j + kk
                            for h in range(2):
                                last = mm(ps[CAP * h:CAP * h + CAP, 3, :], actT[:, k % 4, k // 4, :], w[:, kk, 512 * h:512 * h + 512],
                                          start=(k == 0), stop=(k == KD - 1), skip_group_check=True)
                        last.then_inc(w_used, 1)
            combine(count)

        @block.scalar
        def _(act):
            link = linker(act, S["lnA"])
            act.dma_start(are[:, :], a_re[0].rearrange("(s q) p -> s (q p)", q=2)).then_inc(S["ssm_in"], 16)
            act.dma_start(aim[:, :], a_im[0].rearrange("(s q) p -> s (q p)", q=2)).then_inc(S["ssm_in"], 16)
            act.dma_start(ldt[:, :], log_dt.rearrange("a (s q) -> (a s) q", q=2)).then_inc(S["ssm_in"], 16)
            for r, (b, cc) in enumerate(((b_re, c_re), (b_im, c_im))):
                act.dma_start(b_in[:, r], b[0].rearrange("(s q) p c -> (q p) s c", q=2)).then_inc(S["bc_in"], 16)
                act.dma_start(c_in[:, r], cc[0].rearrange("(m g) c p -> (g c) m p", m=KW)).then_inc(S["bc_in"], 16)
            act.wait_ge(S["ssm_in"], 48)
            nc.scalar.activation(ldt[:, :], ldt[:, :], ACT.Exp).then_inc(S["dt_set"], 1)
            act.wait_ge(S["lrdt_set"], 1)
            nc.scalar.activation(sprow[:, 0, :], sprow[:, 5, :], ACT.Exp).then_inc(S["mag_set"], 1)
            act.wait_ge(S["angle_set"], 1)
            nc.scalar.activation(sprow[:, 2, :], sprow[:, 6, :], ACT.Sin).then_inc(S["trig_set"], 1)
            nc.scalar.activation(sprow[:, 7, :], sprow[:, 6, :], ACT.Sin, scale=0.5).then_inc(S["trig_set"], 1)
            act.wait_ge(S["cols_sb"], 1)
            link(nc.scalar.activation(cond[:, :], cols[:, R_C:R_C + KD], ACT.Sigmoid))
            act.wait_ge(S["x_in"], 16)
            act.wait_ge(S["lnD"], 1)
            for i in range(TT):
                link(nc.scalar.activation(hT[:, 4 * i:4 * i + 4, :].rearrange("p k t -> p (k t)"), x_tok[:, i, :], ACT.Square,
                                          accum_out=stat[:, 0, i:i + 1]))
            nc.scalar.activation(stat[:, 1, :], stat[:, 0, :], ACT.Sqrt, bias=stat[:, 3, 0:1], scale=1.0 / D).then_inc(S["sq1"], 1)
            def row_copy(n):
                act.wait_ge(w_used, (KD, PIECE_ADA2 + KD, PIECE_ADA2 + 2 * KD)[n])
                nc.scalar.copy(modrow[:, :], ps[:, (5, 0, 1)[n], :]).then_inc(S["modrow_sb"], 1)

            row_copy(0)
            act.wait_ge(S["BT_up"], 1)
            nc.scalar.copy(BT[:, :, :, :].rearrange("p r m n -> p (r m n)"), ps[:, 6:8, :].rearrange("p b n -> p (b n)")).then_inc(S["BT_sb"], 1)
            for r in range(2):
                act.wait_ge(S[f"CT{r}_up"], 1)
                nc.scalar.activation(CT[:, r].rearrange("p m n -> p (m n)"), ps[:, 4 + r, :], ACT.Copy,
                                     scale=(1.0 if r == 0 else -1.0)).then_inc(S[f"CT{r}_sb"], 1)

            def head(h):
                act.wait_ge(S["negmax"], h + 1)
                for j, (a, b) in enumerate(((0, P), (P, 3 * P))):
                    last = nc.scalar.activation(prob[:, h % 2, a:b], prob[:, h % 2, a:b], ACT.Exp, bias=mx[:, h % 2, j:j + 1],
                                                scale=HD ** -0.5, accum_out=mx[:, h % 2, 2 + j:3 + j])
                    last.then_inc(S["expd"], 1)
                act.wait_ge(S["probsT_up"], h + 1)
                nc.scalar.copy(probT[:, h % 2, :], ps[:, 4 + h % 2, 0:3 * P]).then_inc(S["probsT_sb"], 1)
                act.wait_ge(S["o_up"], h + 1)
                a = HD * (h % 2)
                nc.scalar.copy(oT[a:a + HD, h // 2, :], ps[a:a + HD, 4 + h % 2, 0:T]).then_inc(S["o_sb"], 1)

            for g, dst in enumerate((uT, qT, kT, v_tok, gaT[:, 0:4, :], gaT[:, 4:8, :], gbT[:, 0:4, :], gbT[:, 4:8, :])):
                act.wait_ge(w_used, PIECE_IN + 2 * g + 2)
                nc.scalar.copy(dst, ps[:, 2 * (g % 2):2 * (g % 2) + 2, :].rearrange(
                    "p b (m t) -> p (b m) t", t=dst.shape[2])).then_inc(S["proj_sb"], 1)
                if g == 5:
                    head(0), head(1)
                if g == 6:
                    head(2), head(3)
            row_copy(1)
            head(4)
            row_copy(2)
            head(5)
            head(6)
            for j, dst in enumerate((gate_mix, gate_ffn)):
                act.wait_ge(S["row_up"], j + 1)
                nc.scalar.copy(dst[:, :], ps[:, (2, 0)[j]:(2, 0)[j] + 2, :].rearrange("p b n -> p (b n)")).then_inc(S["row_sb"], 1)
            head(7)
            act.wait_ge(S["y_skip"], 1)
            nc.scalar.activation(gluT, yaT[:, 0:KW, :], ACT.Gelu_apprx_tanh).then_inc(S["gelu"], 1)
            nc.scalar.activation(gaT, gaT, ACT.Sigmoid).then_inc(S["sig_ga"], 1)
            nc.scalar.activation(gbT, gbT, ACT.Sigmoid).then_inc(S["sig_gb"], 1)
            for h in range(2):
                act.wait_ge(w_used, PIECE_GLU + 2 * h + 2)
                if h == 1:
                    act.wait_ge(S["ya_set"], 1)
                nc.scalar.activation(sigb, ps[:, 4 * h + 2:4 * h + 4, :].rearrange("p b (m t) -> p (b m) t", t=T), ACT.Sigmoid).then_inc(S["sigb_set"], 1)
            act.wait_ge(S["merged"], 2)
            act.dma_start(wr[:, :, :], w_router[0].rearrange("(k p) e -> p k e", p=P)).then_inc(S["late_in"], 16)
            act.dma_start(brt[:, :], b_router.to_broadcast([P, EXPERTS])).then_inc(S["late_in"], 16)
            act.wait_ge(S["zeroed"], 1)
            act.dma_start(bgu_rows[0:EXPERTS, :], b_gu[0]).then_inc(S["late_in"], 16)
            act.dma_start(bdn_rows[0:EXPERTS, :], b_down[0]).then_inc(S["late_in"], 16)
            act.dma_start(gfin, g_final.rearrange("(a d) -> a d", a=1).to_broadcast([P, D])).then_inc(S["late_in"], 16)
            for i in range(TT):
                act.wait_ge(S["x1"], i + 1)
                nc.scalar.activation(hT[:, 4 * i:4 * i + 4, :].rearrange("p k t -> p (k t)"), x_tok[:, i, :], ACT.Square,
                                     accum_out=stat[:, 0, i:i + 1]).then_inc(S["lnA"], 1)
            act.wait_ge(S["lnA"], 5)
            nc.scalar.activation(stat[:, 1, :], stat[:, 0, :], ACT.Sqrt, bias=stat[:, 3, 0:1], scale=1.0 / D).then_inc(S["sq2"], 1)
            act.wait_ge(S["xn2"], TT)
            nc.scalar.copy(xpart[:, 0], xn_tok[:, :, :]).then_inc(S["xh_set"], 1)
            act.wait_ge(S["x2T_up"], 1)
            for k in range(KD):
                nc.scalar.activation(hT[:, k, :], ps[:, k // 2, (k % 2) * T:(k % 2) * T + T], ACT.Identity,
                                     bias=mod[:, SH2 + k:SH2 + k + 1], scale=scale2[:, k:k + 1]).then_inc(S["h2_sb"], 1)
            act.wait_ge(S["xr_set"], 1)
            nc.scalar.copy(xpart[:, 1], gate_rest).then_inc(S["xm_set"], 1)
            act.wait_ge(S["top_set"], 1)
            for i in range(TT):
                nc.scalar.activation(rt[:, 3, i, :], lg[:, i, :], ACT.Exp, bias=rs[:, i, 0:1]).then_inc(S["ex_set"], 1)
            act.wait_ge(S["rT_up"], 1)
            act.wait_ge(S["zeroed"], 1)
            nc.scalar.copy(rowT[0:EXPERTS, :, :].rearrange("p j t -> p (j t)"), ps[0:EXPERTS, 7, :]).then_inc(S["rT_sb"], 1)
            act.wait_ge(S["x_split"], 1)
            for i in range(TT):
                act.wait_ge(S["bias_up"], i + 1)
                nc.scalar.copy(acc[:, i, :], ps[:, 6:8, :].rearrange("p b n -> p (b n)")).then_inc(S["acc_set"], 1)
            act.wait_ge(S["item_sb"], 4)
            count = act.value_load(icnt[0:1, 0:1], min_val=EXPERTS, max_val=ITEMS)

            def combine_copies(i):
                act.wait_ge(S["pwT_up"], i + 1)
                nc.scalar.copy(pickwT.rearrange("p h t -> p (h t)"), ps[:, 5, :]).then_inc(S["pwT_sb"], 1)

            with act.Fori(0, ITEMS) as i:
                with act.If(i < count):
                    act.wait_ge(S["gated"], i + 1)
                    nc.scalar.activation(sig, gate, ACT.Sigmoid, scale=ALPHA).then_inc(S["sig_set"], 1)
                    combine_copies(i)
                    act.wait_ge(S["actT_up"], i + 1)
                    nc.scalar.copy(actT.rearrange("p j h s -> p (j h s)"), ps[:, 4, :]).then_inc(S["actT_sb"], 1)
                    act.wait_ge(w_used, i * SLOTS + (PRE + SLOTS))
                    nc.scalar.copy(ysb, ps[:, 3, :]).then_inc(S["y_sb"], 1)
            combine_copies(count)
            for i in range(TT):
                act.wait_ge(S["fin"], i + 1)
                nc.scalar.activation(xn_tok[:, i, :], x_tok[:, i, :], ACT.Square,
                                     accum_out=stat[:, 0, i:i + 1]).then_inc(S["lnA"], 1)
                act.wait_ge(S["lnA"], 6 + i)
                nc.scalar.activation(stat[:, 1, i:i + 1], stat[:, 0, i:i + 1], ACT.Sqrt, bias=stat[:, 3, 0:1], scale=1.0 / D).then_inc(S["sq3"], 1)

        @block.gpsimd
        def _(pool):
            nc.gpsimd.memset(ones[:, :], 1.0).then_inc(S["ones_set"], 1)
            link = linker(pool, S["lnP"])
            pool.wait_ge(S["sprm_sb"], 1)
            link(nc.gpsimd.memset(ecos[:, :, 0:1], 1.0))
            link(nc.gpsimd.memset(esin[:, :, 0:1], 0.0))
            link(nc.gpsimd.tensor_copy(ecos[:, :, 1:2], sprm[:, 1, :].unsqueeze(2)))
            link(nc.gpsimd.tensor_copy(esin[:, :, 1:2], sprm[:, 2, :].unsqueeze(2)))
            for n in (2, 4, 8, 16, 32, 64):
                square(nc.gpsimd, link, n)
                double(nc.gpsimd, link, n, xs[:, 0])
            pool.engine_nop().then_inc(S["phase_lo"], 1)
            for j in range(8):
                b = j % 2
                zr, zi = z[:, b, 0, :].rearrange("p (s t) -> p s t", s=2), z[:, b, 1, :].rearrange("p (s t) -> p s t", s=2)
                cs, sn = ecos[:, 2 * j:2 * j + 2, :], esin[:, 2 * j:2 * j + 2, :]
                xr, xi = xs[:, b, 0, :].rearrange("p (s t) -> p s t", s=2), xs[:, b, 1, :].rearrange("p (s t) -> p s t", s=2)
                t = ptmp[:, :].rearrange("p (s t) -> p s t", s=2)
                pool.wait_ge(S["scanned"], j + 1)
                if j >= 2:
                    pool.wait_ge(S["xs_read"], j - 1)
                link(nc.gpsimd.tensor_tensor(xr, zr, cs, ALU.mult))
                link(nc.gpsimd.tensor_tensor(t, zi, sn, ALU.mult))
                link(nc.gpsimd.tensor_tensor(xr, xr, t, ALU.subtract))
                link(nc.gpsimd.tensor_tensor(xi, zr, sn, ALU.mult))
                link(nc.gpsimd.tensor_tensor(t, zi, cs, ALU.mult))
                nc.gpsimd.tensor_tensor(xi, xi, t, ALU.add).then_inc(S["xs_set"], 1)
                pool.wait_ge(S["xs_set"], j + 1)
            pool.wait_ge(S["merged"], 2)
            for dst in (bgu_rows, bdn_rows):
                link(nc.gpsimd.memset(dst, 0.0))
            nc.gpsimd.memset(rowT, 0.0).then_inc(S["zeroed"], 1)
            pool.wait_ge(w_used, PRE)
            link(nc.gpsimd.memset(pickw, 0.0))
            nc.gpsimd.memset(ysb, 0.0).then_inc(S["ysb_zero"], 1)

        @block.vector
        def _(dve):
            link = linker(dve, S["lnD"])
            V = nc.vector
            link(V.memset(stat[:, 3, :], EPS))
            link(V.memset(hot[:, :, :], 0.0))
            dve.wait_ge(S["cols_up"], 1)
            V.tensor_copy(cols[:, :], ps[:, 7, 0:R_ALL]).then_inc(S["cols_sb"], 1)
            dve.wait_ge(S["dt_set"], 1)
            dve.wait_ge(S["ssm_in"], 48)
            dtb = ldt[:, :].unsqueeze(2).to_broadcast([ST, 2, N])

            def mod_group(ap, n):
                return ap[:, 2 * KD * n:2 * KD * (n + 1)].rearrange("p (j c) -> p c j", j=4)

            def modT(bank):
                return ps[:, bank, :].rearrange("p (c j r) -> p c j r", c=4, j=4)[:, :, :, 0]

            def row(j):
                return sprow[:, j, :]

            def two(ap):
                return ap.rearrange("s (q n) -> s q n", q=2)

            V.tensor_tensor(two(row(5)), two(are[:, :]), dtb, ALU.mult).then_inc(S["lrdt_set"], 1)
            link(V.tensor_tensor(two(row(6)), two(aim[:, :]), dtb, ALU.mult))
            link(V.tensor_scalar(row(8), row(6), 1.0 / TWO_PI, ROUND, ALU.mult, ALU.add))
            link(V.tensor_scalar(row(8), row(8), -ROUND, None, ALU.add))
            parts, rest = [], TWO_PI
            for bits in (2.0 ** -6, 2.0 ** -16):
                parts.append(np.floor(rest / bits) * bits)
                rest -= parts[-1]
            for part in parts + [rest]:
                link(V.scalar_tensor_tensor(row(6), row(8), -float(part), row(6), ALU.mult, ALU.add))
            V.tensor_scalar(row(6), row(6), float(np.float32(3.1415925)), -float(np.float32(3.1415925)), ALU.min, ALU.max).then_inc(S["angle_set"], 1)
            dve.wait_ge(S["mag_set"], 1)
            dve.wait_ge(S["trig_set"], 2)
            link(V.tensor_tensor(row(1), row(7), row(7), ALU.mult))
            link(V.tensor_scalar(row(1), row(1), -2.0, 1.0, ALU.mult, ALU.add))
            link(V.tensor_tensor(row(8), row(0), row(1), ALU.mult))
            link(V.tensor_tensor(row(9), row(0), row(2), ALU.mult))
            link(V.tensor_scalar(row(8), row(8), -1.0, None, ALU.add))
            link(V.tensor_tensor(row(10), are[:, :], are[:, :], ALU.mult))
            link(V.tensor_tensor(row(11), aim[:, :], aim[:, :], ALU.mult))
            link(V.tensor_tensor(row(10), row(10), row(11), ALU.add))
            link(V.reciprocal(row(10), row(10)))
            link(V.tensor_tensor(row(11), row(8), are[:, :], ALU.mult))
            link(V.tensor_tensor(row(12), row(9), aim[:, :], ALU.mult))
            link(V.tensor_tensor(row(11), row(11), row(12), ALU.add))
            link(V.tensor_tensor(row(3), row(11), row(10), ALU.mult))
            link(V.tensor_tensor(row(11), row(9), are[:, :], ALU.mult))
            link(V.tensor_tensor(row(12), row(8), aim[:, :], ALU.mult))
            link(V.tensor_tensor(row(11), row(11), row(12), ALU.subtract))
            V.tensor_tensor(row(4), row(11), row(10), ALU.mult).then_inc(S["ssm_rows"], 1)
            dve.wait_ge(S["lnA"], 1)
            dve.wait_ge(S["cols_sb"], 1)
            link(V.tensor_tensor(cond[:, :], cond[:, :], cols[:, R_C:R_C + KD], ALU.mult))
            V.tensor_copy(condb[:, :, :], cond[:, :].unsqueeze(2).to_broadcast([P, KD, 32])).then_inc(S["cond_set"], 1)
            dve.wait_ge(S["sprm_up"], 1)
            V.tensor_copy(sprm[:, :, :].rearrange("p j s -> p (j s)"), ps[:, 6, 0:5 * ST]).then_inc(S["sprm_sb"], 1)
            dve.wait_ge(S["sprm_sb"], 1)
            dve.wait_ge(S["bc_in"], 64)
            dve.wait_ge(S["const_in"], 16)
            cr = sprm[:, 3, :].unsqueeze(2).to_broadcast([P, ST, C])
            ci = sprm[:, 4, :].unsqueeze(2).to_broadcast([P, ST, C])
            t0 = tmp[:, 0, 0:256].rearrange("p (s c) -> p s c", s=ST)
            t1 = tmp[:, 0, 256:512].rearrange("p (s c) -> p s c", s=ST)
            for r in range(2):
                link(V.tensor_tensor(t0, b_in[:, r], cr, ALU.mult))
                link(V.tensor_tensor(t1, b_in[:, 1 - r], ci, ALU.mult))
                link(V.tensor_tensor(t0, t0, t1, ALU.subtract if r == 0 else ALU.add))
                for q in range(2):
                    last = V.tensor_scalar(Bblk[:, r, :, q, :], t0, cst[:, C_MB + q:C_MB + q + 1], None, ALU.mult)
                    if r == 0 or q == 0:
                        link(last)
            last.then_inc(S["Bblk_set"], 1)
            for r in range(2):
                for q in range(2):
                    last = V.tensor_scalar(Cblk[:, r, :, q, :], c_in[:, r], cst[:, C_MC + q:C_MC + q + 1], None, ALU.mult)
                    if q == 0:
                        link(last)
                last.then_inc(S[f"Cblk{r}_set"], 1)
                if r == 0:
                    dve.wait_ge(S["sq1"], 1)
                    link(V.reciprocal(stat[:, 2, :], stat[:, 1, :]))
                    for i in range(TT):
                        V.tensor_scalar(xn_tok[:, i, :], x_tok[:, i, :], stat[:, 2, i:i + 1], None, ALU.mult).then_inc(S["xn1"], 1)
                    dve.wait_ge(S["modT_up"], 1)
                    V.tensor_tensor(mod_group(mod, 0), modT(5), mod_group(cols[:, R_ADA:R_ADA + 6 * KD], 0), ALU.add).then_inc(S["mod1_sb"], 1)
                    dve.wait_ge(S["mod1_sb"], 1)
                    link(V.scalar_tensor_tensor(scale1[:, :], mod[:, SC1:SC1 + KD], 1.0, cols[:, R_GMIX:R_GMIX + KD], ALU.add, ALU.mult))
                    dve.wait_ge(S["xT_up"], 1)
                    for k in range(KD):
                        V.tensor_scalar(hT[:, k, :], ps[:, k // 2, (k % 2) * T:(k % 2) * T + T], scale1[:, k:k + 1],
                                        mod[:, SH1 + k:SH1 + k + 1], ALU.mult, ALU.add).then_inc(S["h_sb"], 1)

            dve.wait_ge(S["BT_up"], 1)
            dve.wait_ge(S["CT1_up"], 1)
            dve.wait_ge(S["phase_lo"], 1)
            square(V, link, T // 2)
            double(V, link, T // 2, tmp)
            V.engine_nop().then_inc(S["phases"], 1)
            for j in range(8):
                b = j % 2
                cs, sn = ecos[:, 2 * j:2 * j + 2, :], esin[:, 2 * j:2 * j + 2, :]
                br, bi = (ps[:, 4:6, T * r:T * r + T] for r in range(2))
                tz = [tmp[:, r, :].rearrange("p (s t) -> p s t", s=2) for r in range(2)]
                zz = [z[:, b, r, :].rearrange("p (s t) -> p s t", s=2) for r in range(2)]
                dve.wait_ge(S["bu_up"], j + 1)
                if j >= 2:
                    dve.wait_ge(S["xs_set"], j - 1)
                link(V.tensor_tensor(zz[0], br, cs, ALU.mult))
                link(V.tensor_tensor(tz[0], bi, sn, ALU.mult))
                link(V.tensor_tensor(zz[0], zz[0], tz[0], ALU.add))
                link(V.tensor_tensor(zz[1], bi, cs, ALU.mult))
                V.tensor_tensor(tz[0], br, sn, ALU.mult).then_inc(S["bu_read"], 1)
                dve.wait_ge(S["bu_read"], j + 1)
                link(V.tensor_tensor(zz[1], zz[1], tz[0], ALU.subtract))
                for r in range(2):
                    for q in range(2):
                        s = 2 * j + q
                        last = V.tensor_tensor_scan(zz[r][:, q, :], sprm[:, 0, s:s + 1].to_broadcast([P, T]), zz[r][:, q, :], 0.0,
                                                    ALU.mult, ALU.add)
                        if r == 0 or q == 0:
                            link(last)
                last.then_inc(S["scanned"], 1)
            for n, dst in enumerate((qT, kT)):
                dve.wait_ge(S["rot_up"], n + 1)
                cosb = cst[:, C_COS:C_COS + T].unsqueeze(1).to_broadcast([P, KW, T])
                for m in range(KW):
                    t = tmp[:, m % 2, 0:T]
                    last = V.tensor_tensor(t, ps[:, 4 + m // 2, (m % 2) * T:(m % 2) * T + T], cst[:, C_SIN:C_SIN + T], ALU.mult)
                    if m == KW - 1:
                        last.then_inc(S["rot_read"], 1)
                        dve.wait_ge(S["rot_read"], n + 1)
                    else:
                        link(last)
                    link(V.tensor_tensor(dst[:, m, :], dst[:, m, :], cst[:, C_COS:C_COS + T], ALU.mult))
                    last = V.tensor_tensor(dst[:, m, :], dst[:, m, :], t, ALU.add)
                    if m < KW - 1:
                        link(last)
                last.then_inc(S["rope_set"], 1)

            def head(h):
                b = h % 2
                dve.wait_ge(S["sc_up"], h + 1)
                link(V.tensor_tensor(prob[:, b, :], ps[:, 4 + b, 0:3 * P], cst[:, C_CAUSAL:C_CAUSAL + 3 * P], ALU.add))
                link(V.tensor_reduce(mx[:, b, 0:1], prob[:, b, 0:P], AX.X, ALU.max))
                link(V.tensor_reduce(mx[:, b, 1:2], prob[:, b, P:3 * P], AX.X, ALU.max))
                V.tensor_scalar(mx[:, b, 0:2], mx[:, b, 0:2], -HD ** -0.5, None, ALU.mult).then_inc(S["negmax"], 1)
                dve.wait_ge(S["expd"], 2 * h + 2)
                link(V.reciprocal(mx[:, b, 2:4], mx[:, b, 2:4]))
                link(V.tensor_scalar(prob[:, b, 0:P], prob[:, b, 0:P], mx[:, b, 2:3], None, ALU.mult))
                V.tensor_scalar(prob[:, b, P:3 * P], prob[:, b, P:3 * P], mx[:, b, 3:4], None, ALU.mult).then_inc(S["probs"], 1)
                dve.wait_ge(S["probs"], h + 1)

            def skip():
                dve.wait_ge(S["xs_read"], 8)
                dve.wait_ge(S["xs_set"], 8)
                for m in range(KW):
                    last = V.scalar_tensor_tensor(yaT[:, m, :], uT[:, m, :], cols[:, R_D + m:R_D + m + 1],
                                                  ps[:, 6 + m // 2, (m % 2) * T:(m % 2) * T + T], ALU.mult, ALU.add)
                    if m < KW - 1:
                        link(last)
                last.then_inc(S["y_skip"], 1)

            skip()
            for h in range(6):
                head(h)
            for n in (1, 2):
                dve.wait_ge(S["modT_up"], n + 1)
                last = V.tensor_tensor(mod_group(mod, n), modT(n - 1), mod_group(cols[:, R_ADA:R_ADA + 6 * KD], n), ALU.add)
                if n == 1:
                    link(last)
            last.then_inc(S["mod2_sb"], 1)
            head(6), head(7)
            dve.wait_ge(S["mod2_sb"], 1)
            link(V.scalar_tensor_tensor(scale2[:, :], mod[:, SC2:SC2 + KD], 1.0, cols[:, R_GFFN:R_GFFN + KD], ALU.add, ALU.mult))
            for h in range(2):
                dve.wait_ge(S["sigb_set"], h + 1)
                V.tensor_tensor(yaT[:, 4 * h:4 * h + 4, :], ps[:, 4 * h:4 * h + 2, :].rearrange("p b (m t) -> p (b m) t", t=T), sigb,
                                ALU.mult).then_inc(S["ya_set"], 1)
            dve.wait_ge(S["sig_ga"], 1)
            dve.wait_ge(S["sig_gb"], 1)
            for h in range(2):
                m4 = slice(4 * h, 4 * h + 4)
                dve.wait_ge(S["ya_set"], h + 1)
                link(V.tensor_tensor(mergedT[:, m4, :], yaT[:, m4, :], gaT[:, m4, :], ALU.mult))
                dve.wait_ge(w_used, PIECE_AO + h + 1)
                V.tensor_tensor(ybT[:, m4, :], ps[:, 2 * h:2 * h + 2, :].rearrange("p b (m t) -> p (b m) t", t=T),
                                gbT[:, m4, :], ALU.mult).then_inc(S["yb_used"], 1)
                dve.wait_ge(S["yb_used"], h + 1)
                V.tensor_tensor(mergedT[:, m4, :], mergedT[:, m4, :], ybT[:, m4, :], ALU.add).then_inc(S["merged"], 1)
            dve.wait_ge(w_used, PRE)
            dve.wait_ge(S["row_sb"], 2)
            for i in range(TT):
                scr = xn_tok[:, i, :]
                link(V.tensor_tensor(scr, ps[:, 4 + 2 * i:6 + 2 * i, :].rearrange("p b n -> p (b n)"), gate_mix[:, :], ALU.mult))
                V.tensor_tensor(x_tok[:, i, :], x_tok[:, i, :], scr, ALU.add).then_inc(S["x1"], 1)
            dve.wait_ge(S["x1"], TT)
            dve.wait_ge(S["sq2"], 1)
            link(V.reciprocal(stat[:, 2, :], stat[:, 1, :]))
            for i in range(TT):
                V.tensor_scalar(xn_tok[:, i, :], x_tok[:, i, :], stat[:, 2, i:i + 1], None, ALU.mult).then_inc(S["xn2"], 1)
            dve.wait_ge(S["xh_set"], 1)
            V.tensor_tensor(gate_rest, xn_tok[:, :, :], xpart[:, 0], ALU.subtract).then_inc(S["xr_set"], 1)
            sel, pos, wgt, ex, eq, run = (rt[:, j] for j in range(6))
            dve.wait_ge(S["logit_up"], 1)
            link(V.tensor_tensor(lg[:, :, :], ps[:, 4, 0:TT * EXPERTS].rearrange("p (i e) -> p i e", i=TT),
                                 brt[:, :].unsqueeze(1).to_broadcast([P, TT, EXPERTS]), ALU.add))
            for i in range(TT):
                link(V.max(top[:, i, :], lg[:, i, :]))
            V.tensor_scalar(rs[:, :, 0:1], top[:, :, 0:1], -1.0, None, ALU.mult).then_inc(S["top_set"], 1)
            dve.wait_ge(S["ones_set"], 1)
            for i in range(TT):
                t4 = top[:, i, TOPK - 1:TOPK]
                link(V.tensor_scalar(sel[:, i, :], lg[:, i, :], t4, None, ALU.is_gt))
                link(V.tensor_reduce(rs[:, i, 1:2], sel[:, i, :], AX.X, ALU.add))
                link(V.tensor_scalar(rs[:, i, 1:2], rs[:, i, 1:2], -1.0, float(TOPK), ALU.mult, ALU.add))
                link(V.tensor_scalar(eq[:, i, :], lg[:, i, :], t4, None, ALU.is_equal))
                link(V.tensor_tensor_scan(run[:, i, :], ones[:, 0:EXPERTS], eq[:, i, :], 0.0, ALU.mult, ALU.add))
                link(V.tensor_scalar(run[:, i, :], run[:, i, :], rs[:, i, 1:2], None, ALU.is_le))
                link(V.tensor_tensor(eq[:, i, :], eq[:, i, :], run[:, i, :], ALU.mult))
                last = V.tensor_tensor(sel[:, i, :], sel[:, i, :], eq[:, i, :], ALU.add)
                if i < TT - 1:
                    link(last)
            last.then_inc(S["sel_set"], 1)
            dve.wait_ge(S["sel_set"], 1)
            dve.wait_ge(S["ex_set"], TT)
            link(V.tensor_tensor(ex, ex, sel, ALU.mult))
            link(V.tensor_reduce(rs[:, :, 2:3], ex, AX.X, ALU.add))
            link(V.reciprocal(rs[:, :, 2:3], rs[:, :, 2:3]))
            for i in range(TT):
                link(V.tensor_scalar(wgt[:, i, :], ex[:, i, :], rs[:, i, 2:3], None, ALU.mult))
            dve.wait_ge(S["pos_up"], 1)
            V.scalar_tensor_tensor(pos, ps[:, 5, 0:TT * EXPERTS].rearrange("p (i e) -> p i e", i=TT), 1.0, sel,
                                   ALU.add, ALU.mult).then_inc(S["pos_sb"], 1)
            link(V.tensor_copy(chunk[:, 0:1], ps[0:EXPERTS, 6, 0:1]))
            link(V.tensor_scalar(chunk[:, 3:4], chunk[:, 0:1], float(CAP), None, ALU.is_gt))
            link(V.tensor_scalar(chunk[:, 1:2], chunk[:, 0:1], float(2 * CAP), None, ALU.is_gt))
            link(V.tensor_scalar(chunk[:, 2:3], chunk[:, 0:1], float(3 * CAP), None, ALU.is_gt))
            link(V.tensor_tensor(chunk[:, 3:4], chunk[:, 3:4], chunk[:, 1:2], ALU.add))
            V.tensor_tensor(chunk[:, 3:4], chunk[:, 3:4], chunk[:, 2:3], ALU.add).then_inc(S["extra_set"], 1)
            dve.wait_ge(S["extra_set"], 1)
            dve.wait_ge(S["cum_up"], 1)
            link(V.tensor_copy(chunk[:, 4:5], ps[0:EXPERTS, 6, 1:2]))
            link(V.tensor_tensor(chunk[:, 5:6], chunk[:, 4:5], chunk[:, 3:4], ALU.subtract))
            iq = cst[0:EXPERTS, C_Q:C_Q + OVER]
            oh, base, hs = (hot[0:EXPERTS, j, EXPERTS:ITEMS] for j in range(3))
            link(V.tensor_scalar(oh, iq, chunk[:, 5:6], None, ALU.is_ge))
            link(V.tensor_scalar(hs, iq, chunk[:, 4:5], None, ALU.is_lt))
            link(V.tensor_tensor(oh, oh, hs, ALU.mult))
            link(V.tensor_scalar(base, iq, chunk[:, 5:6], 1.0, ALU.subtract, ALU.add))
            link(V.scalar_tensor_tensor(base, base, -float(CAP), oh, ALU.mult, ALU.mult))
            V.tensor_copy(hot[0:EXPERTS, 0, 0:EXPERTS], cst[0:EXPERTS, C_ID32:C_ID32 + EXPERTS]).then_inc(S["hot_set"], 1)
            dve.wait_ge(S["xm_set"], 1)
            V.tensor_tensor(xpart[:, 2], gate_rest, xpart[:, 1], ALU.subtract).then_inc(S["x_split"], 1)
            dve.wait_ge(S["x_split"], 1)
            for col in (0, COLS - 1):
                link(V.memset(posI[:, :, col:col + 1], 0.0))
                link(V.memset(wI[:, :, col:col + 1], 0.0))
            dve.wait_ge(S["item_up"], 1)
            V.tensor_copy(posI[:, :, 1:1 + ITEMS], ps[:, 4, 0:TT * 48].rearrange("p (i n) -> p i n", i=TT)[:, :, 0:ITEMS]).then_inc(S["item_sb"], 1)
            V.tensor_copy(wI[:, :, 1:1 + ITEMS], ps[:, 5, 0:TT * 48].rearrange("p (i n) -> p i n", i=TT)[:, :, 0:ITEMS]).then_inc(S["item_sb"], 1)
            V.tensor_copy(itab[:, 0:ITEMS], ps[0:1, 6, 8:8 + ITEMS]).then_inc(S["item_sb"], 1)
            V.tensor_scalar(icnt[:, 0:1], ps[0:1, 6, 2:3], float(EXPERTS), None, ALU.add).then_inc(S["item_sb"], 1)
            dve.wait_ge(S["item_sb"], 4)
            slots = cst[:, C_SLOT:C_SLOT + CAP]

            def choose(col):
                for t in range(TT):
                    last = V.tensor_scalar(pick[:, t, :], slots, posI[:, t, bass.ds(col, 1)], None, ALU.is_equal)
                    last.then_inc(S["pick_half" if t == 0 else "pick_set"], 1)

            def modulated(done):
                dve.wait_ge(S["hg_up"], done)
                V.tensor_tensor(hg, ps[:, 2, :].rearrange("p (f s) -> p f s", f=KD),
                                scale2[:, :].unsqueeze(2).to_broadcast([P, KD, CAP]), ALU.mult).then_inc(S["hg_half"], 1)
                dve.wait_ge(S["hg_half"], done)
                V.tensor_tensor(hg, hg, mod[:, SH2:SH2 + KD].unsqueeze(2).to_broadcast([P, KD, CAP]), ALU.add).then_inc(S["hg_sb"], 1)

            choose(1)
            modulated(1)
            dve.wait_ge(S["acc_set"], TT)
            count = dve.value_load(icnt[0:1, 0:1], min_val=EXPERTS, max_val=ITEMS)

            def weights_of(col, i):
                dve.wait_ge(S["pwT_up"], i)
                for t in range(TT):
                    for h in range(2):
                        last = V.tensor_scalar(pickw[:, t, h, CAP * h:CAP * h + CAP], slots, posI[:, t, bass.ds(col, 1)],
                                               wI[:, t, bass.ds(col, 1)], ALU.is_equal, ALU.mult)
                        last.then_inc(S["pickw_set" if t + h == 2 else "pickw_half"], 1)

            def expert_of(i):
                V.tensor_copy(hotb, hot[:, 0, bass.ds(i, 1)].to_broadcast([P, CAP])).then_inc(S["hotb_set"], 1)

            expert_of(0)
            dve.wait_ge(S["ysb_zero"], 1)

            def add_item(i):
                for t in range(TT):
                    for h in range(2):
                        dve.wait_ge(S["comb_up"], i * 4 + (2 * t + h + 1))
                        V.tensor_tensor(acc[:, t, 512 * h:512 * h + 512], acc[:, t, 512 * h:512 * h + 512], ps[:, 6 + h, :],
                                        ALU.add).then_inc(S["comb_add"], 1)

            with dve.Fori(0, ITEMS) as i:
                with dve.If(i < count):
                    dve.wait_ge(S["hg_up"], i + 1)
                    choose(i + 2)
                    weights_of(i, i)
                    dve.wait_ge(w_used, i * SLOTS + (PRE + GU_PIECES))
                    V.tensor_scalar(gate, ps[:, 0, :], LIMIT, None, ALU.min).then_inc(S["gated"], 1)
                    V.tensor_scalar(up, ps[:, 1, :], LIMIT, -LIMIT, ALU.min, ALU.max).then_inc(S["up_c"], 1)
                    dve.wait_ge(S["sig_set"], i + 1)
                    V.tensor_tensor(gate, gate, sig, ALU.mult).then_inc(S["gate_s"], 1)
                    dve.wait_ge(S["gate_s"], i + 1)
                    dve.wait_ge(S["up_c"], i + 1)
                    V.scalar_tensor_tensor(act_, up, 1.0, gate, ALU.add, ALU.mult).then_inc(S["act_set"], 1)
                    expert_of(i + 1)
                    modulated(i + 2)
                    add_item(i)
            weights_of(count, count)
            add_item(count)
            for i in range(TT):
                dve.wait_ge(S["comb_add"], count * 4 + 4)
                link(V.tensor_tensor(acc[:, i, :], acc[:, i, :], gate_ffn[:, :], ALU.mult))
                V.tensor_tensor(x_tok[:, i, :], x_tok[:, i, :], acc[:, i, :], ALU.add).then_inc(S["fin"], 1)
            for i in range(TT):
                dve.wait_ge(S["sq3"], i + 1)
                link(V.reciprocal(stat[:, 2, i:i + 1], stat[:, 1, i:i + 1]))
                V.scalar_tensor_tensor(x_tok[:, i, :], x_tok[:, i, :], stat[:, 2, i:i + 1], gfin, ALU.mult, ALU.mult).then_inc(S["fin_out"], 1)

    ctx.close()


_INS = ["x", "c", "w_ada", "b_ada", "g_mix", "w_in", "ssm_a_re", "ssm_a_im", "ssm_log_dt", "ssm_b_re", "ssm_b_im",
        "ssm_c_re", "ssm_c_im", "ssm_d", "w_glu", "w_attn_o", "w_out", "g_ffn", "w_router", "b_router", "w_gu", "b_gu",
        "w_down", "b_down", "g_final"]


def kernel(**inputs):
    from concourse import bacc
    from concourse.bass_utils import run_bass_kernel_spmd

    nc = bacc.Bacc("TRN2", target_bir_lowering=False, num_devices=1, dynamic_dma_scratch_size=1024)
    arrays = {f"in_{n}": np.ascontiguousarray(inputs[n]) for n in _INS}
    arrays["in_const"] = constants()
    args = [nc.dram_tensor(n, a.shape, F32, kind="ExternalInput").ap() for n, a in arrays.items()]
    out = nc.dram_tensor("out_0", (1, T, D), F32, kind="ExternalOutput").ap()
    build(nc, *args, out)
    r = run_bass_kernel_spmd(nc, [arrays], core_ids=[0])
    return r.results[0]["out_0"]
```

```python
from contextlib import ExitStack

import numpy as np

import concourse.bass as bass
from concourse import mybir

F32 = mybir.dt.float32
I32 = mybir.dt.int32
ALU = mybir.AluOpType
ACT = mybir.ActivationFunctionType
AX = mybir.AxisListType

P = 128
D = 1024
T = 256
TT = T // P
KD = D // P
W = D // 2
KW = W // P
HEADS, HD = 8, 64
G, N, C = 32, 64, 16
ST = G * N // P
EXPERTS, TOPK = 32, 4
CAP = 64
OVER = 15
ITEMS = EXPERTS + OVER
COLS = ITEMS + 2
SLOTS = 12
SLOT = 2048
EPS = 1e-5
LIMIT, ALPHA = 7.0, 1.702
THETA = 500000.0
HALF = HD // 8
TWO_PI = 2.0 * np.pi
ROUND = 1.5 * 2.0 ** 23

C_ID, C_COS, C_SIN, C_ROT, C_TRI, C_CAUSAL = 0, 128, 384, 640, 768, 896
C_SLOT, C_TRI32, C_ID32, C_Q, C_E, C_MB, C_MC = 1280, 1344, 1376, 1408, 1424, 1425, 1427
C_ALL = 1429
BF16 = mybir.dt.bfloat16
R_C, R_GMIX, R_GFFN, R_ADA, R_D, R_ALL = 0, 8, 16, 24, 72, 76
SH1, SC1, GT1, SH2, SC2, GT2 = (8 * j for j in range(6))


def constants():
    c = np.zeros((P, C_ALL), np.float32)
    p = np.arange(P)
    c[:, C_ID:C_ID + P] = np.eye(P)
    inv = (1.0 / THETA ** (np.arange(0, 2 * HALF, 2, dtype=np.float32) / (2 * HALF))).astype(np.float32)
    ang = np.arange(T, dtype=np.float32)[None, :] * inv[p % HALF][:, None]
    turned = (p % HD < 2 * HALF)[:, None]
    c[:, C_COS:C_COS + T] = np.where(turned, np.cos(ang), 1.0)
    c[:, C_SIN:C_SIN + T] = np.where(turned, np.sin(ang), 0.0)
    for j in range(P):
        if j % HD < HALF:
            c[j + HALF, C_ROT + j] = -1.0
        elif j % HD < 2 * HALF:
            c[j - HALF, C_ROT + j] = 1.0
    c[:, C_TRI:C_TRI + P] = p[:, None] < p[None, :]
    past = np.where(p[None, :] <= p[:, None], 0.0, -1e30)
    c[:, C_CAUSAL:C_CAUSAL + P] = past
    c[:, C_CAUSAL + 2 * P:C_CAUSAL + 3 * P] = past
    c[:, C_SLOT:C_SLOT + CAP] = np.arange(1, CAP + 1)
    e = np.arange(EXPERTS)
    c[:EXPERTS, C_TRI32:C_TRI32 + EXPERTS] = e[:, None] <= e[None, :]
    c[:EXPERTS, C_ID32:C_ID32 + EXPERTS] = np.eye(EXPERTS)
    c[:, C_Q:C_Q + OVER + 1] = np.arange(OVER + 1)
    c[:EXPERTS, C_E] = e
    c[:, C_MB:C_MB + 2] = (p // N)[:, None] == np.arange(2)
    c[:, C_MC:C_MC + 2] = (p % (2 * C) // C)[:, None] == np.arange(2)
    return c


def build(nc, x, c, w_ada, b_ada, g_mix, w_in, a_re, a_im, log_dt, b_re, b_im, c_re, c_im, ssm_d,
          w_glu, w_attn_o, w_out, g_ffn, w_router, b_router, w_gu, b_gu, w_down, b_down, g_final,
          const, out):
    ctx = ExitStack()

    def sb(name, shape, dt=F32):
        return ctx.enter_context(nc.sbuf_tensor(name, shape, dt))

    def sem(name):
        return ctx.enter_context(nc.semaphore(name))

    ring = sb("ring", [P, SLOTS, SLOT])
    x_tok = sb("x_tok", [P, TT, D])
    xn_tok = sb("xn_tok", [P, TT, D])
    hT = sb("hT", [P, KD, T])
    cst = sb("cst", [P, C_ALL])
    ones = sb("ones", [P, P])
    cols = sb("cols", [P, R_ALL])
    mod = sb("mod", [P, 6 * KD])
    scale1 = sb("scale1", [P, KD])
    scale2 = sb("scale2", [P, KD])
    cond = sb("cond", [P, KD])
    condb = sb("condb", [P, KD, 32])
    stat = sb("stat", [P, 4, TT])
    ident = cst[:, C_ID:C_ID + P]

    zone = sb("zone", [P, 19456])
    at = [0]

    def cut(n):
        at[0] += n
        assert at[0] <= zone.shape[1]
        return zone[:, at[0] - n:at[0]]

    ecos = cut(ST * T).rearrange("p (s t) -> p s t", s=ST)
    esin = cut(ST * T).rearrange("p (s t) -> p s t", s=ST)
    uT = cut(KW * T).rearrange("p (m t) -> p m t", m=KW)
    qT = cut(KW * T).rearrange("p (m t) -> p m t", m=KW)
    kT = cut(KW * T).rearrange("p (m t) -> p m t", m=KW)
    oT = cut(KW * T).rearrange("p (m t) -> p m t", m=KW)
    v_tok = cut(TT * W).rearrange("p (i n) -> p i n", i=TT)
    gaT = xn_tok[:, :, :].rearrange("p i d -> p (i d)").rearrange("p (m t) -> p m t", m=KD)
    gbT = cut(KD * T).rearrange("p (m t) -> p m t", m=KD)
    z = cut(4 * 512).rearrange("p (b r n) -> p b r n", b=2, r=2)
    BT = cut(2 * KW * P).rearrange("p (r m n) -> p r m n", r=2, m=KW)
    CT = cut(2 * KW * P).rearrange("p (r m n) -> p r m n", r=2, m=KW)
    gates = z.rearrange("p b r n -> p (b r n)")
    gate_mix, gate_ffn = gates[:, 0:D], gates[:, D:2 * D]
    xs = sb("xs", [P, 2, 2, 512])
    tmp = sb("tmp", [P, 2, 512])
    ptmp = sb("ptmp", [P, 512])
    modrow = (ptmp[:, :], tmp[:, 0, :], tmp[:, 1, :])
    gluT = ecos.rearrange("p s t -> p (s t)")[:, 0:KW * T].rearrange("p (m t) -> p m t", m=KW)
    yaT = ecos.rearrange("p s t -> p (s t)")[:, 1024:3072].rearrange("p (m t) -> p m t", m=KD)
    sigb = ecos.rearrange("p s t -> p (s t)")[:, 3072:4096].rearrange("p (m t) -> p m t", m=KW)
    mergedT = esin.rearrange("p s t -> p (s t)")[:, 0:2048].rearrange("p (m t) -> p m t", m=KD)
    ybT = esin.rearrange("p s t -> p (s t)")[:, 2048:4096].rearrange("p (m t) -> p m t", m=KD)
    prob = sb("prob", [P, 3 * P])
    probT = sb("probT", [P, 3 * P])
    mx = sb("mx", [P, 2, 4])
    raw = v_tok.rearrange("p i n -> p (i n)")
    are, aim, ldt = raw[0:ST, 0:P], raw[0:ST, P:2 * P], raw[0:ST, 2 * P:2 * P + 2]
    rows = raw[0:R_ALL, 3 * P:4 * P]
    b_in = kT.rearrange("p m t -> p (m t)")[:, 0:512].rearrange("p (r s c) -> p r s c", r=2, s=ST)
    c_in = oT.rearrange("p m t -> p (m t)")[:, 0:512].rearrange("p (r m n) -> p r m n", r=2, m=KW)
    sprow = gbT.rearrange("p m t -> p (m t)")[0:ST, :].rearrange("p (j n) -> p j n", n=P)
    sprm = sb("sprm", [P, 5, ST])
    blk = z.rearrange("p b r n -> p (b r n)")
    Bblk = blk[:, 0:1024].rearrange("p (r s q c) -> p r s q c", r=2, s=ST, q=2)
    Cblk = blk[:, 1024:2048].rearrange("p (r m q n) -> p r m q n", r=2, m=KW, q=2)
    at[0] = 0
    acc = cut(TT * D).rearrange("p (i n) -> p i n", i=TT)
    hg = cut(KD * CAP).rearrange("p (f s) -> p f s", f=KD)
    gate, up, sig = cut(D // 2), cut(D // 2), cut(D // 2)
    act_ = cut(D // 2)
    actT = cut(D // 2).rearrange("p (j h s) -> p j h s", j=4, h=2)
    ysb = cut(D // 2)
    pickw = cut(2 * TT * P).rearrange("p (i h n) -> p i h n", i=TT, h=2)
    pickwT = cut(2 * T).rearrange("p (h t) -> p h t", h=2)
    pick = cut(TT * CAP // 2).bitcast(BF16).rearrange("p (i s) -> p i s", i=TT)
    hotb = cut(CAP)
    bgu_rows = cut(2 * D)
    bdn_rows = cut(D)
    gfin = cut(D)
    xpart = cut(3 * TT * D // 2).bitcast(BF16).rearrange("p (c i d) -> p c i d", c=3, i=TT)
    wr = cut(KD * EXPERTS).rearrange("p (k e) -> p k e", k=KD)
    rowT = cut(2 * T).rearrange("p (j t) -> p j t", j=2)
    rt = cut(6 * TT * EXPERTS).rearrange("p (j i e) -> p j i e", j=6, i=TT)
    lg = cut(TT * EXPERTS).rearrange("p (i e) -> p i e", i=TT)
    brt = cut(EXPERTS)
    top = cut(TT * 8).rearrange("p (i n) -> p i n", i=TT)
    rs = cut(TT * 4).rearrange("p (i n) -> p i n", i=TT)
    chunk = cut(8)[0:EXPERTS, :]
    assert at[0] <= 4096 * 2 + 1024 * 5 + 2048
    gate_rest = zone[:, 0:TT * D].rearrange("p (i d) -> p i d", i=TT)
    hot = sb("hot", [P, 3, 48])
    posI = sb("posI", [P, TT, COLS])
    wI = sb("wI", [P, TT, COLS])
    itab = sb("itab", [1, 48], I32)
    icnt = sb("icnt", [1, 2], I32)
    ps = ctx.enter_context(nc.psum_tensor("ps", [P, 8, 512], F32))

    arrived = [sem(f"arrived{s}") for s in range(SLOTS)]
    w_used = sem("w_used")
    names = """x_in const_in rows_in ssm_in bc_in late_in out_stored
        ones_set cols_up cols_sb cond_set ssm_rows sprm_up sprm_sb Bblk_set Cblk0_set Cblk1_set
        BT_up CT0_up CT1_up BT_sb CT0_sb CT1_sb phases mod_up modrow_sb modT_up mod1_sb sq1 xn1 xT_up h_sb
        proj_up proj_sb bu_up bu_read scanned z_read xs_set xs_read rot_up rot_read rope_set
        sc_up sc_read negmax expd probs probsT_up probsT_sb o_up o_sb mod2_up mod2_sb row_up row_sb y_skip gelu
        sig_ga sig_gb a_up sigb_set ya_set yb_up yb_used merged out_up x1 sq2 xn2 x2T_up h2_sb logit_up
        logit_sb top_set ex_set sel_set pos_up pos_sb rT_up rT_sb extra_set cum_up hot_set item_up item_sb zeroed
        hotb_set bias_up acc_set pick_set hg_up hg_sb gu_up gated sig_set act_set y_sb pickw_set pwT_up
        pwT_sb actT_up actT_sb comb_up comb_add ysb_zero exp_end fin sq3 fin_out
        dt_set mag_set trig_set lrdt_set angle_set phase_lo pick_half pickw_half hg_half gates_up up_c gate_s xh_set xr_set xm_set x_split
        scale1_set turn turned row_max probs_half sqsum2 sqsum3 acc_half lnD lnA lnP cond_half""".split()
    S = {n: sem(n) for n in names}

    def linker(eng, s):
        count = [0]

        def link(ins):
            count[0] += 1
            ins.then_inc(s, 1)
            eng.wait_ge(s, count[0])
        return link

    def square(eng, link, n):
        a, b = ecos[:, :, n // 2:n // 2 + 1], esin[:, :, n // 2:n // 2 + 1]
        c1, s1 = ecos[:, :, n + 1:n + 2], esin[:, :, n + 1:n + 2]
        link(eng.tensor_tensor(c1, a, a, ALU.mult))
        link(eng.tensor_tensor(s1, b, b, ALU.mult))
        link(eng.tensor_tensor(ecos[:, :, n:n + 1], c1, s1, ALU.subtract))
        link(eng.tensor_tensor(c1, a, b, ALU.mult))
        link(eng.tensor_tensor(esin[:, :, n:n + 1], c1, c1, ALU.add))

    def double(eng, link, n, scratch):
        w = min(ST, 512 // n)
        for s in range(0, ST, w):
            shape = [P, w, n - 1]
            cn, sn = (e[:, s:s + w, n:n + 1].to_broadcast(shape) for e in (ecos, esin))
            ct, st = ecos[:, s:s + w, 1:n], esin[:, s:s + w, 1:n]
            t0, t1 = (scratch[:, r, 0:w * (n - 1)].rearrange("p (s t) -> p s t", s=w) for r in range(2))
            link(eng.tensor_tensor(t0, ct, cn, ALU.mult))
            link(eng.tensor_tensor(t1, st, sn, ALU.mult))
            link(eng.tensor_tensor(ecos[:, s:s + w, n + 1:2 * n], t0, t1, ALU.subtract))
            link(eng.tensor_tensor(t0, ct, sn, ALU.mult))
            link(eng.tensor_tensor(t1, st, cn, ALU.mult))
            link(eng.tensor_tensor(esin[:, s:s + w, n + 1:2 * n], t0, t1, ALU.add))

    def kp(w):
        return w.rearrange("(k p) n -> p k n", p=P)

    GROUPS = (1, 2, 0, 3, 4, 5, 6, 7)
    ada, win, glu, wao, wo = kp(w_ada[0]), kp(w_in[0]), kp(w_glu[0]), kp(w_attn_o[0]), kp(w_out[0])
    pieces = [ada[:, k:k + 1, 0:2 * D] for k in range(KD)]
    pieces += [win[:, 4 * h:4 * h + 4, W * g:W * g + W] for g in GROUPS for h in range(2)]
    pieces += [ada[:, k:k + 1, 2 * D * j:2 * D * (j + 1)] for j in (1, 2) for k in range(KD)]
    pieces += [glu[:, :, W * j:W * j + W] for j in (0, 2, 1, 3)]
    pieces += [wao[:, :, W * j:W * j + W] for j in range(2)]
    pieces += [wo[:, 2 * j:2 * j + 2, :] for j in range(4)]
    PRE = len(pieces)
    PIECE_ADA1, PIECE_IN, PIECE_ADA2, PIECE_GLU, PIECE_AO, PIECE_OUT = 0, 8, 24, 40, 44, 46
    GU_PIECES, DN_PIECES = 8, 4
    slot_of = [(PRE + j) % SLOTS for j in range(SLOTS)]
    round_of = [(PRE + j) // SLOTS for j in range(SLOTS)]

    BIAS_BANKS = ((0, 1), (7, 2))

    def slot(n, k):
        return ring[:, n % SLOTS, :].rearrange("p (k n) -> p k n", k=k)

    with nc.Block() as block:

        @block.sync
        def _(sp):
            sp.dma_start(rows[R_C:R_C + KD, :], c.rearrange("a (k p) -> (a k) p", p=P)).then_inc(S["rows_in"], 16)
            sp.dma_start(rows[R_GMIX:R_GMIX + KD, :], g_mix.rearrange("a (k p) -> (a k) p", p=P)).then_inc(S["rows_in"], 16)
            sp.dma_start(rows[R_GFFN:R_GFFN + KD, :], g_ffn.rearrange("a (k p) -> (a k) p", p=P)).then_inc(S["rows_in"], 16)
            sp.dma_start(rows[R_ADA:R_ADA + 6 * KD, :], b_ada.rearrange("a (k p) -> (a k) p", p=P)).then_inc(S["rows_in"], 16)
            sp.dma_start(rows[R_D:R_D + KW, :], ssm_d.rearrange("a (k p) -> (a k) p", p=P)).then_inc(S["rows_in"], 16)
            sp.dma_start(cst[:, :], const).then_inc(S["const_in"], 16)
            for n, src in enumerate(pieces):
                if n >= SLOTS:
                    sp.wait_ge(w_used, n - SLOTS + 1)
                sp.dma_start(slot(n, src.shape[1]), src).then_inc(arrived[n % SLOTS], 16)
                if n == 3:
                    sp.dma_start(x_tok[:, :, :], x[0].rearrange("(i p) d -> p i d", p=P)).then_inc(S["x_in"], 16)

            def expert_load(item, e):
                gu = w_gu[0, bass.ds(e, 1)].rearrange("e (k p) n -> p (e k) n", p=P)
                dn = w_down[0, bass.ds(e, 1)].rearrange("e (k p) n -> p (e k) n", p=P)
                for j in range(SLOTS):
                    sp.wait_ge(w_used, item * SLOTS + (PRE + j - SLOTS + 1))
                    src = gu[:, j:j + 1, :] if j < GU_PIECES else dn[:, 2 * (j - GU_PIECES):2 * (j - GU_PIECES) + 2, :]
                    sp.dma_start(slot(PRE + j, src.shape[1]), src).then_inc(arrived[slot_of[j]], 16)

            with sp.Fori(0, EXPERTS) as i:
                expert_load(i, i)
            sp.wait_ge(S["item_sb"], 4)
            count = sp.value_load(icnt[0:1, 0:1], min_val=EXPERTS, max_val=ITEMS)
            with sp.If(count > EXPERTS):
                with sp.Fori(EXPERTS, ITEMS) as i:
                    with sp.If(i < count):
                        expert_load(i, sp.value_load(itab[0:1, bass.ds(i, 1)], min_val=0, max_val=EXPERTS - 1))
            for i in range(TT):
                sp.wait_ge(S["fin_out"], i + 1)
                sp.dma_start(out[0, P * i:P * i + P, :], x_tok[:, i, :]).then_inc(S["out_stored"], 16)
            sp.wait_ge(S["out_stored"], 16 * TT)

        @block.tensor
        def _(pe):
            mm = nc.tensor.matmul

            def take(n):
                pe.wait_ge(arrived[n % SLOTS], 16 * (n // SLOTS + 1))

            pe.wait_ge(S["rows_in"], 80)
            pe.wait_ge(S["const_in"], 16)
            nc.tensor.transpose(ps[:, 7, 0:R_ALL], rows[:, :], cst[0:R_ALL, C_ID:C_ID + R_ALL]).then_inc(S["cols_up"], 1)
            pe.wait_ge(S["cond_set"], 1)

            def modulation_products(first, bank, ks):
                for k in ks:
                    take(first + k)
                    w = slot(first + k, 1)
                    for j in range(4):
                        last = mm(ps[32 * j:32 * j + 32, bank, :], condb[:, k, :], w[:, 0, 512 * j:512 * j + 512],
                                  start=(k == 0), stop=(k == KD - 1), skip_group_check=True)
                    last.then_inc(w_used, 1)

            def modulation_columns(bank, n):
                pe.wait_ge(S["modrow_sb"], n + 1)
                for cb in range(4):
                    last = nc.tensor.transpose(ps[:, bank, P * cb:P * cb + P], modrow[n][:, P * cb:P * cb + P], ident)
                last.then_inc(S["modT_up"], 1)

            modulation_products(PIECE_ADA1, 5, range(4))
            pe.wait_ge(S["ssm_rows"], 1)
            for j in range(5):
                last = nc.tensor.transpose(ps[:, 6, ST * j:ST * j + ST], sprow[:, j, :], cst[0:ST, C_ID:C_ID + ST])
            last.then_inc(S["sprm_up"], 1)
            modulation_products(PIECE_ADA1, 5, range(4, 6))
            pe.wait_ge(S["xn1"], TT)
            for k in range(KD):
                for i in range(TT):
                    last = nc.tensor.transpose(ps[:, k // 2, (k % 2) * T + P * i:(k % 2) * T + P * i + P],
                                               xn_tok[:, i, P * k:P * k + P], ident)
            last.then_inc(S["xT_up"], 1)
            modulation_products(PIECE_ADA1, 5, range(6, 8))
            pe.wait_ge(S["Bblk_set"], 1)
            pe.wait_ge(S["sprm_sb"], 1)
            for r in range(2):
                for m in range(KW):
                    last = nc.tensor.transpose(ps[:, 6 + r, P * m:P * m + P],
                                               Bblk[:, r, 4 * m:4 * m + 4].rearrange("p s q c -> p (s q c)"), ident)
            last.then_inc(S["BT_up"], 1)
            modulation_columns(5, 0)
            for r in range(2):
                pe.wait_ge(S[f"Cblk{r}_set"], 1)
                if r == 1:
                    pe.wait_ge(S["BT_sb"], 1)
                for m in range(KW):
                    last = nc.tensor.transpose(ps[:, 4 + 2 * r, P * m:P * m + P],
                                               Cblk[:, r, m].rearrange("p q n -> p (q n)"), ident)
                last.then_inc(S[f"CT{r}_up"], 1)

            def proj(g, h):
                n = PIECE_IN + 2 * g + h
                take(n)
                w = slot(n, 4)
                b = 2 * (g % 2)
                if h == 0:
                    if g < 2:
                        pe.wait_ge(S["h_sb"], KD)
                    else:
                        pe.wait_ge(S["proj_sb"], g - 1)
                for kk in range(4):
                    k = 4 * h + kk
                    if g == 3:
                        for i in range(TT):
                            last = mm(ps[:, b + i, :], hT[:, k, P * i:P * i + P], w[:, kk, :], start=(k == 0), stop=(k == KD - 1))
                    else:
                        for m in range(4):
                            last = mm(ps[:, b + m // 2, (m % 2) * T:(m % 2) * T + T], w[:, kk, P * m:P * m + P], hT[:, k, :],
                                      start=(k == 0 and m % 2 == 0), stop=(k == KD - 1), skip_group_check=True)
                last.then_inc(w_used, 1)

            def b_u(j):
                if j == 0:
                    pe.wait_ge(S["proj_sb"], 3)
                    pe.wait_ge(S["rot_read"], 2)
                else:
                    pe.wait_ge(S["bu_read"], j)
                for q in range(2):
                    s = 2 * j + q
                    a = 32 * (s % 4)
                    for r in range(2):
                        last = mm(ps[:, 4 + q, T * r:T * r + T], BT[a:a + 32, r, s // 4, :], uT[a:a + 32, s // 4, :],
                                  start=True, stop=True, skip_group_check=True)
                last.then_inc(S["bu_up"], 1)

            def c_x(j):
                pe.wait_ge(S["xs_set"], j + 1)
                if j == 0:
                    pe.wait_ge(S["CT1_sb"], 1)
                if j % 2 == 0 and j >= 2:
                    pe.wait_ge(S["y_skip"], j // 2)
                for q in range(2):
                    s = 2 * j + q
                    m, a = s // 4, 32 * (s % 4)
                    for r in range(2):
                        last = mm(ps[a:a + 32, 6, (m % 2) * T:(m % 2) * T + T], CT[:, r, m, a:a + 32],
                                  xs[:, j % 2, r, T * q:T * q + T], start=(r == 0), stop=(r == 1), skip_group_check=True)
                last.then_inc(S["xs_read"], 1)

            def rotate(src, n):
                pe.wait_ge(S["proj_sb"], 1 + n)
                if n == 0:
                    pe.wait_ge(S["CT0_sb"], 1)
                    pe.wait_ge(S["mod1_sb"], 1)
                else:
                    pe.wait_ge(S["rot_read"], 1)
                for m in range(KW):
                    last = mm(ps[:, 4 + m // 2, (m % 2) * T:(m % 2) * T + T], cst[:, C_ROT:C_ROT + P], src[:, m, :],
                              start=True, stop=True, skip_group_check=True)
                last.then_inc(S["rot_up"], 1)

            def scores(h):
                if h == 0:
                    pe.wait_ge(S["rope_set"], 2)
                    pe.wait_ge(S["BT_sb"], 1)
                else:
                    pe.wait_ge(S["o_sb"], h)
                a, m = HD * (h % 2), h // 2
                mm(ps[:, 7, 0:P], qT[a:a + HD, m, 0:P], kT[a:a + HD, m, 0:P], start=True, stop=True, skip_group_check=True)
                mm(ps[:, 7, P:3 * P], qT[a:a + HD, m, P:T], kT[a:a + HD, m, :], start=True, stop=True,
                   skip_group_check=True).then_inc(S["sc_up"], 1)

            def weigh(h):
                a = HD * (h % 2)
                pe.wait_ge(S["probs"], h + 1)
                for j in range(3):
                    last = nc.tensor.transpose(ps[:, 7, P * j:P * j + P], prob[:, P * j:P * j + P], ident)
                last.then_inc(S["probsT_up"], 1)
                pe.wait_ge(S["probsT_sb"], h + 1)
                mm(ps[a:a + HD, 7, 0:T], v_tok[:, 0, HD * h:HD * h + HD], probT[:, 0:T], start=True, stop=False,
                   skip_group_check=True)
                mm(ps[a:a + HD, 7, P:T], v_tok[:, 1, HD * h:HD * h + HD], probT[:, T:3 * P], start=False, stop=True,
                   skip_group_check=True).then_inc(S["o_up"], 1)

            for n in range(16):
                if n >= 8:
                    scores(n - 8)
                proj(n // 2, n % 2)
                if n == 2:
                    rotate(qT, 0)
                if n == 4:
                    rotate(kT, 1)
                if 6 <= n < 14:
                    b_u(n - 6)
                if n >= 10:
                    c_x(n - 10)
                if n >= 8:
                    weigh(n - 8)
            pe.wait_ge(S["proj_sb"], 7)
            modulation_products(PIECE_ADA2, 0, range(KD))
            c_x(6)
            modulation_columns(0, 1)
            c_x(7)
            modulation_products(PIECE_ADA2 + KD, 1, range(KD))
            modulation_columns(1, 2)
            pe.wait_ge(S["mod2_sb"], 1)
            pe.wait_ge(S["proj_sb"], 8)
            for j, t in enumerate((GT1, GT2)):
                for k in range(KD):
                    b = (2, 0)[j] + k // 4
                    last = mm(ps[:, b, P * (k % 4):P * (k % 4) + P], mod[:, t + k:t + k + 1].to_broadcast([P, P]), ident,
                              start=True, stop=True, skip_group_check=True)
                last.then_inc(S["row_up"], 1)
            for n, b in enumerate((0, 2, 4, 6)):
                take(PIECE_GLU + n)
                w = slot(PIECE_GLU + n, 4)
                if n == 0:
                    pe.wait_ge(S["row_sb"], 2)
                    pe.wait_ge(S["gelu"], 1)
                    pe.wait_ge(S["o_sb"], HEADS)
                for kk in range(KW):
                    for m in range(4):
                        last = mm(ps[:, b + m // 2, (m % 2) * T:(m % 2) * T + T], w[:, kk, P * m:P * m + P], gluT[:, kk, :],
                                  start=(kk == 0 and m % 2 == 0), stop=(kk == KW - 1), skip_group_check=True)
                last.then_inc(w_used, 1)
            for n in range(2):
                take(PIECE_AO + n)
                w = slot(PIECE_AO + n, 4)
                pe.wait_ge(S["ya_set"], 1)
                for kk in range(KW):
                    for m in range(4):
                        last = mm(ps[:, 2 * n + m // 2, (m % 2) * T:(m % 2) * T + T], w[:, kk, P * m:P * m + P], oT[:, kk, :],
                                  start=(kk == 0 and m % 2 == 0), stop=(kk == KW - 1), skip_group_check=True)
                last.then_inc(w_used, 1)
            for i in range(TT):
                for n in range(4):
                    w = slot(PIECE_OUT + n, 2)
                    if i == 0:
                        take(PIECE_OUT + n)
                        if n == 0:
                            pe.wait_ge(S["ya_set"], 2)
                        pe.wait_ge(S["merged"], 1 if n < 2 else 2)
                    for kk in range(2):
                        k = 2 * n + kk
                        for h in range(2):
                            last = mm(ps[:, 4 + 2 * i + h, :], mergedT[:, k, P * i:P * i + P], w[:, kk, 512 * h:512 * h + 512],
                                      start=(k == 0), stop=(k == KD - 1))
                    if i == TT - 1:
                        last.then_inc(w_used, 1)
                if i == 0:
                    last.then_inc(S["out_up"], 1)
            pe.wait_ge(S["yb_used"], 2)
            pe.wait_ge(S["x1"], 1)
            pe.wait_ge(S["late_in"], 80)
            for i in range(TT):
                pe.wait_ge(S["xn2"], i + 1)
                for k in range(KD):
                    last = nc.tensor.transpose(ps[:, 2 * i + k // 4, P * (k % 4):P * (k % 4) + P], xn_tok[:, i, P * k:P * k + P], ident)
                last.then_inc(S["x2T_up"], 1)
                pe.wait_ge(S["h2_sb"], KD * (i + 1))
                for k in range(KD):
                    for h in range(2):
                        a = P * i + CAP * h
                        last = mm(ps[CAP * h:CAP * h + CAP, 4 + i, 0:EXPERTS], hT[:, k, a:a + CAP], wr[:, k, :],
                                  start=(k == 0), stop=(k == KD - 1), skip_group_check=True)
                last.then_inc(S["logit_up"], 1)
            sel = rt[:, 0]
            tri = cst[:, C_TRI:C_TRI + P]
            pe.wait_ge(S["sel_set"], TT)
            pe.wait_ge(S["ones_set"], 1)
            pe.wait_ge(S["x1"], TT)
            for a in (0, CAP):
                for n, (lhs, src, dst) in enumerate(((tri, 0, 0), (ones, 0, 1), (tri, 1, 1))):
                    mm(ps[a:a + CAP, 7, EXPERTS * dst:EXPERTS * dst + EXPERTS], lhs[:, a:a + CAP], sel[:, src, :],
                       start=(n < 2), stop=(n != 1), skip_group_check=True)
            mm(ps[0:EXPERTS, 6, 0:1], sel[:, 0, :], ones[:, 0:1], start=True, stop=False, skip_group_check=True)
            mm(ps[0:EXPERTS, 6, 0:1], sel[:, 1, :], ones[:, 0:1], start=False, stop=True, skip_group_check=True).then_inc(S["pos_up"], 1)
            pe.wait_ge(S["pos_sb"], 1)
            for j, src in enumerate((rt[:, 1], rt[:, 2])):
                for i in range(TT):
                    last = nc.tensor.transpose(ps[0:EXPERTS, 3, T * j + P * i:T * j + P * i + P], src[:, i, :], ident)
            last.then_inc(S["rT_up"], 1)
            pe.wait_ge(S["extra_set"], 1)
            mm(ps[0:EXPERTS, 6, 1:2], cst[0:EXPERTS, C_TRI32:C_TRI32 + EXPERTS], chunk[:, 3:4], start=True, stop=True,
               skip_group_check=True)
            mm(ps[0:1, 6, 2:3], ones[0:EXPERTS, 0:1], chunk[:, 3:4], start=True, stop=True,
               skip_group_check=True).then_inc(S["cum_up"], 1)
            pe.wait_ge(S["rT_sb"], 1)
            for i in range(TT):
                for h in range(2):
                    last = mm(ps[:, BIAS_BANKS[i][h], :], rowT[:, 1, P * i:P * i + P], bdn_rows[:, 512 * h:512 * h + 512],
                              start=True, stop=True)
                last.then_inc(S["bias_up"], 1)
            pe.wait_ge(S["hot_set"], 1)
            for i in range(TT):
                for a in (0, CAP):
                    t = P * i + a
                    mm(ps[a:a + CAP, 4, 48 * i:48 * i + ITEMS], rowT[:, 0, t:t + CAP], hot[:, 0, 0:ITEMS], start=True, stop=False,
                       skip_group_check=True)
                    mm(ps[a:a + CAP, 4, 48 * i:48 * i + ITEMS], ones[:, 0:CAP], hot[:, 1, 0:ITEMS], start=False, stop=True,
                       skip_group_check=True)
                    mm(ps[a:a + CAP, 5, 48 * i:48 * i + ITEMS], rowT[:, 1, t:t + CAP], hot[:, 0, 0:ITEMS], start=True, stop=True,
                       skip_group_check=True)
            mm(ps[0:1, 6, 8:8 + ITEMS], cst[:, C_E:C_E + 1], hot[:, 0, 0:ITEMS], start=True, stop=True,
               skip_group_check=True).then_inc(S["item_up"], 1)

            def gather():
                for f in range(KD):
                    for i in range(TT):
                        for c in range(3):
                            last = mm(ps[:, 2, CAP * f:CAP * f + CAP], xpart[:, c, i, P * f:P * f + P], pick[:, i, :],
                                      start=(i == 0 and c == 0), stop=(i == TT - 1 and c == 2), skip_group_check=True)
                last.then_inc(S["hg_up"], 1)

            pe.wait_ge(S["pick_set"], 1)
            pe.wait_ge(S["x_split"], TT)
            pe.wait_ge(S["acc_set"], 2)
            gather()
            pe.wait_ge(S["ysb_zero"], 1)
            pe.wait_ge(S["item_sb"], 4)
            count = pe.value_load(icnt[0:1, 0:1], min_val=EXPERTS, max_val=ITEMS)

            def combine(i):
                pe.wait_ge(S["pickw_set"], i + 1)
                for t in range(TT):
                    for h in range(2):
                        last = nc.tensor.transpose(ps[:, 5, T * h + P * t:T * h + P * t + P], pickw[:, t, h, :], ident)
                last.then_inc(S["pwT_up"], 1)
                pe.wait_ge(S["y_sb"], i)
                pe.wait_ge(S["pwT_sb"], i + 1)
                for t in range(TT):
                    for h in range(2):
                        if t + h:
                            pe.wait_ge(S["comb_add"], i * 4 + (2 * t + h - 1))
                        else:
                            pe.wait_ge(S["comb_add"], i * 4)
                        mm(ps[:, 6 + h, :], pickwT[:, h, P * t:P * t + P], ysb, start=True, stop=True).then_inc(S["comb_up"], 1)

            def item(i):
                pe.wait_ge(S["hotb_set"], i + 1)
                for b in range(2):
                    for h in range(2):
                        mm(ps[CAP * h:CAP * h + CAP, b, :], hotb, bgu_rows[:, D * b + 512 * h:D * b + 512 * h + 512],
                           start=True, stop=False, skip_group_check=True)
                pe.wait_ge(S["hg_sb"], i + 1)
                for j in range(GU_PIECES):
                    pe.wait_ge(arrived[slot_of[j]], i * 16 + 16 * (round_of[j] + 1))
                    w = slot(PRE + j, 1)
                    for b in range(2):
                        for h in range(2):
                            last = mm(ps[CAP * h:CAP * h + CAP, b, :], hg[:, j, :],
                                      w[:, 0, D * b + 512 * h:D * b + 512 * h + 512],
                                      start=False, stop=(j == GU_PIECES - 1), skip_group_check=True)
                    last.then_inc(w_used, 1)
                pe.wait_ge(S["pick_set"], i + 2)
                gather()
                combine(i)
                pe.wait_ge(S["act_set"], i + 1)
                for j in range(4):
                    last = nc.tensor.transpose(ps[:, 4, P * j:P * j + P], act_[:, P * j:P * j + P], ident)
                last.then_inc(S["actT_up"], 1)
                pe.wait_ge(S["actT_sb"], i + 1)
                for j in range(DN_PIECES):
                    pe.wait_ge(arrived[slot_of[GU_PIECES + j]], i * 16 + 16 * (round_of[GU_PIECES + j] + 1))
                    w = slot(PRE + GU_PIECES + j, 2)
                    for kk in range(2):
                        k = 2 * j + kk
                        for h in range(2):
                            last = mm(ps[CAP * h:CAP * h + CAP, 3, :], actT[:, k % 4, k // 4, :], w[:, kk, 512 * h:512 * h + 512],
                                      start=(k == 0), stop=(k == KD - 1), skip_group_check=True)
                    last.then_inc(w_used, 1)

            with pe.Fori(0, EXPERTS) as i:
                item(i)
            with pe.If(count > EXPERTS):
                with pe.Fori(EXPERTS, ITEMS) as i:
                    with pe.If(i < count):
                        item(i)
            combine(count)

        @block.scalar
        def _(act):
            link = linker(act, S["lnA"])
            act.dma_start(are[:, :], a_re[0].rearrange("(s q) p -> s (q p)", q=2)).then_inc(S["ssm_in"], 16)
            act.dma_start(aim[:, :], a_im[0].rearrange("(s q) p -> s (q p)", q=2)).then_inc(S["ssm_in"], 16)
            act.dma_start(ldt[:, :], log_dt.rearrange("a (s q) -> (a s) q", q=2)).then_inc(S["ssm_in"], 16)
            act.wait_ge(S["cols_sb"], 1)
            nc.scalar.activation(cond[:, :], cols[:, R_C:R_C + KD], ACT.Sigmoid).then_inc(S["cond_half"], 1)
            for r, (b, cc) in enumerate(((b_re, c_re), (b_im, c_im))):
                act.dma_start(b_in[:, r], b[0].rearrange("(s q) p c -> (q p) s c", q=2)).then_inc(S["bc_in"], 16)
                act.dma_start(c_in[:, r], cc[0].rearrange("(m g) c p -> (g c) m p", m=KW)).then_inc(S["bc_in"], 16)
            act.wait_ge(S["ssm_in"], 48)
            nc.scalar.activation(ldt[:, :], ldt[:, :], ACT.Exp).then_inc(S["dt_set"], 1)
            act.wait_ge(S["lrdt_set"], 1)
            nc.scalar.activation(sprow[:, 0, :], sprow[:, 5, :], ACT.Exp).then_inc(S["mag_set"], 1)
            act.wait_ge(S["angle_set"], 1)
            nc.scalar.activation(sprow[:, 2, :], sprow[:, 6, :], ACT.Sin).then_inc(S["trig_set"], 1)
            nc.scalar.activation(sprow[:, 7, :], sprow[:, 6, :], ACT.Sin, scale=0.5).then_inc(S["trig_set"], 1)
            act.wait_ge(S["x_in"], 16)
            act.wait_ge(S["lnD"], 1)
            for i in range(TT):
                link(nc.scalar.activation(hT[:, 4 * i:4 * i + 4, :].rearrange("p k t -> p (k t)"), x_tok[:, i, :], ACT.Square,
                                          accum_out=stat[:, 0, i:i + 1]))
            nc.scalar.activation(stat[:, 1, :], stat[:, 0, :], ACT.Sqrt, bias=stat[:, 3, 0:1], scale=1.0 / D).then_inc(S["sq1"], 1)
            def row_copy(n):
                act.wait_ge(w_used, (KD, PIECE_ADA2 + KD, PIECE_ADA2 + 2 * KD)[n])
                nc.scalar.copy(modrow[n], ps[:, (5, 0, 1)[n], :]).then_inc(S["modrow_sb"], 1)

            act.wait_ge(S["BT_up"], 1)
            nc.scalar.copy(BT[:, :, :, :].rearrange("p r m n -> p (r m n)"), ps[:, 6:8, :].rearrange("p b n -> p (b n)")).then_inc(S["BT_sb"], 1)
            row_copy(0)
            act.wait_ge(S["mod1_sb"], 1)
            act.wait_ge(S["scale1_set"], 1)
            act.wait_ge(S["xT_up"], 1)
            for k in range(KD // 2, KD):
                nc.scalar.activation(hT[:, k, :], ps[:, k // 2, (k % 2) * T:(k % 2) * T + T], ACT.Identity,
                                     bias=mod[:, SH1 + k:SH1 + k + 1], scale=scale1[:, k:k + 1]).then_inc(S["h_sb"], 1)
            for r in range(2):
                act.wait_ge(S[f"CT{r}_up"], 1)
                nc.scalar.activation(CT[:, r].rearrange("p m n -> p (m n)"), ps[:, 4 + 2 * r, :], ACT.Copy,
                                     scale=(1.0 if r == 0 else -1.0)).then_inc(S[f"CT{r}_sb"], 1)

            def head(h):
                act.wait_ge(S["negmax"], h + 1)
                for j, (a, b) in enumerate(((0, P), (P, 3 * P))):
                    last = nc.scalar.activation(prob[:, a:b], prob[:, a:b], ACT.Exp, bias=mx[:, h % 2, j:j + 1],
                                                scale=HD ** -0.5, accum_out=mx[:, h % 2, 2 + j:3 + j])
                    last.then_inc(S["expd"], 1)
                act.wait_ge(S["probsT_up"], h + 1)
                nc.scalar.copy(probT[:, :], ps[:, 7, 0:3 * P]).then_inc(S["probsT_sb"], 1)
                act.wait_ge(S["o_up"], h + 1)
                a = HD * (h % 2)
                nc.scalar.copy(oT[a:a + HD, h // 2, :], ps[a:a + HD, 7, 0:T]).then_inc(S["o_sb"], 1)

            for g, dst in enumerate((qT, kT, uT, v_tok, gaT[:, 0:4, :], gaT[:, 4:8, :], gbT[:, 0:4, :], gbT[:, 4:8, :])):
                act.wait_ge(w_used, PIECE_IN + 2 * g + 2)
                nc.scalar.copy(dst, ps[:, 2 * (g % 2):2 * (g % 2) + 2, :].rearrange(
                    "p b (m t) -> p (b m) t", t=dst.shape[2])).then_inc(S["proj_sb"], 1)
                if g >= 3 and g < 7:
                    head(2 * g - 6), head(2 * g - 5)
            row_copy(1)
            row_copy(2)
            for j, dst in enumerate((gate_mix, gate_ffn)):
                act.wait_ge(S["row_up"], j + 1)
                nc.scalar.copy(dst[:, :], ps[:, (2, 0)[j]:(2, 0)[j] + 2, :].rearrange("p b n -> p (b n)")).then_inc(S["row_sb"], 1)
            act.wait_ge(S["y_skip"], KW)
            nc.scalar.activation(gluT, uT, ACT.Gelu_apprx_tanh).then_inc(S["gelu"], 1)
            nc.scalar.activation(gaT, gaT, ACT.Sigmoid).then_inc(S["sig_ga"], 1)
            nc.scalar.activation(gbT, gbT, ACT.Sigmoid).then_inc(S["sig_gb"], 1)
            for h in range(2):
                act.wait_ge(w_used, PIECE_GLU + 2 * h + 2)
                if h == 1:
                    act.wait_ge(S["ya_set"], 1)
                nc.scalar.activation(sigb, ps[:, 4 * h + 2:4 * h + 4, :].rearrange("p b (m t) -> p (b m) t", t=T), ACT.Sigmoid).then_inc(S["sigb_set"], 1)
            act.wait_ge(S["merged"], 2)
            act.dma_start(wr[:, :, :], w_router[0].rearrange("(k p) e -> p k e", p=P)).then_inc(S["late_in"], 16)
            act.dma_start(brt[:, :], b_router.to_broadcast([P, EXPERTS])).then_inc(S["late_in"], 16)
            act.wait_ge(S["zeroed"], 1)
            act.dma_start(bgu_rows[0:EXPERTS, :], b_gu[0]).then_inc(S["late_in"], 16)
            act.dma_start(bdn_rows[0:EXPERTS, :], b_down[0]).then_inc(S["late_in"], 16)
            act.dma_start(gfin, g_final.rearrange("(a d) -> a d", a=1).to_broadcast([P, D])).then_inc(S["late_in"], 16)
            for i in range(TT):
                act.wait_ge(S["x1"], i + 1)
                nc.scalar.activation(hT[:, 4 * i:4 * i + 4, :].rearrange("p k t -> p (k t)"), x_tok[:, i, :], ACT.Square,
                                     accum_out=stat[:, 0, i:i + 1]).then_inc(S["sqsum2"], 1)
                act.wait_ge(S["sqsum2"], i + 1)
                nc.scalar.activation(stat[:, 1, i:i + 1], stat[:, 0, i:i + 1], ACT.Sqrt, bias=stat[:, 3, 0:1], scale=1.0 / D).then_inc(S["sq2"], 1)
            for i in range(TT):
                act.wait_ge(S["x2T_up"], i + 1)
                for k in range(KD):
                    nc.scalar.activation(hT[:, k, P * i:P * i + P], ps[:, 2 * i + k // 4, P * (k % 4):P * (k % 4) + P], ACT.Identity,
                                         bias=mod[:, SH2 + k:SH2 + k + 1], scale=scale2[:, k:k + 1]).then_inc(S["h2_sb"], 1)
                nc.scalar.copy(xpart[:, 0, i], xn_tok[:, i, :]).then_inc(S["xh_set"], 1)
                act.wait_ge(S["top_set"], i + 1)
                nc.scalar.activation(rt[:, 3, i, :], lg[:, i, :], ACT.Exp, bias=rs[:, i, 0:1]).then_inc(S["ex_set"], 1)
                act.wait_ge(S["xr_set"], i + 1)
                nc.scalar.copy(xpart[:, 1, i], gate_rest[:, i, :]).then_inc(S["xm_set"], 1)
            act.wait_ge(S["rT_up"], 1)
            act.wait_ge(S["zeroed"], 1)
            nc.scalar.copy(rowT[0:EXPERTS, :, :].rearrange("p j t -> p (j t)"), ps[0:EXPERTS, 3, :]).then_inc(S["rT_sb"], 1)
            act.wait_ge(S["x_split"], TT)
            for i in range(TT):
                act.wait_ge(S["bias_up"], i + 1)
                for h in range(2):
                    last = nc.scalar.copy(acc[:, i, 512 * h:512 * h + 512], ps[:, BIAS_BANKS[i][h], :])
                    last.then_inc(S["acc_half" if h == 0 else "acc_set"], 1)
            act.wait_ge(S["item_sb"], 4)
            count = act.value_load(icnt[0:1, 0:1], min_val=EXPERTS, max_val=ITEMS)

            def combine_copies(i):
                act.wait_ge(S["pwT_up"], i + 1)
                nc.scalar.copy(pickwT.rearrange("p h t -> p (h t)"), ps[:, 5, :]).then_inc(S["pwT_sb"], 1)

            def item(i):
                act.wait_ge(S["gated"], i + 1)
                nc.scalar.activation(sig, gate, ACT.Sigmoid, scale=ALPHA).then_inc(S["sig_set"], 1)
                combine_copies(i)
                act.wait_ge(S["actT_up"], i + 1)
                nc.scalar.copy(actT.rearrange("p j h s -> p (j h s)"), ps[:, 4, :]).then_inc(S["actT_sb"], 1)
                act.wait_ge(w_used, i * SLOTS + (PRE + SLOTS))
                nc.scalar.copy(ysb, ps[:, 3, :]).then_inc(S["y_sb"], 1)

            with act.Fori(0, EXPERTS) as i:
                item(i)
            with act.If(count > EXPERTS):
                with act.Fori(EXPERTS, ITEMS) as i:
                    with act.If(i < count):
                        item(i)
            combine_copies(count)
            for i in range(TT):
                act.wait_ge(S["fin"], i + 1)
                nc.scalar.activation(xn_tok[:, i, :], x_tok[:, i, :], ACT.Square,
                                     accum_out=stat[:, 0, i:i + 1]).then_inc(S["sqsum3"], 1)
                act.wait_ge(S["sqsum3"], i + 1)
                nc.scalar.activation(stat[:, 1, i:i + 1], stat[:, 0, i:i + 1], ACT.Sqrt, bias=stat[:, 3, 0:1], scale=1.0 / D).then_inc(S["sq3"], 1)

        @block.gpsimd
        def _(pool):
            nc.gpsimd.memset(ones[:, :], 1.0).then_inc(S["ones_set"], 1)
            link = linker(pool, S["lnP"])
            pool.wait_ge(S["sprm_sb"], 1)
            link(nc.gpsimd.memset(ecos[:, :, 0:1], 1.0))
            link(nc.gpsimd.memset(esin[:, :, 0:1], 0.0))
            link(nc.gpsimd.tensor_copy(ecos[:, :, 1:2], sprm[:, 1, :].unsqueeze(2)))
            link(nc.gpsimd.tensor_copy(esin[:, :, 1:2], sprm[:, 2, :].unsqueeze(2)))
            for n in (2, 4, 8, 16, 32):
                square(nc.gpsimd, link, n)
                double(nc.gpsimd, link, n, xs[:, 0])
            pool.engine_nop().then_inc(S["phase_lo"], 1)
            for j in range(8):
                b = j % 2
                zr, zi = z[:, b, 0, :].rearrange("p (s t) -> p s t", s=2), z[:, b, 1, :].rearrange("p (s t) -> p s t", s=2)
                cs, sn = ecos[:, 2 * j:2 * j + 2, :], esin[:, 2 * j:2 * j + 2, :]
                xr, xi = xs[:, b, 0, :].rearrange("p (s t) -> p s t", s=2), xs[:, b, 1, :].rearrange("p (s t) -> p s t", s=2)
                t = ptmp[:, :].rearrange("p (s t) -> p s t", s=2)
                pool.wait_ge(S["scanned"], 4 * j + 4)
                if j == 0:
                    pool.wait_ge(S["phases"], 1)
                if j >= 2:
                    pool.wait_ge(S["xs_read"], j - 1)
                link(nc.gpsimd.tensor_tensor(xr, zr, cs, ALU.mult))
                link(nc.gpsimd.tensor_tensor(t, zi, sn, ALU.mult))
                link(nc.gpsimd.tensor_tensor(xr, xr, t, ALU.subtract))
                link(nc.gpsimd.tensor_tensor(xi, zr, sn, ALU.mult))
                link(nc.gpsimd.tensor_tensor(t, zi, cs, ALU.mult))
                nc.gpsimd.tensor_tensor(xi, xi, t, ALU.add).then_inc(S["xs_set"], 1)
                pool.wait_ge(S["xs_set"], j + 1)
            pool.wait_ge(S["merged"], 2)
            for dst in (bgu_rows, bdn_rows):
                link(nc.gpsimd.memset(dst, 0.0))
            nc.gpsimd.memset(rowT, 0.0).then_inc(S["zeroed"], 1)
            pool.wait_ge(w_used, PRE)
            link(nc.gpsimd.memset(pickw, 0.0))
            nc.gpsimd.memset(ysb, 0.0).then_inc(S["ysb_zero"], 1)

        @block.vector
        def _(dve):
            link = linker(dve, S["lnD"])
            V = nc.vector
            link(V.memset(stat[:, 3, :], EPS))
            for table in (hot, posI, wI):
                link(V.memset(table[:, :, :], 0.0))
            dve.wait_ge(S["cols_up"], 1)
            V.tensor_copy(cols[:, :], ps[:, 7, 0:R_ALL]).then_inc(S["cols_sb"], 1)
            dve.wait_ge(S["cols_sb"], 1)
            dve.wait_ge(S["cond_half"], 1)
            link(V.tensor_tensor(cond[:, :], cond[:, :], cols[:, R_C:R_C + KD], ALU.mult))
            V.tensor_copy(condb[:, :, :], cond[:, :].unsqueeze(2).to_broadcast([P, KD, 32])).then_inc(S["cond_set"], 1)
            dve.wait_ge(S["dt_set"], 1)
            dve.wait_ge(S["ssm_in"], 48)
            dtb = ldt[:, :].unsqueeze(2).to_broadcast([ST, 2, N])

            def mod_group(ap, n):
                return ap[:, 2 * KD * n:2 * KD * (n + 1)].rearrange("p (j c) -> p c j", j=4)

            def modT(bank):
                return ps[:, bank, :].rearrange("p (c j r) -> p c j r", c=4, j=4)[:, :, :, 0]

            def row(j):
                return sprow[:, j, :]

            def two(ap):
                return ap.rearrange("s (q n) -> s q n", q=2)

            V.tensor_tensor(two(row(5)), two(are[:, :]), dtb, ALU.mult).then_inc(S["lrdt_set"], 1)
            link(V.tensor_tensor(two(row(6)), two(aim[:, :]), dtb, ALU.mult))
            link(V.tensor_scalar(row(8), row(6), 1.0 / TWO_PI, ROUND, ALU.mult, ALU.add))
            link(V.tensor_scalar(row(8), row(8), -ROUND, None, ALU.add))
            parts, rest = [], TWO_PI
            for bits in (2.0 ** -6, 2.0 ** -16):
                parts.append(np.floor(rest / bits) * bits)
                rest -= parts[-1]
            for part in parts + [rest]:
                link(V.scalar_tensor_tensor(row(6), row(8), -float(part), row(6), ALU.mult, ALU.add))
            V.tensor_scalar(row(6), row(6), float(np.float32(3.1415925)), -float(np.float32(3.1415925)), ALU.min, ALU.max).then_inc(S["angle_set"], 1)
            dve.wait_ge(S["mag_set"], 1)
            dve.wait_ge(S["trig_set"], 2)
            link(V.tensor_tensor(row(1), row(7), row(7), ALU.mult))
            link(V.tensor_scalar(row(1), row(1), -2.0, 1.0, ALU.mult, ALU.add))
            link(V.tensor_tensor(row(8), row(0), row(1), ALU.mult))
            link(V.tensor_tensor(row(9), row(0), row(2), ALU.mult))
            link(V.tensor_scalar(row(8), row(8), -1.0, None, ALU.add))
            link(V.tensor_tensor(row(10), are[:, :], are[:, :], ALU.mult))
            link(V.tensor_tensor(row(11), aim[:, :], aim[:, :], ALU.mult))
            link(V.tensor_tensor(row(10), row(10), row(11), ALU.add))
            link(V.reciprocal(row(10), row(10)))
            link(V.tensor_tensor(row(11), row(8), are[:, :], ALU.mult))
            link(V.tensor_tensor(row(12), row(9), aim[:, :], ALU.mult))
            link(V.tensor_tensor(row(11), row(11), row(12), ALU.add))
            link(V.tensor_tensor(row(3), row(11), row(10), ALU.mult))
            link(V.tensor_tensor(row(11), row(9), are[:, :], ALU.mult))
            link(V.tensor_tensor(row(12), row(8), aim[:, :], ALU.mult))
            link(V.tensor_tensor(row(11), row(11), row(12), ALU.subtract))
            V.tensor_tensor(row(4), row(11), row(10), ALU.mult).then_inc(S["ssm_rows"], 1)
            dve.wait_ge(S["sq1"], 1)
            link(V.reciprocal(stat[:, 2, :], stat[:, 1, :]))
            for i in range(TT):
                V.tensor_scalar(xn_tok[:, i, :], x_tok[:, i, :], stat[:, 2, i:i + 1], None, ALU.mult).then_inc(S["xn1"], 1)
            dve.wait_ge(S["sprm_up"], 1)
            V.tensor_copy(sprm[:, :, :].rearrange("p j s -> p (j s)"), ps[:, 6, 0:5 * ST]).then_inc(S["sprm_sb"], 1)
            dve.wait_ge(S["sprm_sb"], 1)
            dve.wait_ge(S["bc_in"], 64)
            dve.wait_ge(S["const_in"], 16)
            cr = sprm[:, 3, :].unsqueeze(2).to_broadcast([P, ST, C])
            ci = sprm[:, 4, :].unsqueeze(2).to_broadcast([P, ST, C])
            t0 = tmp[:, 0, 0:256].rearrange("p (s c) -> p s c", s=ST)
            t1 = tmp[:, 0, 256:512].rearrange("p (s c) -> p s c", s=ST)
            for r in range(2):
                link(V.tensor_tensor(t0, b_in[:, r], cr, ALU.mult))
                link(V.tensor_tensor(t1, b_in[:, 1 - r], ci, ALU.mult))
                link(V.tensor_tensor(t0, t0, t1, ALU.subtract if r == 0 else ALU.add))
                for q in range(2):
                    last = V.tensor_scalar(Bblk[:, r, :, q, :], t0, cst[:, C_MB + q:C_MB + q + 1], None, ALU.mult)
                    if r == 0 or q == 0:
                        link(last)
            last.then_inc(S["Bblk_set"], 1)
            for r in range(2):
                for q in range(2):
                    last = V.tensor_scalar(Cblk[:, r, :, q, :], c_in[:, r], cst[:, C_MC + q:C_MC + q + 1], None, ALU.mult)
                    if q == 0:
                        link(last)
                last.then_inc(S[f"Cblk{r}_set"], 1)
            dve.wait_ge(S["modT_up"], 1)
            V.tensor_tensor(mod_group(mod, 0), modT(5), mod_group(cols[:, R_ADA:R_ADA + 6 * KD], 0), ALU.add).then_inc(S["mod1_sb"], 1)
            dve.wait_ge(S["mod1_sb"], 1)
            V.scalar_tensor_tensor(scale1[:, :], mod[:, SC1:SC1 + KD], 1.0, cols[:, R_GMIX:R_GMIX + KD], ALU.add, ALU.mult).then_inc(S["scale1_set"], 1)
            dve.wait_ge(S["scale1_set"], 1)
            dve.wait_ge(S["xT_up"], 1)
            for k in range(KD // 2):
                V.tensor_scalar(hT[:, k, :], ps[:, k // 2, (k % 2) * T:(k % 2) * T + T], scale1[:, k:k + 1],
                                mod[:, SH1 + k:SH1 + k + 1], ALU.mult, ALU.add).then_inc(S["h_sb"], 1)

            def rotary(n):
                dst = (qT, kT)[n]
                dve.wait_ge(S["rot_up"], n + 1)
                for m in range(KW):
                    t = tmp[:, m % 2, 0:T]
                    last = V.tensor_tensor(t, ps[:, 4 + m // 2, (m % 2) * T:(m % 2) * T + T], cst[:, C_SIN:C_SIN + T], ALU.mult)
                    if m == KW - 1:
                        last.then_inc(S["rot_read"], 1)
                        dve.wait_ge(S["rot_read"], n + 1)
                    else:
                        link(last)
                    link(V.tensor_tensor(dst[:, m, :], dst[:, m, :], cst[:, C_COS:C_COS + T], ALU.mult))
                    last = V.tensor_tensor(dst[:, m, :], dst[:, m, :], t, ALU.add)
                    if m < KW - 1:
                        link(last)
                last.then_inc(S["rope_set"], 1)
                dve.wait_ge(S["rope_set"], n + 1)

            def recurrence(j):
                b = j % 2
                cs, sn = ecos[:, 2 * j:2 * j + 2, :], esin[:, 2 * j:2 * j + 2, :]
                br, bi = (ps[:, 4:6, T * r:T * r + T] for r in range(2))
                tz = [tmp[:, r, :].rearrange("p (s t) -> p s t", s=2) for r in range(2)]
                zz = [z[:, b, r, :].rearrange("p (s t) -> p s t", s=2) for r in range(2)]
                dve.wait_ge(S["bu_up"], j + 1)
                if j >= 2:
                    dve.wait_ge(S["xs_set"], j - 1)
                V.tensor_tensor(zz[0], br, cs, ALU.mult).then_inc(S["turn"], 1)
                V.tensor_tensor(tz[0], bi, sn, ALU.mult).then_inc(S["turn"], 1)
                V.tensor_tensor(zz[1], bi, cs, ALU.mult).then_inc(S["turn"], 1)
                V.tensor_tensor(tz[1], br, sn, ALU.mult).then_inc(S["bu_read"], 1)
                dve.wait_ge(S["turn"], 3 * j + 3)
                dve.wait_ge(S["bu_read"], j + 1)
                V.tensor_tensor(zz[0], zz[0], tz[0], ALU.add).then_inc(S["turned"], 1)
                V.tensor_tensor(zz[1], zz[1], tz[1], ALU.subtract).then_inc(S["turned"], 1)
                for r in range(2):
                    dve.wait_ge(S["turned"], 2 * j + 1 + r)
                    for q in range(2):
                        s = 2 * j + q
                        last = V.tensor_tensor_scan(zz[r][:, q, :], sprm[:, 0, s:s + 1].to_broadcast([P, T]), zz[r][:, q, :], 0.0,
                                                    ALU.mult, ALU.add)
                        last.then_inc(S["scanned"], 1)

            def head(h):
                b = h % 2
                dve.wait_ge(S["sc_up"], h + 1)
                link(V.tensor_tensor(prob[:, :], ps[:, 7, 0:3 * P], cst[:, C_CAUSAL:C_CAUSAL + 3 * P], ALU.add))
                V.tensor_reduce(mx[:, b, 0:1], prob[:, 0:P], AX.X, ALU.max).then_inc(S["row_max"], 1)
                V.tensor_reduce(mx[:, b, 1:2], prob[:, P:3 * P], AX.X, ALU.max).then_inc(S["row_max"], 1)
                dve.wait_ge(S["row_max"], 2 * h + 2)
                V.tensor_scalar(mx[:, b, 0:2], mx[:, b, 0:2], -HD ** -0.5, None, ALU.mult).then_inc(S["negmax"], 1)
                dve.wait_ge(S["expd"], 2 * h + 2)
                link(V.reciprocal(mx[:, b, 2:4], mx[:, b, 2:4]))
                V.tensor_scalar(prob[:, 0:P], prob[:, 0:P], mx[:, b, 2:3], None, ALU.mult).then_inc(S["probs_half"], 1)
                V.tensor_scalar(prob[:, P:3 * P], prob[:, P:3 * P], mx[:, b, 3:4], None, ALU.mult).then_inc(S["probs"], 1)
                dve.wait_ge(S["probs_half"], h + 1)
                dve.wait_ge(S["probs"], h + 1)

            def skip(m):
                dve.wait_ge(S["xs_read"], 2 * m + 2)
                V.scalar_tensor_tensor(uT[:, m, :], uT[:, m, :], cols[:, R_D + m:R_D + m + 1],
                                       ps[:, 6, (m % 2) * T:(m % 2) * T + T], ALU.mult, ALU.add).then_inc(S["y_skip"], 1)

            dve.wait_ge(S["phase_lo"], 1)
            square(V, link, T // 4)
            double(V, link, T // 4, tmp)
            rotary(0)
            square(V, link, T // 2)
            double(V, link, T // 2, tmp)
            V.engine_nop().then_inc(S["phases"], 1)
            rotary(1)
            dve.wait_ge(S["BT_up"], 1)
            dve.wait_ge(S["CT1_up"], 1)
            recurrence(0)
            recurrence(1)
            for h in range(HEADS):
                head(h)
                if h + 2 < 8:
                    recurrence(h + 2)
                if h in (3, 5):
                    skip((h - 3) // 2)
            skip(2)
            skip(3)
            for n in (1, 2):
                dve.wait_ge(S["modT_up"], n + 1)
                last = V.tensor_tensor(mod_group(mod, n), modT(n - 1), mod_group(cols[:, R_ADA:R_ADA + 6 * KD], n), ALU.add)
                if n == 1:
                    link(last)
            last.then_inc(S["mod2_sb"], 1)
            dve.wait_ge(S["mod2_sb"], 1)
            link(V.scalar_tensor_tensor(scale2[:, :], mod[:, SC2:SC2 + KD], 1.0, cols[:, R_GFFN:R_GFFN + KD], ALU.add, ALU.mult))
            for h in range(2):
                dve.wait_ge(S["sigb_set"], h + 1)
                V.tensor_tensor(yaT[:, 4 * h:4 * h + 4, :], ps[:, 4 * h:4 * h + 2, :].rearrange("p b (m t) -> p (b m) t", t=T), sigb,
                                ALU.mult).then_inc(S["ya_set"], 1)
            dve.wait_ge(S["sig_ga"], 1)
            dve.wait_ge(S["sig_gb"], 1)
            for h in range(2):
                m4 = slice(4 * h, 4 * h + 4)
                dve.wait_ge(S["ya_set"], h + 1)
                link(V.tensor_tensor(mergedT[:, m4, :], yaT[:, m4, :], gaT[:, m4, :], ALU.mult))
                dve.wait_ge(w_used, PIECE_AO + h + 1)
                V.tensor_tensor(ybT[:, m4, :], ps[:, 2 * h:2 * h + 2, :].rearrange("p b (m t) -> p (b m) t", t=T),
                                gbT[:, m4, :], ALU.mult).then_inc(S["yb_used"], 1)
                dve.wait_ge(S["yb_used"], h + 1)
                V.tensor_tensor(mergedT[:, m4, :], mergedT[:, m4, :], ybT[:, m4, :], ALU.add).then_inc(S["merged"], 1)
            def part_rest(i):
                dve.wait_ge(S["xh_set"], i + 1)
                V.tensor_tensor(gate_rest[:, i, :], xn_tok[:, i, :], xpart[:, 0, i], ALU.subtract).then_inc(S["xr_set"], 1)

            def part_last(i):
                dve.wait_ge(S["xm_set"], i + 1)
                V.tensor_tensor(xpart[:, 2, i], gate_rest[:, i, :], xpart[:, 1, i], ALU.subtract).then_inc(S["x_split"], 1)
                dve.wait_ge(S["x_split"], i + 1)

            dve.wait_ge(S["row_sb"], 2)
            for i in range(TT):
                if i == 0:
                    dve.wait_ge(S["out_up"], 1)
                else:
                    dve.wait_ge(w_used, PRE)
                scr = xn_tok[:, i, :]
                link(V.tensor_tensor(scr, ps[:, 4 + 2 * i:6 + 2 * i, :].rearrange("p b n -> p (b n)"), gate_mix[:, :], ALU.mult))
                V.tensor_tensor(x_tok[:, i, :], x_tok[:, i, :], scr, ALU.add).then_inc(S["x1"], 1)
                dve.wait_ge(S["x1"], i + 1)
                dve.wait_ge(S["sq2"], i + 1)
                link(V.reciprocal(stat[:, 2, i:i + 1], stat[:, 1, i:i + 1]))
                V.tensor_scalar(xn_tok[:, i, :], x_tok[:, i, :], stat[:, 2, i:i + 1], None, ALU.mult).then_inc(S["xn2"], 1)
                dve.wait_ge(S["xn2"], i + 1)
            sel, pos, wgt, ex, eq, run = (rt[:, j] for j in range(6))
            dve.wait_ge(S["ones_set"], 1)
            for i in range(TT):
                dve.wait_ge(S["logit_up"], i + 1)
                link(V.tensor_tensor(lg[:, i, :], ps[:, 4 + i, 0:EXPERTS], brt[:, :], ALU.add))
                link(V.max(top[:, i, :], lg[:, i, :]))
                V.tensor_scalar(rs[:, i, 0:1], top[:, i, 0:1], -1.0, None, ALU.mult).then_inc(S["top_set"], 1)
                t4 = top[:, i, TOPK - 1:TOPK]
                link(V.tensor_scalar(sel[:, i, :], lg[:, i, :], t4, None, ALU.is_gt))
                link(V.tensor_reduce(rs[:, i, 1:2], sel[:, i, :], AX.X, ALU.add))
                link(V.tensor_scalar(rs[:, i, 1:2], rs[:, i, 1:2], -1.0, float(TOPK), ALU.mult, ALU.add))
                link(V.tensor_scalar(eq[:, i, :], lg[:, i, :], t4, None, ALU.is_equal))
                link(V.tensor_tensor_scan(run[:, i, :], ones[:, 0:EXPERTS], eq[:, i, :], 0.0, ALU.mult, ALU.add))
                link(V.scalar_tensor_tensor(eq[:, i, :], run[:, i, :], rs[:, i, 1:2], eq[:, i, :], ALU.is_le, ALU.mult))
                V.tensor_tensor(sel[:, i, :], sel[:, i, :], eq[:, i, :], ALU.add).then_inc(S["sel_set"], 1)
                dve.wait_ge(S["sel_set"], i + 1)
                dve.wait_ge(S["ex_set"], i + 1)
                link(V.tensor_tensor(ex[:, i, :], ex[:, i, :], sel[:, i, :], ALU.mult))
                link(V.tensor_reduce(rs[:, i, 2:3], ex[:, i, :], AX.X, ALU.add))
                link(V.reciprocal(rs[:, i, 2:3], rs[:, i, 2:3]))
                link(V.tensor_scalar(wgt[:, i, :], ex[:, i, :], rs[:, i, 2:3], None, ALU.mult))
                if i == 0:
                    part_rest(0), part_last(0)
            dve.wait_ge(S["pos_up"], 1)
            V.scalar_tensor_tensor(pos, ps[:, 7, 0:TT * EXPERTS].rearrange("p (i e) -> p i e", i=TT), 1.0, sel,
                                   ALU.add, ALU.mult).then_inc(S["pos_sb"], 1)
            link(V.tensor_copy(chunk[:, 0:1], ps[0:EXPERTS, 6, 0:1]))
            link(V.tensor_scalar(chunk[:, 1:2], chunk[:, 0:1], float(CAP), None, ALU.is_gt))
            link(V.tensor_scalar(chunk[:, 2:3], chunk[:, 0:1], float(2 * CAP), chunk[:, 1:2], ALU.is_gt, ALU.add))
            V.tensor_scalar(chunk[:, 3:4], chunk[:, 0:1], float(3 * CAP), chunk[:, 2:3], ALU.is_gt, ALU.add).then_inc(S["extra_set"], 1)
            part_rest(1)
            dve.wait_ge(S["extra_set"], 1)
            dve.wait_ge(S["cum_up"], 1)
            link(V.tensor_copy(chunk[:, 4:5], ps[0:EXPERTS, 6, 1:2]))
            link(V.tensor_tensor(chunk[:, 5:6], chunk[:, 4:5], chunk[:, 3:4], ALU.subtract))
            iq = cst[0:EXPERTS, C_Q:C_Q + OVER]
            oh, base, hs = (hot[0:EXPERTS, j, EXPERTS:ITEMS] for j in range(3))
            link(V.tensor_scalar(oh, iq, chunk[:, 5:6], None, ALU.is_ge))
            link(V.tensor_scalar(hs, iq, chunk[:, 4:5], None, ALU.is_lt))
            link(V.tensor_tensor(oh, oh, hs, ALU.mult))
            link(V.tensor_scalar(base, iq, chunk[:, 5:6], 1.0, ALU.subtract, ALU.add))
            link(V.scalar_tensor_tensor(base, base, -float(CAP), oh, ALU.mult, ALU.mult))
            V.tensor_copy(hot[0:EXPERTS, 0, 0:EXPERTS], cst[0:EXPERTS, C_ID32:C_ID32 + EXPERTS]).then_inc(S["hot_set"], 1)
            part_last(1)
            dve.wait_ge(S["item_up"], 1)
            V.tensor_copy(posI[:, :, 1:1 + ITEMS], ps[:, 4, 0:TT * 48].rearrange("p (i n) -> p i n", i=TT)[:, :, 0:ITEMS]).then_inc(S["item_sb"], 1)
            dve.wait_ge(S["item_sb"], 1)
            slots = cst[:, C_SLOT:C_SLOT + CAP]

            def choose(col):
                for t in range(TT):
                    last = V.tensor_scalar(pick[:, t, :], slots, posI[:, t, bass.ds(col, 1)], None, ALU.is_equal)
                    last.then_inc(S["pick_half" if t == 0 else "pick_set"], 1)

            choose(1)
            V.tensor_copy(wI[:, :, 1:1 + ITEMS], ps[:, 5, 0:TT * 48].rearrange("p (i n) -> p i n", i=TT)[:, :, 0:ITEMS]).then_inc(S["item_sb"], 1)
            V.tensor_copy(itab[:, 0:ITEMS], ps[0:1, 6, 8:8 + ITEMS]).then_inc(S["item_sb"], 1)
            V.tensor_scalar(icnt[:, 0:1], ps[0:1, 6, 2:3], float(EXPERTS), None, ALU.add).then_inc(S["item_sb"], 1)
            dve.wait_ge(S["item_sb"], 4)
            def expert_of(i):
                V.tensor_copy(hotb, hot[:, 0, bass.ds(i, 1)].to_broadcast([P, CAP])).then_inc(S["hotb_set"], 1)

            def modulated(done):
                dve.wait_ge(S["hg_up"], done)
                V.tensor_tensor(hg, ps[:, 2, :].rearrange("p (f s) -> p f s", f=KD),
                                scale2[:, :].unsqueeze(2).to_broadcast([P, KD, CAP]), ALU.mult).then_inc(S["hg_half"], 1)
                dve.wait_ge(S["hg_half"], done)
                V.tensor_tensor(hg, hg, mod[:, SH2:SH2 + KD].unsqueeze(2).to_broadcast([P, KD, CAP]), ALU.add).then_inc(S["hg_sb"], 1)

            expert_of(0)
            modulated(1)
            dve.wait_ge(S["acc_set"], TT)
            dve.wait_ge(S["ysb_zero"], 1)
            count = dve.value_load(icnt[0:1, 0:1], min_val=EXPERTS, max_val=ITEMS)

            def weights_of(col, i):
                dve.wait_ge(S["pwT_up"], i)
                for t in range(TT):
                    for h in range(2):
                        last = V.tensor_scalar(pickw[:, t, h, CAP * h:CAP * h + CAP], slots, posI[:, t, bass.ds(col, 1)],
                                               wI[:, t, bass.ds(col, 1)], ALU.is_equal, ALU.mult)
                        last.then_inc(S["pickw_set" if t + h == 2 else "pickw_half"], 1)

            def add_item(i):
                for t in range(TT):
                    for h in range(2):
                        dve.wait_ge(S["comb_up"], i * 4 + (2 * t + h + 1))
                        V.tensor_tensor(acc[:, t, 512 * h:512 * h + 512], acc[:, t, 512 * h:512 * h + 512], ps[:, 6 + h, :],
                                        ALU.add).then_inc(S["comb_add"], 1)

            def item(i):
                dve.wait_ge(S["hg_up"], i + 1)
                choose(i + 2)
                weights_of(i, i)
                dve.wait_ge(w_used, i * SLOTS + (PRE + GU_PIECES))
                V.tensor_scalar(gate, ps[:, 0, :], LIMIT, None, ALU.min).then_inc(S["gated"], 1)
                V.tensor_scalar(up, ps[:, 1, :], LIMIT, -LIMIT, ALU.min, ALU.max).then_inc(S["up_c"], 1)
                dve.wait_ge(S["sig_set"], i + 1)
                V.tensor_tensor(gate, gate, sig, ALU.mult).then_inc(S["gate_s"], 1)
                dve.wait_ge(S["gate_s"], i + 1)
                dve.wait_ge(S["up_c"], i + 1)
                V.scalar_tensor_tensor(act_, up, 1.0, gate, ALU.add, ALU.mult).then_inc(S["act_set"], 1)
                expert_of(i + 1)
                modulated(i + 2)
                add_item(i)

            with dve.Fori(0, EXPERTS) as i:
                item(i)
            with dve.If(count > EXPERTS):
                with dve.Fori(EXPERTS, ITEMS) as i:
                    with dve.If(i < count):
                        item(i)
            weights_of(count, count)
            add_item(count)
            for i in range(TT):
                dve.wait_ge(S["comb_add"], count * 4 + 4)
                link(V.tensor_tensor(acc[:, i, :], acc[:, i, :], gate_ffn[:, :], ALU.mult))
                V.tensor_tensor(x_tok[:, i, :], x_tok[:, i, :], acc[:, i, :], ALU.add).then_inc(S["fin"], 1)
            for i in range(TT):
                dve.wait_ge(S["sq3"], i + 1)
                link(V.reciprocal(stat[:, 2, i:i + 1], stat[:, 1, i:i + 1]))
                V.scalar_tensor_tensor(x_tok[:, i, :], x_tok[:, i, :], stat[:, 2, i:i + 1], gfin, ALU.mult, ALU.mult).then_inc(S["fin_out"], 1)

    ctx.close()


_INS = ["x", "c", "w_ada", "b_ada", "g_mix", "w_in", "ssm_a_re", "ssm_a_im", "ssm_log_dt", "ssm_b_re", "ssm_b_im",
        "ssm_c_re", "ssm_c_im", "ssm_d", "w_glu", "w_attn_o", "w_out", "g_ffn", "w_router", "b_router", "w_gu", "b_gu",
        "w_down", "b_down", "g_final"]


def kernel(**inputs):
    from concourse import bacc
    from concourse.bass_utils import run_bass_kernel_spmd

    nc = bacc.Bacc("TRN2", target_bir_lowering=False, num_devices=1, dynamic_dma_scratch_size=1024)
    arrays = {f"in_{n}": np.ascontiguousarray(inputs[n]) for n in _INS}
    arrays["in_const"] = constants()
    args = [nc.dram_tensor(n, a.shape, F32, kind="ExternalInput").ap() for n, a in arrays.items()]
    out = nc.dram_tensor("out_0", (1, T, D), F32, kind="ExternalOutput").ap()
    build(nc, *args, out)
    r = run_bass_kernel_spmd(nc, [arrays], core_ids=[0])
    return r.results[0]["out_0"]
```

```python
from contextlib import ExitStack

import numpy as np

import concourse.bass as bass
from concourse import mybir

F32 = mybir.dt.float32
I32 = mybir.dt.int32
ALU = mybir.AluOpType
ACT = mybir.ActivationFunctionType
AX = mybir.AxisListType

P = 128
D = 1024
T = 256
TT = T // P
KD = D // P
W = D // 2
KW = W // P
HEADS, HD = 8, 64
G, N, C = 32, 64, 16
ST = G * N // P
EXPERTS, TOPK = 32, 4
CAP = 64
OVER = 15
ITEMS = EXPERTS + OVER
COLS = ITEMS + 1
SLOTS = 12
SLOT = 2048
EPS = 1e-5
LIMIT, ALPHA = 7.0, 1.702
THETA = 500000.0
HALF = HD // 8
TWO_PI = 2.0 * np.pi
ROUND = 1.5 * 2.0 ** 23

C_ID, C_COS, C_SIN, C_ROT, C_TRI, C_CAUSAL = 0, 128, 384, 640, 768, 896
C_SLOT, C_TRI32, C_ID32, C_Q, C_E, C_MB, C_MC = 1280, 1344, 1376, 1408, 1424, 1425, 1427
C_ALL = 1429
BF16 = mybir.dt.bfloat16
R_C, R_GMIX, R_GFFN, R_ADA, R_D, R_ALL = 0, 8, 16, 24, 72, 76
SH1, SC1, GT1, SH2, SC2, GT2 = (8 * j for j in range(6))


def constants():
    c = np.zeros((P, C_ALL), np.float32)
    p = np.arange(P)
    c[:, C_ID:C_ID + P] = np.eye(P)
    inv = (1.0 / THETA ** (np.arange(0, 2 * HALF, 2, dtype=np.float32) / (2 * HALF))).astype(np.float32)
    ang = np.arange(T, dtype=np.float32)[None, :] * inv[p % HALF][:, None]
    turned = (p % HD < 2 * HALF)[:, None]
    c[:, C_COS:C_COS + T] = np.where(turned, np.cos(ang), 1.0)
    c[:, C_SIN:C_SIN + T] = np.where(turned, np.sin(ang), 0.0)
    for j in range(P):
        if j % HD < HALF:
            c[j + HALF, C_ROT + j] = -1.0
        elif j % HD < 2 * HALF:
            c[j - HALF, C_ROT + j] = 1.0
    c[:, C_TRI:C_TRI + P] = p[:, None] < p[None, :]
    past = np.where(p[None, :] <= p[:, None], 0.0, -1e30)
    c[:, C_CAUSAL:C_CAUSAL + P] = past
    c[:, C_CAUSAL + 2 * P:C_CAUSAL + 3 * P] = past
    c[:, C_SLOT:C_SLOT + CAP] = np.arange(1, CAP + 1)
    e = np.arange(EXPERTS)
    c[:EXPERTS, C_TRI32:C_TRI32 + EXPERTS] = e[:, None] <= e[None, :]
    c[:EXPERTS, C_ID32:C_ID32 + EXPERTS] = np.eye(EXPERTS)
    c[:, C_Q:C_Q + OVER + 1] = np.arange(OVER + 1)
    c[:EXPERTS, C_E] = e
    c[:, C_MB:C_MB + 2] = (p // N)[:, None] == np.arange(2)
    c[:, C_MC:C_MC + 2] = (p % (2 * C) // C)[:, None] == np.arange(2)
    return c


def build(nc, x, c, w_ada, b_ada, g_mix, w_in, a_re, a_im, log_dt, b_re, b_im, c_re, c_im, ssm_d,
          w_glu, w_attn_o, w_out, g_ffn, w_router, b_router, w_gu, b_gu, w_down, b_down, g_final,
          const, out):
    ctx = ExitStack()

    def sb(name, shape, dt=F32):
        return ctx.enter_context(nc.sbuf_tensor(name, shape, dt))

    def sem(name):
        return ctx.enter_context(nc.semaphore(name))

    ring = sb("ring", [P, SLOTS, SLOT])
    x_tok = sb("x_tok", [P, TT, D])
    xn_tok = sb("xn_tok", [P, TT, D])
    hT = sb("hT", [P, KD, T])
    cst = sb("cst", [P, C_ALL])
    ones = sb("ones", [P, P])
    cols = sb("cols", [P, R_ALL])
    mod = sb("mod", [P, 6 * KD])
    scale1 = sb("scale1", [P, KD])
    scale2 = sb("scale2", [P, KD])
    cond = sb("cond", [P, KD])
    condb = sb("condb", [P, KD, 32])
    stat = sb("stat", [P, 4, TT])
    ident = cst[:, C_ID:C_ID + P]

    zone = sb("zone", [P, 19456])
    at = [0]

    def cut(n):
        at[0] += n
        assert at[0] <= zone.shape[1]
        return zone[:, at[0] - n:at[0]]

    ecos = cut(ST * T).rearrange("p (s t) -> p s t", s=ST)
    esin = cut(ST * T).rearrange("p (s t) -> p s t", s=ST)
    uT = cut(KW * T).rearrange("p (m t) -> p m t", m=KW)
    qT = cut(KW * T).rearrange("p (m t) -> p m t", m=KW)
    kT = cut(KW * T).rearrange("p (m t) -> p m t", m=KW)
    oT = cut(KW * T).rearrange("p (m t) -> p m t", m=KW)
    v_tok = cut(TT * W).rearrange("p (i n) -> p i n", i=TT)
    gaT = xn_tok[:, :, :].rearrange("p i d -> p (i d)").rearrange("p (m t) -> p m t", m=KD)
    gbT = cut(KD * T).rearrange("p (m t) -> p m t", m=KD)
    z = cut(4 * 512).rearrange("p (b r n) -> p b r n", b=2, r=2)
    BT = cut(2 * KW * P).rearrange("p (r m n) -> p r m n", r=2, m=KW)
    CT = cut(2 * KW * P).rearrange("p (r m n) -> p r m n", r=2, m=KW)
    gates = z.rearrange("p b r n -> p (b r n)")
    gate_mix, gate_ffn = gates[:, 0:D], gates[:, D:2 * D]
    xs = sb("xs", [P, 2, 2, 512])
    tmp = sb("tmp", [P, 2, 512])
    ptmp = sb("ptmp", [P, 512])
    modrow = [gbT.rearrange("p m t -> p (m t)")[:, 512 * j:512 * j + 512] for j in (1, 2, 3)]
    gluT = ecos.rearrange("p s t -> p (s t)")[:, 0:KW * T].rearrange("p (m t) -> p m t", m=KW)
    yaT = ecos.rearrange("p s t -> p (s t)")[:, 1024:3072].rearrange("p (m t) -> p m t", m=KD)
    sigb = ecos.rearrange("p s t -> p (s t)")[:, 3072:4096].rearrange("p (m t) -> p m t", m=KW)
    mergedT = esin.rearrange("p s t -> p (s t)")[:, 0:2048].rearrange("p (m t) -> p m t", m=KD)
    ybT = esin.rearrange("p s t -> p (s t)")[:, 2048:4096].rearrange("p (m t) -> p m t", m=KD)
    prob = sb("prob", [P, 3 * P])
    probT = sb("probT", [P, 3 * P])
    mx = sb("mx", [P, 2, 4])
    raw = v_tok.rearrange("p i n -> p (i n)")
    are, aim, ldt = raw[0:ST, 0:P], raw[0:ST, P:2 * P], raw[0:ST, 2 * P:2 * P + 2]
    rows = raw[0:R_ALL, 3 * P:4 * P]
    b_in = kT.rearrange("p m t -> p (m t)")[:, 0:512].rearrange("p (r s c) -> p r s c", r=2, s=ST)
    c_in = oT.rearrange("p m t -> p (m t)")[:, 0:512].rearrange("p (r m n) -> p r m n", r=2, m=KW)
    sprow = gbT.rearrange("p m t -> p (m t)")[0:ST, :].rearrange("p (j n) -> p j n", n=P)
    sprm = sb("sprm", [P, 5, ST])
    blk = z.rearrange("p b r n -> p (b r n)")
    Bblk = blk[:, 0:1024].rearrange("p (r s q c) -> p r s q c", r=2, s=ST, q=2)
    Cblk = blk[:, 1024:2048].rearrange("p (r m q n) -> p r m q n", r=2, m=KW, q=2)
    at[0] = 0
    acc = cut(TT * D).rearrange("p (i n) -> p i n", i=TT)
    hg = cut(KD * CAP).rearrange("p (f s) -> p f s", f=KD)
    gate, up, sig = cut(D // 2), cut(D // 2), cut(D // 2)
    act_ = cut(D // 2)
    actT = cut(D // 2).rearrange("p (j h s) -> p j h s", j=4, h=2)
    ysb = cut(D // 2)
    pickw = cut(2 * TT * P).rearrange("p (i h n) -> p i h n", i=TT, h=2)
    pickwT = cut(2 * T).rearrange("p (h t) -> p h t", h=2)
    pick = cut(TT * CAP // 2).bitcast(BF16).rearrange("p (i s) -> p i s", i=TT)
    hotb = cut(CAP)
    bgu_rows = cut(2 * D)
    bdn_rows = cut(D)
    gfin = cut(D)
    xpart = cut(3 * TT * D // 2).bitcast(BF16).rearrange("p (c i d) -> p c i d", c=3, i=TT)
    wr = cut(KD * EXPERTS).rearrange("p (k e) -> p k e", k=KD)
    rowT = cut(2 * T).rearrange("p (j t) -> p j t", j=2)
    rt = cut(6 * TT * EXPERTS).rearrange("p (j i e) -> p j i e", j=6, i=TT)
    lg = cut(TT * EXPERTS).rearrange("p (i e) -> p i e", i=TT)
    brt = cut(EXPERTS)
    top = cut(TT * 8).rearrange("p (i n) -> p i n", i=TT)
    rs = cut(TT * 4).rearrange("p (i n) -> p i n", i=TT)
    chunk = cut(8)[0:EXPERTS, :]
    assert at[0] <= 4096 * 2 + 1024 * 5 + 2048
    squares = tmp.rearrange("p r n -> p (r n)")
    gate_rest = zone[:, 0:TT * D].rearrange("p (i d) -> p i d", i=TT)
    hot = sb("hot", [P, 3, 48])
    posI = sb("posI", [P, TT, COLS])
    wI = sb("wI", [P, TT, COLS])
    itab = sb("itab", [1, 48], I32)
    icnt = sb("icnt", [1, 2], I32)
    ps = ctx.enter_context(nc.psum_tensor("ps", [P, 8, 512], F32))

    arrived = [sem(f"arrived{s}") for s in range(SLOTS)]
    w_used = sem("w_used")
    names = """x_in ident_in const_in rows_in ssm_in bc_in late_in out_stored aside2 aside3 aside6 aside7 aside9
        aside10 aside11 ones_set cols_up cols_sb cond_set ssm_rows sprm_up sprm_sb Bblk_set Cblk0_set
        Cblk1_set BT_up CT0_up CT1_up BT_sb CT0_sb CT1_sb phases modrow_sb modT_up mod1_sb sq1 xn1 xT_up
        h_sb proj_sb bu_up bu_read scanned xs_set xs_read rot_up rot_read rope_set sc_up negmax expd probs
        probsT_up probsT_sb o_up o_sb mod2_sb row_up row_sb y_skip gelu sig_ga sig_gb sigb_set ya_set
        yb_used merged out_up x1 sq2 xn2 x2T_up h2_sb logit_up top_set ex_set sel_set pos_up pos_sb pos_half rT_up
        rT_sb extra_set cum_up hot_set item_up item_sb zeroed hotb_set pick_set hg_up hg_sb gated sig_set
        act_set y_sb pickw_set pwT_up pwT_sb actT_up actT_sb comb_up comb_add fin sq3 fin_out dt_set mag_set
        trig_set lrdt_set angle_set phase_lo pick_half pickw_half hg_half up_c gate_s xh_set xr_set xm_set
        x_split ffn_gated x_but_last scale1_set turn turned row_max probs_half sqsum2 sqsum3 lnD lnA lnP
        cond_half""".split()
    S = {n: sem(n) for n in names}

    def linker(eng, s):
        count = [0]

        def link(ins):
            count[0] += 1
            ins.then_inc(s, 1)
            eng.wait_ge(s, count[0])
        return link

    def square(eng, link, n):
        a, b = ecos[:, :, n // 2:n // 2 + 1], esin[:, :, n // 2:n // 2 + 1]
        c1, s1 = ecos[:, :, n + 1:n + 2], esin[:, :, n + 1:n + 2]
        link(eng.tensor_tensor(c1, a, a, ALU.mult))
        link(eng.tensor_tensor(s1, b, b, ALU.mult))
        link(eng.tensor_tensor(ecos[:, :, n:n + 1], c1, s1, ALU.subtract))
        link(eng.tensor_tensor(c1, a, b, ALU.mult))
        link(eng.tensor_tensor(esin[:, :, n:n + 1], c1, c1, ALU.add))

    def double(eng, link, n, scratch):
        w = min(ST, 512 // n)
        for s in range(0, ST, w):
            shape = [P, w, n - 1]
            cn, sn = (e[:, s:s + w, n:n + 1].to_broadcast(shape) for e in (ecos, esin))
            ct, st = ecos[:, s:s + w, 1:n], esin[:, s:s + w, 1:n]
            t0, t1 = (scratch[:, r, 0:w * (n - 1)].rearrange("p (s t) -> p s t", s=w) for r in range(2))
            link(eng.tensor_tensor(t0, ct, cn, ALU.mult))
            link(eng.tensor_tensor(t1, st, sn, ALU.mult))
            link(eng.tensor_tensor(ecos[:, s:s + w, n + 1:2 * n], t0, t1, ALU.subtract))
            link(eng.tensor_tensor(t0, ct, sn, ALU.mult))
            link(eng.tensor_tensor(t1, st, cn, ALU.mult))
            link(eng.tensor_tensor(esin[:, s:s + w, n + 1:2 * n], t0, t1, ALU.add))

    def kp(w):
        return w.rearrange("(k p) n -> p k n", p=P)

    GROUPS = (1, 2, 0, 3, 4, 5, 6, 7)
    ada, win, glu, wao, wo = kp(w_ada[0]), kp(w_in[0]), kp(w_glu[0]), kp(w_attn_o[0]), kp(w_out[0])
    BEHIND = {2: 3, 3: 3, 4: 3, 5: 4, 6: 3}
    order = [("ada", k) for k in range(KD)]
    for n in range(16):
        order.append(("in", n))
        order += [("ada", len([o for o in order if o[0] == "ada"]) + a) for a in range(BEHIND.get(n, 0))]
    order += [("ao", j) for j in range(2)] + [("glu", j) for j in range(4)] + [("out", j) for j in range(4)]
    place = {o: n for n, o in enumerate(order)}
    PRE = len(order)

    def source(kind, n):
        if kind == "ada":
            return ada[:, n % KD:n % KD + 1, 2 * D * (n // KD):2 * D * (n // KD + 1)]
        if kind == "in":
            return win[:, 4 * (n % 2):4 * (n % 2) + 4, W * GROUPS[n // 2]:W * GROUPS[n // 2] + W]
        if kind == "ao":
            return wao[:, :, W * n:W * n + W]
        if kind == "glu":
            j = (0, 2, 1, 3)[n]
            return glu[:, :, W * j:W * j + W]
        return wo[:, 2 * n:2 * n + 2, :]

    pieces = [source(*o) for o in order]
    first_behind = [KD + sum(BEHIND.get(m, 0) for m in range(n)) for n in range(16)]
    ada_behind = [range(first_behind[n], first_behind[n] + BEHIND.get(n, 0)) for n in range(16)]
    MOD_BANK = (5, 6, 7)
    GU_PIECES, DN_PIECES = 8, 4
    halves = (gate_mix, tmp.rearrange("p r n -> p (r n)"))
    aside = {2: zone[:, 17408:19456], 3: xs.rearrange("p b r n -> p (b r n)"),
             6: zone[:, 2560:4608], 7: zone[:, 4608:6656],
             9: None,
             10: hT.rearrange("p k t -> p (k t)"), 11: xn_tok.rearrange("p i d -> p (i d)")}
    ring0 = [j for j in range(SLOTS) if j not in aside]
    RING0 = len(ring0)
    slot_of = [(PRE + RING0 + j) % SLOTS for j in range(SLOTS)]
    round_of = [(PRE + RING0 + j) // SLOTS for j in range(SLOTS)]

    def slot(n, k):
        return ring[:, n % SLOTS, :].rearrange("p (k n) -> p k n", k=k)

    with nc.Block() as block:

        @block.sync
        def _(sp):
            sp.dma_start(rows[R_C:R_C + KD, :], c.rearrange("a (k p) -> (a k) p", p=P)).then_inc(S["rows_in"], 16)
            sp.dma_start(rows[R_GMIX:R_GMIX + KD, :], g_mix.rearrange("a (k p) -> (a k) p", p=P)).then_inc(S["rows_in"], 16)
            sp.dma_start(rows[R_GFFN:R_GFFN + KD, :], g_ffn.rearrange("a (k p) -> (a k) p", p=P)).then_inc(S["rows_in"], 16)
            sp.dma_start(rows[R_ADA:R_ADA + 6 * KD, :], b_ada.rearrange("a (k p) -> (a k) p", p=P)).then_inc(S["rows_in"], 16)
            sp.dma_start(rows[R_D:R_D + KW, :], ssm_d.rearrange("a (k p) -> (a k) p", p=P)).then_inc(S["rows_in"], 16)
            sp.dma_start(ident, const[:, C_ID:C_ID + P]).then_inc(S["ident_in"], 16)
            for n, src in enumerate(pieces):
                if n >= SLOTS:
                    sp.wait_ge(w_used, n - SLOTS + 1)
                sp.dma_start(slot(n, src.shape[1]), src).then_inc(arrived[n % SLOTS], 16)
                if n == KD:
                    sp.dma_start(cst[:, P:], const[:, P:]).then_inc(S["const_in"], 16)
                    for r, (b, cc) in enumerate(((b_re, c_re), (b_im, c_im))):
                        sp.dma_start(b_in[:, r], b[0].rearrange("(s q) p c -> (q p) s c", q=2)).then_inc(S["bc_in"], 16)
                        sp.dma_start(c_in[:, r], cc[0].rearrange("(m g) c p -> (g c) m p", m=KW)).then_inc(S["bc_in"], 16)
                if n == 3:
                    sp.dma_start(x_tok[:, :, :], x[0].rearrange("(i p) d -> p i d", p=P)).then_inc(S["x_in"], 16)

            def expert_piece(e, j):
                if j < GU_PIECES:
                    return w_gu[0, bass.ds(e, 1)].rearrange("e (k p) n -> p (e k) n", p=P)[:, j:j + 1, :]
                k = 2 * (j - GU_PIECES)
                return w_down[0, bass.ds(e, 1)].rearrange("e (k p) n -> p (e k) n", p=P)[:, k:k + 2, :]

            def beside(j):
                src = expert_piece(0, j)
                if j == 9:
                    for k, dst in enumerate(halves):
                        sp.dma_start(dst, src[:, k, :]).then_inc(S["aside9"], 16)
                else:
                    sp.dma_start(aside[j].rearrange("p (k n) -> p k n", k=src.shape[1]), src).then_inc(S[f"aside{j}"], 16)

            def ringed(n, e, j):
                src = expert_piece(e, j)
                sp.dma_start(slot(n, src.shape[1]), src).then_inc(arrived[n % SLOTS], 16)

            for n, j in enumerate(ring0):
                sp.wait_ge(w_used, PRE + n - SLOTS + 1)
                ringed(PRE + n, 0, j)
                if n == 1:
                    sp.wait_ge(S["xs_read"], KW * 2)
                    beside(2), beside(3)
            for j in range(SLOTS - RING0):
                n = PRE + RING0 + j
                sp.wait_ge(w_used, n - SLOTS + 1)
                ringed(n, 1, j)
            sp.wait_ge(w_used, PRE)
            beside(6), beside(7)
            sp.wait_ge(S["x1"], TT)
            sp.wait_ge(S["sqsum2"], TT)
            beside(9)
            sp.wait_ge(S["logit_up"], TT)
            beside(10)
            sp.wait_ge(S["xr_set"], TT)
            beside(11)
            for j in range(SLOTS - RING0, SLOTS):
                sp.wait_ge(w_used, PRE + ring0[j - (SLOTS - RING0)] + 1)
                ringed(PRE + RING0 + j, 1, j)

            def expert_load(item, e):
                for j in range(SLOTS):
                    sp.wait_ge(w_used, item * SLOTS + (PRE + j - SLOTS + 1))
                    ringed(PRE + RING0 + j, e, j)

            with sp.Fori(2, EXPERTS) as i:
                expert_load(i, i)
            sp.wait_ge(S["item_sb"], 4)
            count = sp.value_load(icnt[0:1, 0:1], min_val=EXPERTS, max_val=ITEMS)
            with sp.If(count > EXPERTS):
                with sp.Fori(EXPERTS, ITEMS) as i:
                    with sp.If(i < count):
                        expert_load(i, sp.value_load(itab[0:1, bass.ds(i, 1)], min_val=0, max_val=EXPERTS - 1))
            for i in range(TT):
                sp.wait_ge(S["fin_out"], i + 1)
                sp.dma_start(out[0, P * i:P * i + P, :], x_tok[:, i, :]).then_inc(S["out_stored"], 16)
            sp.wait_ge(S["out_stored"], 16 * TT)

        @block.tensor
        def _(pe):
            mm = nc.tensor.matmul

            def take(n):
                pe.wait_ge(arrived[n % SLOTS], 16 * (n // SLOTS + 1))

            pe.wait_ge(S["rows_in"], 80)
            pe.wait_ge(S["ident_in"], 16)
            nc.tensor.transpose(ps[:, 7, 0:R_ALL], rows[:, :], cst[0:R_ALL, C_ID:C_ID + R_ALL]).then_inc(S["cols_up"], 1)
            pe.wait_ge(S["cond_set"], 1)

            def modulation_products(pieces):
                for a in pieces:
                    k, bank = a % KD, MOD_BANK[a // KD]
                    if a == KD:
                        pe.wait_ge(S["CT1_sb"], 1)
                    if a == 2 * KD:
                        pe.wait_ge(S["BT_sb"], 1)
                    take(place["ada", a])
                    w = slot(place["ada", a], 1)
                    for j in range(4):
                        last = mm(ps[32 * j:32 * j + 32, bank, :], condb[:, k, :], w[:, 0, 512 * j:512 * j + 512],
                                  start=(k == 0), stop=(k == KD - 1), skip_group_check=True)
                    last.then_inc(w_used, 1)

            def modulation_columns(n):
                bank = MOD_BANK[n]
                pe.wait_ge(S["modrow_sb"], n + 1)
                for cb in range(4):
                    last = nc.tensor.transpose(ps[:, bank, P * cb:P * cb + P], modrow[n][:, P * cb:P * cb + P], ident)
                last.then_inc(S["modT_up"], 1)

            modulation_products(range(4))
            pe.wait_ge(S["ssm_rows"], 1)
            for j in range(5):
                last = nc.tensor.transpose(ps[:, 6, ST * j:ST * j + ST], sprow[:, j, :], cst[0:ST, C_ID:C_ID + ST])
            last.then_inc(S["sprm_up"], 1)
            modulation_products(range(4, 6))
            pe.wait_ge(S["xn1"], TT)
            for k in range(KD):
                for i in range(TT):
                    last = nc.tensor.transpose(ps[:, k // 2, (k % 2) * T + P * i:(k % 2) * T + P * i + P],
                                               xn_tok[:, i, P * k:P * k + P], ident)
            last.then_inc(S["xT_up"], 1)
            modulation_products(range(6, 8))
            modulation_columns(0)

            def proj(g, h):
                n = place["in", 2 * g + h]
                take(n)
                w = slot(n, 4)
                b = 2 * (g % 2)
                if h == 0:
                    if g < 2:
                        pe.wait_ge(S["h_sb"], KD)
                    else:
                        pe.wait_ge(S["proj_sb"], g - 1)
                for kk in range(4):
                    k = 4 * h + kk
                    if g == 3:
                        for i in range(TT):
                            last = mm(ps[:, b + i, :], hT[:, k, P * i:P * i + P], w[:, kk, :], start=(k == 0), stop=(k == KD - 1))
                    else:
                        for m in range(4):
                            last = mm(ps[:, b + m // 2, (m % 2) * T:(m % 2) * T + T], w[:, kk, P * m:P * m + P], hT[:, k, :],
                                      start=(k == 0 and m % 2 == 0), stop=(k == KD - 1), skip_group_check=True)
                last.then_inc(w_used, 1)

            def b_u(j):
                if j == 0:
                    pe.wait_ge(S["proj_sb"], 3)
                    pe.wait_ge(S["rot_read"], 2)
                else:
                    pe.wait_ge(S["bu_read"], j)
                for q in range(2):
                    s = 2 * j + q
                    a = 32 * (s % 4)
                    for r in range(2):
                        last = mm(ps[:, 4 + q, T * r:T * r + T], BT[a:a + 32, r, s // 4, :], uT[a:a + 32, s // 4, :],
                                  start=True, stop=True, skip_group_check=True)
                last.then_inc(S["bu_up"], 1)

            def c_x(j):
                pe.wait_ge(S["xs_set"], j + 1)
                if j == 0:
                    pe.wait_ge(S["mod2_sb"], 1)
                if j % 2 == 0 and j >= 2:
                    pe.wait_ge(S["y_skip"], j // 2)
                for q in range(2):
                    s = 2 * j + q
                    m, a = s // 4, 32 * (s % 4)
                    for r in range(2):
                        last = mm(ps[a:a + 32, 6, (m % 2) * T:(m % 2) * T + T], CT[:, r, m, a:a + 32],
                                  xs[:, j % 2, r, T * q:T * q + T], start=(r == 0), stop=(r == 1), skip_group_check=True)
                last.then_inc(S["xs_read"], 1)

            def b_and_c():
                pe.wait_ge(S["Bblk_set"], 1)
                pe.wait_ge(S["sprm_sb"], 1)
                for r in range(2):
                    for m in range(KW):
                        last = nc.tensor.transpose(ps[:, 6 + r, P * m:P * m + P],
                                                   Bblk[:, r, 4 * m:4 * m + 4].rearrange("p s q c -> p (s q c)"), ident)
                last.then_inc(S["BT_up"], 1)
                for r in range(2):
                    pe.wait_ge(S[f"Cblk{r}_set"], 1)
                    if r == 1:
                        pe.wait_ge(S["BT_sb"], 1)
                    for m in range(KW):
                        last = nc.tensor.transpose(ps[:, 4 + 2 * r, P * m:P * m + P],
                                                   Cblk[:, r, m].rearrange("p q n -> p (q n)"), ident)
                    last.then_inc(S[f"CT{r}_up"], 1)

            def rotate(src, n):
                pe.wait_ge(S["proj_sb"], 1 + n)
                pe.wait_ge(S["const_in"], 16)
                if n == 0:
                    pe.wait_ge(S["CT0_sb"], 1)
                    pe.wait_ge(S["mod1_sb"], 1)
                else:
                    pe.wait_ge(S["rot_read"], 1)
                for m in range(KW):
                    last = mm(ps[:, 4 + m // 2, (m % 2) * T:(m % 2) * T + T], cst[:, C_ROT:C_ROT + P], src[:, m, :],
                              start=True, stop=True, skip_group_check=True)
                last.then_inc(S["rot_up"], 1)

            def scores(h):
                if h == 0:
                    pe.wait_ge(S["rope_set"], 2)
                    pe.wait_ge(S["mod2_sb"], 2)
                else:
                    pe.wait_ge(S["o_sb"], h)
                a, m = HD * (h % 2), h // 2
                mm(ps[:, 7, 0:P], qT[a:a + HD, m, 0:P], kT[a:a + HD, m, 0:P], start=True, stop=True, skip_group_check=True)
                mm(ps[:, 7, P:3 * P], qT[a:a + HD, m, P:T], kT[a:a + HD, m, :], start=True, stop=True,
                   skip_group_check=True).then_inc(S["sc_up"], 1)

            def weigh(h):
                a = HD * (h % 2)
                pe.wait_ge(S["probs"], h + 1)
                for j in range(3):
                    last = nc.tensor.transpose(ps[:, 7, P * j:P * j + P], prob[:, P * j:P * j + P], ident)
                last.then_inc(S["probsT_up"], 1)
                pe.wait_ge(S["probsT_sb"], h + 1)
                mm(ps[a:a + HD, 7, 0:T], v_tok[:, 0, HD * h:HD * h + HD], probT[:, 0:T], start=True, stop=False,
                   skip_group_check=True)
                mm(ps[a:a + HD, 7, P:T], v_tok[:, 1, HD * h:HD * h + HD], probT[:, T:3 * P], start=False, stop=True,
                   skip_group_check=True).then_inc(S["o_up"], 1)

            for n in range(16):
                if n >= 8:
                    scores(n - 8)
                proj(n // 2, n % 2)
                if n == 1:
                    b_and_c()
                if n == 2:
                    rotate(qT, 0)
                if n == 4:
                    rotate(kT, 1)
                modulation_products(ada_behind[n])
                if n == 6:
                    modulation_columns(1)
                if n == 7:
                    modulation_columns(2)
                if 6 <= n < 14:
                    b_u(n - 6)
                if n >= 8:
                    c_x(n - 8)
                if n >= 8:
                    weigh(n - 8)
            pe.wait_ge(S["o_sb"], HEADS)
            pe.wait_ge(S["proj_sb"], 8)
            for n in range(2):
                take(place["ao", n])
                w = slot(place["ao", n], 4)
                for kk in range(KW):
                    for m in range(4):
                        last = mm(ps[:, 2 * n + m // 2, (m % 2) * T:(m % 2) * T + T], w[:, kk, P * m:P * m + P], oT[:, kk, :],
                                  start=(kk == 0 and m % 2 == 0), stop=(kk == KW - 1), skip_group_check=True)
                last.then_inc(w_used, 1)
                if n == 0:
                    pe.wait_ge(S["bu_read"], KW * 2)
                else:
                    pe.wait_ge(S["y_skip"], KW)
                for k in range(KD):
                    t = (GT1, GT2)[n] + k
                    last = mm(ps[:, 4 + 2 * n + k // 4, P * (k % 4):P * (k % 4) + P], mod[:, t:t + 1].to_broadcast([P, P]), ident,
                              start=True, stop=True, skip_group_check=True)
                last.then_inc(S["row_up"], 1)
            pe.wait_ge(S["gelu"], 1)
            for n, b in enumerate((4, 6, 0, 2)):
                take(place["glu", n])
                w = slot(place["glu", n], 4)
                if n < 2:
                    pe.wait_ge(S["row_sb"], n + 1)
                else:
                    pe.wait_ge(S["yb_used"], n - 1)
                for kk in range(KW):
                    for m in range(4):
                        last = mm(ps[:, b + m // 2, (m % 2) * T:(m % 2) * T + T], w[:, kk, P * m:P * m + P], gluT[:, kk, :],
                                  start=(kk == 0 and m % 2 == 0), stop=(kk == KW - 1), skip_group_check=True)
                last.then_inc(w_used, 1)

            def router_columns(i):
                pe.wait_ge(S["xn2"], i + 1)
                pe.wait_ge(S["ya_set"], 2)
                for k in range(KD):
                    last = nc.tensor.transpose(ps[:, 2 * i + k // 4, P * (k % 4):P * (k % 4) + P], xn_tok[:, i, P * k:P * k + P], ident)
                last.then_inc(S["x2T_up"], 1)

            def router(i):
                pe.wait_ge(S["x1"], 1)
                pe.wait_ge(S["late_in"], 80)
                pe.wait_ge(S["h2_sb"], KD * (i + 1))
                for k in range(KD):
                    for h in range(2):
                        a = P * i + CAP * h
                        last = mm(ps[CAP * h:CAP * h + CAP, 4 + i, 0:EXPERTS], hT[:, k, a:a + CAP], wr[:, k, :],
                                  start=(k == 0), stop=(k == KD - 1), skip_group_check=True)
                last.then_inc(S["logit_up"], 1)

            for i in range(TT):
                for n in range(4):
                    w = slot(place["out", n], 2)
                    if i == 0:
                        take(place["out", n])
                        if n == 0:
                            pe.wait_ge(S["ya_set"], 1)
                        pe.wait_ge(S["merged"], 1 if n < 2 else 2)
                    if i == 1 and n == 2:
                        router_columns(0)
                    for kk in range(2):
                        k = 2 * n + kk
                        for h in range(2):
                            last = mm(ps[:, 4 + 2 * i + h, :], mergedT[:, k, P * i:P * i + P], w[:, kk, 512 * h:512 * h + 512],
                                      start=(k == 0), stop=(k == KD - 1))
                    if i == TT - 1:
                        last.then_inc(w_used, 1)
                if i == 0:
                    last.then_inc(S["out_up"], 1)
            router(0)
            router_columns(1)
            router(1)
            sel = rt[:, 0]
            tri = cst[:, C_TRI:C_TRI + P]
            pe.wait_ge(S["sel_set"], TT)
            pe.wait_ge(S["ones_set"], 1)
            pe.wait_ge(S["x1"], TT)
            for a in (0, CAP):
                for n, (lhs, src, dst) in enumerate(((tri, 0, 0), (ones, 0, 1), (tri, 1, 1))):
                    mm(ps[a:a + CAP, 7, EXPERTS * dst:EXPERTS * dst + EXPERTS], lhs[:, a:a + CAP], sel[:, src, :],
                       start=(n < 2), stop=(n != 1), skip_group_check=True)
            mm(ps[0:EXPERTS, 6, 0:1], sel[:, 0, :], ones[:, 0:1], start=True, stop=False, skip_group_check=True)
            mm(ps[0:EXPERTS, 6, 0:1], sel[:, 1, :], ones[:, 0:1], start=False, stop=True, skip_group_check=True).then_inc(S["pos_up"], 1)
            def gather():
                for f in range(KD):
                    for i in range(TT):
                        for c in range(3):
                            last = mm(ps[:, 2, CAP * f:CAP * f + CAP], xpart[:, c, i, P * f:P * f + P], pick[:, i, :],
                                      start=(i == 0 and c == 0), stop=(i == TT - 1 and c == 2), skip_group_check=True)
                last.then_inc(S["hg_up"], 1)

            pe.wait_ge(S["pick_set"], 1)
            pe.wait_ge(S["x_split"], TT)
            gather()

            def further_items():
                pe.wait_ge(S["pos_sb"], 1)
                for j, src in enumerate((rt[:, 1], rt[:, 2])):
                    for i in range(TT):
                        last = nc.tensor.transpose(ps[0:EXPERTS, 3, T * j + P * i:T * j + P * i + P], src[:, i, :], ident)
                last.then_inc(S["rT_up"], 1)
                pe.wait_ge(S["extra_set"], 1)
                mm(ps[0:EXPERTS, 6, 1:2], cst[0:EXPERTS, C_TRI32:C_TRI32 + EXPERTS], chunk[:, 3:4], start=True, stop=True,
                   skip_group_check=True)
                mm(ps[0:1, 6, 2:3], ones[0:EXPERTS, 0:1], chunk[:, 3:4], start=True, stop=True,
                   skip_group_check=True).then_inc(S["cum_up"], 1)
                pe.wait_ge(S["rT_sb"], 1)
                pe.wait_ge(S["hot_set"], 1)
                for i in range(TT):
                    for a in (0, CAP):
                        t = P * i + a
                        mm(ps[a:a + CAP, 4, 16 * i:16 * i + OVER], rowT[:, 0, t:t + CAP], hot[:, 0, EXPERTS:ITEMS], start=True, stop=False,
                           skip_group_check=True)
                        mm(ps[a:a + CAP, 4, 16 * i:16 * i + OVER], ones[:, 0:CAP], hot[:, 1, EXPERTS:ITEMS], start=False, stop=True,
                           skip_group_check=True)
                        mm(ps[a:a + CAP, 5, 16 * i:16 * i + OVER], rowT[:, 1, t:t + CAP], hot[:, 0, EXPERTS:ITEMS], start=True, stop=True,
                           skip_group_check=True)
                mm(ps[0:1, 6, 8:8 + ITEMS], cst[:, C_E:C_E + 1], hot[:, 0, 0:ITEMS], start=True, stop=True,
                   skip_group_check=True).then_inc(S["item_up"], 1)

            def combine_weights(i):
                pe.wait_ge(S["pickw_set"], i)
                for t in range(TT):
                    for h in range(2):
                        last = nc.tensor.transpose(ps[:, 5, T * h + P * t:T * h + P * t + P], pickw[:, t, h, :], ident)
                last.then_inc(S["pwT_up"], 1)

            def combine(i, t):
                if t == 0:
                    pe.wait_ge(S["y_sb"], i)
                    pe.wait_ge(S["pwT_sb"], i)
                for h in range(2):
                    pe.wait_ge(S["comb_add"], i * 4 + max(2 * t + h - 1, 0))
                    mm(ps[:, 6 + h, :], pickwT[:, h, P * t:P * t + P], ysb, start=True, stop=True).then_inc(S["comb_up"], 1)

            def item_piece(i, j, first):
                k = 1 if j < GU_PIECES else 2
                if not first:
                    pe.wait_ge(arrived[slot_of[j]], i * 16 + 16 * round_of[j])
                    return slot(PRE + RING0 + j, k)
                if j in ring0:
                    take(PRE + ring0.index(j))
                    return slot(PRE + ring0.index(j), k)
                pe.wait_ge(S[f"aside{j}"], 32 if j == 9 else 16)
                return None if j == 9 else aside[j].rearrange("p (k n) -> p k n", k=k)

            def item(i, first=False):
                pe.wait_ge(S["hotb_set"], i + 1)
                for b in range(2):
                    for h in range(2):
                        mm(ps[CAP * h:CAP * h + CAP, b, :], hotb, bgu_rows[:, D * b + 512 * h:D * b + 512 * h + 512],
                           start=True, stop=False, skip_group_check=True)
                pe.wait_ge(S["hg_sb"], i + 1)
                for j in range(GU_PIECES):
                    w = item_piece(i, j, first)
                    for b in range(2):
                        for h in range(2):
                            last = mm(ps[CAP * h:CAP * h + CAP, b, :], hg[:, j, :],
                                      w[:, 0, D * b + 512 * h:D * b + 512 * h + 512],
                                      start=False, stop=(j == GU_PIECES - 1), skip_group_check=True)
                    last.then_inc(w_used, 1)
                    if j == 1 and not first:
                        combine_weights(i)
                    if j == 3 and first:
                        further_items()
                    if j in (3, 4) and not first:
                        combine(i, j - 3)
                pe.wait_ge(S["pick_set"], i + 2)
                gather()
                if first:
                    pe.wait_ge(S["rT_sb"], 1)
                else:
                    pe.wait_ge(S["y_sb"], i)
                for h in range(2):
                    last = mm(ps[CAP * h:CAP * h + CAP, 3, :], hotb, bdn_rows[:, 512 * h:512 * h + 512],
                              start=True, stop=False, skip_group_check=True)
                if first:
                    last.then_inc(S["comb_up"], 2 * TT)
                pe.wait_ge(S["act_set"], i + 1)
                if first:
                    pe.wait_ge(S["item_sb"], 4)
                for j in range(4):
                    last = nc.tensor.transpose(ps[:, 4, P * j:P * j + P], act_[:, P * j:P * j + P], ident)
                last.then_inc(S["actT_up"], 1)
                pe.wait_ge(S["actT_sb"], i + 1)
                for j in range(DN_PIECES):
                    w = item_piece(i, GU_PIECES + j, first)
                    for kk in range(2):
                        k = 2 * j + kk
                        wk = halves[kk] if w is None else w[:, kk, :]
                        for h in range(2):
                            last = mm(ps[CAP * h:CAP * h + CAP, 3, :], actT[:, k % 4, k // 4, :], wk[:, 512 * h:512 * h + 512],
                                      start=False, stop=(k == KD - 1), skip_group_check=True)
                    last.then_inc(w_used, 1)

            item(0, first=True)
            count = pe.value_load(icnt[0:1, 0:1], min_val=EXPERTS, max_val=ITEMS)
            with pe.Fori(1, EXPERTS) as i:
                item(i)
            with pe.If(count > EXPERTS):
                with pe.Fori(EXPERTS, ITEMS) as i:
                    with pe.If(i < count):
                        item(i)
            combine_weights(count)
            combine(count, 0), combine(count, 1)

        @block.scalar
        def _(act):
            link = linker(act, S["lnA"])
            act.dma_start(are[:, :], a_re[0].rearrange("(s q) p -> s (q p)", q=2)).then_inc(S["ssm_in"], 16)
            act.dma_start(aim[:, :], a_im[0].rearrange("(s q) p -> s (q p)", q=2)).then_inc(S["ssm_in"], 16)
            act.dma_start(ldt[:, :], log_dt.rearrange("a (s q) -> (a s) q", q=2)).then_inc(S["ssm_in"], 16)
            act.wait_ge(S["cols_sb"], 1)
            nc.scalar.activation(cond[:, :], cols[:, R_C:R_C + KD], ACT.Sigmoid).then_inc(S["cond_half"], 1)
            act.wait_ge(S["ssm_in"], 48)
            nc.scalar.activation(ldt[:, :], ldt[:, :], ACT.Exp).then_inc(S["dt_set"], 1)
            act.wait_ge(S["lrdt_set"], 1)
            nc.scalar.activation(sprow[:, 0, :], sprow[:, 5, :], ACT.Exp).then_inc(S["mag_set"], 1)
            act.wait_ge(S["angle_set"], 1)
            nc.scalar.activation(sprow[:, 2, :], sprow[:, 6, :], ACT.Sin).then_inc(S["trig_set"], 1)
            nc.scalar.activation(sprow[:, 7, :], sprow[:, 6, :], ACT.Sin, scale=0.5).then_inc(S["trig_set"], 1)
            act.wait_ge(S["x_in"], 16)
            act.wait_ge(S["lnD"], 1)
            for i in range(TT):
                link(nc.scalar.activation(hT[:, 4 * i:4 * i + 4, :].rearrange("p k t -> p (k t)"), x_tok[:, i, :], ACT.Square,
                                          accum_out=stat[:, 0, i:i + 1]))
            nc.scalar.activation(stat[:, 1, :], stat[:, 0, :], ACT.Sqrt, bias=stat[:, 3, 0:1], scale=1.0 / D).then_inc(S["sq1"], 1)
            def row_copy(n):
                act.wait_ge(w_used, place["ada", KD * (n + 1) - 1] + 1)
                nc.scalar.copy(modrow[n], ps[:, MOD_BANK[n], :]).then_inc(S["modrow_sb"], 1)

            row_copy(0)
            act.wait_ge(S["mod1_sb"], 1)
            act.wait_ge(S["scale1_set"], 1)
            act.wait_ge(S["xT_up"], 1)
            for k in range(KD // 2, KD):
                nc.scalar.activation(hT[:, k, :], ps[:, k // 2, (k % 2) * T:(k % 2) * T + T], ACT.Identity,
                                     bias=mod[:, SH1 + k:SH1 + k + 1], scale=scale1[:, k:k + 1]).then_inc(S["h_sb"], 1)
            def head(h):
                act.wait_ge(S["negmax"], h + 1)
                for j, (a, b) in enumerate(((0, P), (P, 3 * P))):
                    last = nc.scalar.activation(prob[:, a:b], prob[:, a:b], ACT.Exp, bias=mx[:, h % 2, j:j + 1],
                                                scale=HD ** -0.5, accum_out=mx[:, h % 2, 2 + j:3 + j])
                    last.then_inc(S["expd"], 1)
                act.wait_ge(S["probsT_up"], h + 1)
                nc.scalar.copy(probT[:, :], ps[:, 7, 0:3 * P]).then_inc(S["probsT_sb"], 1)
                act.wait_ge(S["o_up"], h + 1)
                a = HD * (h % 2)
                nc.scalar.copy(oT[a:a + HD, h // 2, :], ps[a:a + HD, 7, 0:T]).then_inc(S["o_sb"], 1)

            for g, dst in enumerate((qT, kT, uT, v_tok, gaT[:, 0:4, :], gaT[:, 4:8, :], gbT[:, 0:4, :], gbT[:, 4:8, :])):
                act.wait_ge(w_used, place["in", 2 * g + 1] + 1)
                nc.scalar.copy(dst, ps[:, 2 * (g % 2):2 * (g % 2) + 2, :].rearrange(
                    "p b (m t) -> p (b m) t", t=dst.shape[2])).then_inc(S["proj_sb"], 1)
                if g == 0:
                    act.wait_ge(S["BT_up"], 1)
                    nc.scalar.copy(BT[:, :, :, :].rearrange("p r m n -> p (r m n)"), ps[:, 6:8, :].rearrange("p b n -> p (b n)")).then_inc(S["BT_sb"], 1)
                    for r in range(2):
                        act.wait_ge(S[f"CT{r}_up"], 1)
                        nc.scalar.activation(CT[:, r].rearrange("p m n -> p (m n)"), ps[:, 4 + 2 * r, :], ACT.Copy,
                                             scale=(1.0 if r == 0 else -1.0)).then_inc(S[f"CT{r}_sb"], 1)
                if g in (1, 2):
                    row_copy(g)
                if g >= 3 and g < 7:
                    head(2 * g - 6), head(2 * g - 5)
            act.wait_ge(S["y_skip"], KW)
            nc.scalar.activation(gluT, uT, ACT.Gelu_apprx_tanh).then_inc(S["gelu"], 1)
            act.wait_ge(S["proj_sb"], 8)
            nc.scalar.activation(gbT, gbT, ACT.Sigmoid).then_inc(S["sig_gb"], 1)
            for j, dst in enumerate((gate_mix, gate_ffn)):
                act.wait_ge(S["row_up"], j + 1)
                nc.scalar.copy(dst[:, :], ps[:, 4 + 2 * j:6 + 2 * j, :].rearrange("p b n -> p (b n)")).then_inc(S["row_sb"], 1)
            nc.scalar.activation(gaT, gaT, ACT.Sigmoid).then_inc(S["sig_ga"], 1)
            for h in range(2):
                act.wait_ge(w_used, place["glu", 2 * h + 1] + 1)
                if h == 1:
                    act.wait_ge(S["ya_set"], 1)
                b = 6 - 4 * h
                nc.scalar.activation(sigb, ps[:, b:b + 2, :].rearrange("p b (m t) -> p (b m) t", t=T), ACT.Sigmoid).then_inc(S["sigb_set"], 1)
            act.wait_ge(S["merged"], 2)
            act.dma_start(wr[:, :, :], w_router[0].rearrange("(k p) e -> p k e", p=P)).then_inc(S["late_in"], 16)
            act.dma_start(brt[:, :], b_router.to_broadcast([P, EXPERTS])).then_inc(S["late_in"], 16)
            act.wait_ge(S["zeroed"], 1)
            act.dma_start(bgu_rows[0:EXPERTS, :], b_gu[0]).then_inc(S["late_in"], 16)
            act.dma_start(bdn_rows[0:EXPERTS, :], b_down[0]).then_inc(S["late_in"], 16)
            act.dma_start(gfin, g_final.rearrange("(a d) -> a d", a=1).to_broadcast([P, D])).then_inc(S["late_in"], 16)
            for i in range(TT):
                act.wait_ge(S["x1"], i + 1)
                nc.scalar.activation(squares, x_tok[:, i, :], ACT.Square, accum_out=stat[:, 0, i:i + 1]).then_inc(S["sqsum2"], 1)
                act.wait_ge(S["sqsum2"], i + 1)
                nc.scalar.activation(stat[:, 1, i:i + 1], stat[:, 0, i:i + 1], ACT.Sqrt, bias=stat[:, 3, 0:1], scale=1.0 / D).then_inc(S["sq2"], 1)
                act.wait_ge(S["x2T_up"], i + 1)
                for k in range(i * KD // 2, KD):
                    nc.scalar.activation(hT[:, k, P * i:P * i + P], ps[:, 2 * i + k // 4, P * (k % 4):P * (k % 4) + P], ACT.Identity,
                                         bias=mod[:, SH2 + k:SH2 + k + 1], scale=scale2[:, k:k + 1]).then_inc(S["h2_sb"], 1)
                nc.scalar.copy(xpart[:, 0, i], xn_tok[:, i, :]).then_inc(S["xh_set"], 1)
                act.wait_ge(S["xr_set"], i + 1)
                nc.scalar.copy(xpart[:, 1, i], gate_rest[:, i, :]).then_inc(S["xm_set"], 1)
            for i in range(TT):
                act.wait_ge(S["top_set"], i + 1)
                nc.scalar.activation(rt[:, 3, i, :], lg[:, i, :], ACT.Exp, bias=rs[:, i, 0:1]).then_inc(S["ex_set"], 1)
            act.wait_ge(S["rT_up"], 1)
            act.wait_ge(S["zeroed"], 1)
            nc.scalar.copy(rowT[0:EXPERTS, :, :].rearrange("p j t -> p (j t)"), ps[0:EXPERTS, 3, :]).then_inc(S["rT_sb"], 1)

            def combine_copies(i):
                act.wait_ge(S["pwT_up"], i + 1)
                nc.scalar.copy(pickwT.rearrange("p h t -> p (h t)"), ps[:, 5, :]).then_inc(S["pwT_sb"], 1)

            def item(i, first=False):
                if not first:
                    combine_copies(i)
                act.wait_ge(S["gated"], i + 1)
                nc.scalar.activation(sig, gate, ACT.Sigmoid, scale=ALPHA).then_inc(S["sig_set"], 1)
                act.wait_ge(S["actT_up"], i + 1)
                nc.scalar.copy(actT.rearrange("p j h s -> p (j h s)"), ps[:, 4, :]).then_inc(S["actT_sb"], 1)
                act.wait_ge(w_used, i * SLOTS + (PRE + SLOTS))
                nc.scalar.copy(ysb, ps[:, 3, :]).then_inc(S["y_sb"], 1)

            item(0, first=True)
            act.wait_ge(S["item_sb"], 4)
            count = act.value_load(icnt[0:1, 0:1], min_val=EXPERTS, max_val=ITEMS)
            with act.Fori(1, EXPERTS) as i:
                item(i)
            with act.If(count > EXPERTS):
                with act.Fori(EXPERTS, ITEMS) as i:
                    with act.If(i < count):
                        item(i)
            combine_copies(count)
            for i in range(TT):
                act.wait_ge(S["fin"], 2 * i + 2)
                nc.scalar.activation(xn_tok[:, i, :], x_tok[:, i, :], ACT.Square,
                                     accum_out=stat[:, 0, i:i + 1]).then_inc(S["sqsum3"], 1)
                act.wait_ge(S["sqsum3"], i + 1)
                nc.scalar.activation(stat[:, 1, i:i + 1], stat[:, 0, i:i + 1], ACT.Sqrt, bias=stat[:, 3, 0:1], scale=1.0 / D).then_inc(S["sq3"], 1)

        @block.gpsimd
        def _(pool):
            nc.gpsimd.memset(ones[:, :], 1.0).then_inc(S["ones_set"], 1)
            link = linker(pool, S["lnP"])
            pool.wait_ge(S["sprm_sb"], 1)
            link(nc.gpsimd.memset(ecos[:, :, 0:1], 1.0))
            link(nc.gpsimd.memset(esin[:, :, 0:1], 0.0))
            link(nc.gpsimd.tensor_copy(ecos[:, :, 1:2], sprm[:, 1, :].unsqueeze(2)))
            link(nc.gpsimd.tensor_copy(esin[:, :, 1:2], sprm[:, 2, :].unsqueeze(2)))
            for n in (2, 4, 8, 16, 32):
                square(nc.gpsimd, link, n)
                double(nc.gpsimd, link, n, xs[:, 0])
            pool.engine_nop().then_inc(S["phase_lo"], 1)
            for j in range(8):
                b = j % 2
                zr, zi = z[:, b, 0, :].rearrange("p (s t) -> p s t", s=2), z[:, b, 1, :].rearrange("p (s t) -> p s t", s=2)
                cs, sn = ecos[:, 2 * j:2 * j + 2, :], esin[:, 2 * j:2 * j + 2, :]
                xr, xi = xs[:, b, 0, :].rearrange("p (s t) -> p s t", s=2), xs[:, b, 1, :].rearrange("p (s t) -> p s t", s=2)
                t = ptmp[:, :].rearrange("p (s t) -> p s t", s=2)
                pool.wait_ge(S["scanned"], 4 * j + 4)
                if j == 0:
                    pool.wait_ge(S["phases"], 1)
                if j >= 2:
                    pool.wait_ge(S["xs_read"], j - 1)
                link(nc.gpsimd.tensor_tensor(xr, zr, cs, ALU.mult))
                link(nc.gpsimd.tensor_tensor(t, zi, sn, ALU.mult))
                link(nc.gpsimd.tensor_tensor(xr, xr, t, ALU.subtract))
                link(nc.gpsimd.tensor_tensor(xi, zr, sn, ALU.mult))
                link(nc.gpsimd.tensor_tensor(t, zi, cs, ALU.mult))
                nc.gpsimd.tensor_tensor(xi, xi, t, ALU.add).then_inc(S["xs_set"], 1)
                pool.wait_ge(S["xs_set"], j + 1)
            pool.wait_ge(S["merged"], 2)
            for dst in (bgu_rows, bdn_rows):
                link(nc.gpsimd.memset(dst, 0.0))
            nc.gpsimd.memset(rowT, 0.0).then_inc(S["zeroed"], 1)
            for i in range(TT):
                pool.wait_ge(S["xh_set"], i + 1)
                nc.gpsimd.tensor_tensor(gate_rest[:, i, :], xn_tok[:, i, :], xpart[:, 0, i], ALU.subtract).then_inc(S["xr_set"], 1)
                pool.wait_ge(S["xm_set"], i + 1)
                nc.gpsimd.tensor_tensor(xpart[:, 2, i], gate_rest[:, i, :], xpart[:, 1, i], ALU.subtract).then_inc(S["x_split"], 1)
                pool.wait_ge(S["x_split"], i + 1)
            nc.gpsimd.memset(acc, 0.0).then_inc(S["comb_add"], 2 * TT)
            pool.wait_ge(w_used, PRE + GU_PIECES)
            nc.gpsimd.memset(pickw, 0.0).then_inc(S["pwT_up"], 1)

        @block.vector
        def _(dve):
            link = linker(dve, S["lnD"])
            V = nc.vector
            link(V.memset(stat[:, 3, :], EPS))
            for table in (hot, posI, wI):
                link(V.memset(table[:, :, :], 0.0))
            dve.wait_ge(S["cols_up"], 1)
            V.tensor_copy(cols[:, :], ps[:, 7, 0:R_ALL]).then_inc(S["cols_sb"], 1)
            dve.wait_ge(S["cols_sb"], 1)
            dve.wait_ge(S["cond_half"], 1)
            link(V.tensor_tensor(cond[:, :], cond[:, :], cols[:, R_C:R_C + KD], ALU.mult))
            V.tensor_copy(condb[:, :, :], cond[:, :].unsqueeze(2).to_broadcast([P, KD, 32])).then_inc(S["cond_set"], 1)
            dve.wait_ge(S["dt_set"], 1)
            dve.wait_ge(S["ssm_in"], 48)
            dtb = ldt[:, :].unsqueeze(2).to_broadcast([ST, 2, N])

            def mod_group(ap, n):
                return ap[:, 2 * KD * n:2 * KD * (n + 1)].rearrange("p (j c) -> p c j", j=4)

            def modT(bank):
                return ps[:, bank, :].rearrange("p (c j r) -> p c j r", c=4, j=4)[:, :, :, 0]

            def row(j):
                return sprow[:, j, :]

            def two(ap):
                return ap.rearrange("s (q n) -> s q n", q=2)

            V.tensor_tensor(two(row(5)), two(are[:, :]), dtb, ALU.mult).then_inc(S["lrdt_set"], 1)
            link(V.tensor_tensor(two(row(6)), two(aim[:, :]), dtb, ALU.mult))
            link(V.tensor_scalar(row(8), row(6), 1.0 / TWO_PI, ROUND, ALU.mult, ALU.add))
            link(V.tensor_scalar(row(8), row(8), -ROUND, None, ALU.add))
            parts, rest = [], TWO_PI
            for bits in (2.0 ** -6, 2.0 ** -16):
                parts.append(np.floor(rest / bits) * bits)
                rest -= parts[-1]
            for part in parts + [rest]:
                link(V.scalar_tensor_tensor(row(6), row(8), -float(part), row(6), ALU.mult, ALU.add))
            V.tensor_scalar(row(6), row(6), float(np.float32(3.1415925)), -float(np.float32(3.1415925)), ALU.min, ALU.max).then_inc(S["angle_set"], 1)
            dve.wait_ge(S["mag_set"], 1)
            dve.wait_ge(S["trig_set"], 2)
            link(V.tensor_tensor(row(1), row(7), row(7), ALU.mult))
            link(V.tensor_scalar(row(1), row(1), -2.0, 1.0, ALU.mult, ALU.add))
            link(V.tensor_tensor(row(8), row(0), row(1), ALU.mult))
            link(V.tensor_tensor(row(9), row(0), row(2), ALU.mult))
            link(V.tensor_scalar(row(8), row(8), -1.0, None, ALU.add))
            link(V.tensor_tensor(row(10), are[:, :], are[:, :], ALU.mult))
            link(V.tensor_tensor(row(11), aim[:, :], aim[:, :], ALU.mult))
            link(V.tensor_tensor(row(10), row(10), row(11), ALU.add))
            link(V.reciprocal(row(10), row(10)))
            link(V.tensor_tensor(row(11), row(8), are[:, :], ALU.mult))
            link(V.tensor_tensor(row(12), row(9), aim[:, :], ALU.mult))
            link(V.tensor_tensor(row(11), row(11), row(12), ALU.add))
            link(V.tensor_tensor(row(3), row(11), row(10), ALU.mult))
            link(V.tensor_tensor(row(11), row(9), are[:, :], ALU.mult))
            link(V.tensor_tensor(row(12), row(8), aim[:, :], ALU.mult))
            link(V.tensor_tensor(row(11), row(11), row(12), ALU.subtract))
            V.tensor_tensor(row(4), row(11), row(10), ALU.mult).then_inc(S["ssm_rows"], 1)
            dve.wait_ge(S["sq1"], 1)
            link(V.reciprocal(stat[:, 2, :], stat[:, 1, :]))
            for i in range(TT):
                V.tensor_scalar(xn_tok[:, i, :], x_tok[:, i, :], stat[:, 2, i:i + 1], None, ALU.mult).then_inc(S["xn1"], 1)
            dve.wait_ge(S["sprm_up"], 1)
            V.tensor_copy(sprm[:, :, :].rearrange("p j s -> p (j s)"), ps[:, 6, 0:5 * ST]).then_inc(S["sprm_sb"], 1)
            dve.wait_ge(S["sprm_sb"], 1)
            dve.wait_ge(S["modT_up"], 1)
            V.tensor_tensor(mod_group(mod, 0), modT(5), mod_group(cols[:, R_ADA:R_ADA + 6 * KD], 0), ALU.add).then_inc(S["mod1_sb"], 1)
            dve.wait_ge(S["mod1_sb"], 1)
            V.scalar_tensor_tensor(scale1[:, :], mod[:, SC1:SC1 + KD], 1.0, cols[:, R_GMIX:R_GMIX + KD], ALU.add, ALU.mult).then_inc(S["scale1_set"], 1)
            dve.wait_ge(S["scale1_set"], 1)
            dve.wait_ge(S["xT_up"], 1)
            for k in range(KD // 2):
                V.tensor_scalar(hT[:, k, :], ps[:, k // 2, (k % 2) * T:(k % 2) * T + T], scale1[:, k:k + 1],
                                mod[:, SH1 + k:SH1 + k + 1], ALU.mult, ALU.add).then_inc(S["h_sb"], 1)

            dve.wait_ge(S["bc_in"], 64)
            dve.wait_ge(S["const_in"], 16)
            cr = sprm[:, 3, :].unsqueeze(2).to_broadcast([P, ST, C])
            ci = sprm[:, 4, :].unsqueeze(2).to_broadcast([P, ST, C])
            t0 = tmp[:, 0, 0:256].rearrange("p (s c) -> p s c", s=ST)
            t1 = tmp[:, 0, 256:512].rearrange("p (s c) -> p s c", s=ST)
            for r in range(2):
                link(V.tensor_tensor(t0, b_in[:, r], cr, ALU.mult))
                link(V.tensor_tensor(t1, b_in[:, 1 - r], ci, ALU.mult))
                link(V.tensor_tensor(t0, t0, t1, ALU.subtract if r == 0 else ALU.add))
                for q in range(2):
                    last = V.tensor_scalar(Bblk[:, r, :, q, :], t0, cst[:, C_MB + q:C_MB + q + 1], None, ALU.mult)
                    if r == 0 or q == 0:
                        link(last)
            last.then_inc(S["Bblk_set"], 1)
            for r in range(2):
                for q in range(2):
                    last = V.tensor_scalar(Cblk[:, r, :, q, :], c_in[:, r], cst[:, C_MC + q:C_MC + q + 1], None, ALU.mult)
                    if q == 0:
                        link(last)
                last.then_inc(S[f"Cblk{r}_set"], 1)
            def rotary(n):
                dst = (qT, kT)[n]
                dve.wait_ge(S["rot_up"], n + 1)
                for m in range(KW):
                    t = tmp[:, m % 2, 0:T]
                    last = V.tensor_tensor(t, ps[:, 4 + m // 2, (m % 2) * T:(m % 2) * T + T], cst[:, C_SIN:C_SIN + T], ALU.mult)
                    if m == KW - 1:
                        last.then_inc(S["rot_read"], 1)
                        dve.wait_ge(S["rot_read"], n + 1)
                    else:
                        link(last)
                    link(V.tensor_tensor(dst[:, m, :], dst[:, m, :], cst[:, C_COS:C_COS + T], ALU.mult))
                    last = V.tensor_tensor(dst[:, m, :], dst[:, m, :], t, ALU.add)
                    if m < KW - 1:
                        link(last)
                last.then_inc(S["rope_set"], 1)
                dve.wait_ge(S["rope_set"], n + 1)

            def recurrence(j):
                b = j % 2
                cs, sn = ecos[:, 2 * j:2 * j + 2, :], esin[:, 2 * j:2 * j + 2, :]
                br, bi = (ps[:, 4:6, T * r:T * r + T] for r in range(2))
                tz = [tmp[:, r, :].rearrange("p (s t) -> p s t", s=2) for r in range(2)]
                zz = [z[:, b, r, :].rearrange("p (s t) -> p s t", s=2) for r in range(2)]
                dve.wait_ge(S["bu_up"], j + 1)
                if j >= 2:
                    dve.wait_ge(S["xs_set"], j - 1)
                V.tensor_tensor(zz[0], br, cs, ALU.mult).then_inc(S["turn"], 1)
                V.tensor_tensor(tz[0], bi, sn, ALU.mult).then_inc(S["turn"], 1)
                V.tensor_tensor(zz[1], bi, cs, ALU.mult).then_inc(S["turn"], 1)
                V.tensor_tensor(tz[1], br, sn, ALU.mult).then_inc(S["bu_read"], 1)
                dve.wait_ge(S["turn"], 3 * j + 3)
                dve.wait_ge(S["bu_read"], j + 1)
                V.tensor_tensor(zz[0], zz[0], tz[0], ALU.add).then_inc(S["turned"], 1)
                V.tensor_tensor(zz[1], zz[1], tz[1], ALU.subtract).then_inc(S["turned"], 1)
                for r in range(2):
                    dve.wait_ge(S["turned"], 2 * j + 1 + r)
                    for q in range(2):
                        s = 2 * j + q
                        last = V.tensor_tensor_scan(zz[r][:, q, :], sprm[:, 0, s:s + 1].to_broadcast([P, T]), zz[r][:, q, :], 0.0,
                                                    ALU.mult, ALU.add)
                        last.then_inc(S["scanned"], 1)

            def head(h):
                b = h % 2
                dve.wait_ge(S["sc_up"], h + 1)
                link(V.tensor_tensor(prob[:, :], ps[:, 7, 0:3 * P], cst[:, C_CAUSAL:C_CAUSAL + 3 * P], ALU.add))
                V.tensor_reduce(mx[:, b, 0:1], prob[:, 0:P], AX.X, ALU.max).then_inc(S["row_max"], 1)
                V.tensor_reduce(mx[:, b, 1:2], prob[:, P:3 * P], AX.X, ALU.max).then_inc(S["row_max"], 1)
                dve.wait_ge(S["row_max"], 2 * h + 2)
                V.tensor_scalar(mx[:, b, 0:2], mx[:, b, 0:2], -HD ** -0.5, None, ALU.mult).then_inc(S["negmax"], 1)
                dve.wait_ge(S["expd"], 2 * h + 2)
                link(V.reciprocal(mx[:, b, 2:4], mx[:, b, 2:4]))
                V.tensor_scalar(prob[:, 0:P], prob[:, 0:P], mx[:, b, 2:3], None, ALU.mult).then_inc(S["probs_half"], 1)
                V.tensor_scalar(prob[:, P:3 * P], prob[:, P:3 * P], mx[:, b, 3:4], None, ALU.mult).then_inc(S["probs"], 1)
                dve.wait_ge(S["probs_half"], h + 1)
                dve.wait_ge(S["probs"], h + 1)

            def skip(m):
                dve.wait_ge(S["xs_read"], 2 * m + 2)
                V.scalar_tensor_tensor(uT[:, m, :], uT[:, m, :], cols[:, R_D + m:R_D + m + 1],
                                       ps[:, 6, (m % 2) * T:(m % 2) * T + T], ALU.mult, ALU.add).then_inc(S["y_skip"], 1)

            def modulation(n):
                dve.wait_ge(S["modT_up"], n + 1)
                V.tensor_tensor(mod_group(mod, n), modT(MOD_BANK[n]), mod_group(cols[:, R_ADA:R_ADA + 6 * KD], n),
                                ALU.add).then_inc(S["mod2_sb"], 1)
                dve.wait_ge(S["mod2_sb"], n)
                if n == 2:
                    link(V.scalar_tensor_tensor(scale2[:, :], mod[:, SC2:SC2 + KD], 1.0, cols[:, R_GFFN:R_GFFN + KD], ALU.add, ALU.mult))

            dve.wait_ge(S["phase_lo"], 1)
            square(V, link, T // 4)
            double(V, link, T // 4, tmp)
            rotary(0)
            square(V, link, T // 2)
            double(V, link, T // 2, tmp)
            V.engine_nop().then_inc(S["phases"], 1)
            rotary(1)
            dve.wait_ge(S["BT_up"], 1)
            dve.wait_ge(S["CT1_up"], 1)
            modulation(1)
            recurrence(0)
            modulation(2)
            recurrence(1)
            for h in range(HEADS):
                head(h)
                if h + 2 < 8:
                    recurrence(h + 2)
                if h % 2 == 1:
                    skip(h // 2)
            dve.wait_ge(S["sig_gb"], 1)
            for h in range(2):
                dve.wait_ge(w_used, place["ao", h] + 1)
                V.tensor_tensor(ybT[:, 4 * h:4 * h + 4, :], ps[:, 2 * h:2 * h + 2, :].rearrange("p b (m t) -> p (b m) t", t=T),
                                gbT[:, 4 * h:4 * h + 4, :], ALU.mult).then_inc(S["yb_used"], 1)
            dve.wait_ge(S["sig_ga"], 1)
            dve.wait_ge(S["yb_used"], 2)
            for h in range(2):
                m4 = slice(4 * h, 4 * h + 4)
                b = 4 - 4 * h
                dve.wait_ge(S["sigb_set"], h + 1)
                V.tensor_tensor(yaT[:, m4, :], ps[:, b:b + 2, :].rearrange("p b (m t) -> p (b m) t", t=T), sigb,
                                ALU.mult).then_inc(S["ya_set"], 1)
                dve.wait_ge(S["ya_set"], h + 1)
                link(V.tensor_tensor(mergedT[:, m4, :], yaT[:, m4, :], gaT[:, m4, :], ALU.mult))
                V.tensor_tensor(mergedT[:, m4, :], mergedT[:, m4, :], ybT[:, m4, :], ALU.add).then_inc(S["merged"], 1)
            dve.wait_ge(S["row_sb"], 2)
            for i in range(TT):
                if i == 0:
                    dve.wait_ge(S["out_up"], 1)
                else:
                    dve.wait_ge(w_used, PRE)
                scr = xn_tok[:, i, :]
                link(V.tensor_tensor(scr, ps[:, 4 + 2 * i:6 + 2 * i, :].rearrange("p b n -> p (b n)"), gate_mix[:, :], ALU.mult))
                V.tensor_tensor(x_tok[:, i, :], x_tok[:, i, :], scr, ALU.add).then_inc(S["x1"], 1)
                dve.wait_ge(S["x1"], i + 1)
                dve.wait_ge(S["sq2"], i + 1)
                link(V.reciprocal(stat[:, 2, i:i + 1], stat[:, 1, i:i + 1]))
                V.tensor_scalar(xn_tok[:, i, :], x_tok[:, i, :], stat[:, 2, i:i + 1], None, ALU.mult).then_inc(S["xn2"], 1)
                dve.wait_ge(S["xn2"], i + 1)
            dve.wait_ge(S["x2T_up"], TT)
            for k in range(KD // 2):
                V.tensor_scalar(hT[:, k, P:T], ps[:, 2, P * k:P * k + P], scale2[:, k:k + 1],
                                mod[:, SH2 + k:SH2 + k + 1], ALU.mult, ALU.add).then_inc(S["h2_sb"], 1)
            sel, pos, wgt, ex, eq, run = (rt[:, j] for j in range(6))
            dve.wait_ge(S["ones_set"], 1)
            for i in range(TT):
                dve.wait_ge(S["logit_up"], i + 1)
                link(V.tensor_tensor(lg[:, i, :], ps[:, 4 + i, 0:EXPERTS], brt[:, :], ALU.add))
                link(V.max(top[:, i, :], lg[:, i, :]))
                V.tensor_scalar(rs[:, i, 0:1], top[:, i, 0:1], -1.0, None, ALU.mult).then_inc(S["top_set"], 1)
                t4 = top[:, i, TOPK - 1:TOPK]
                link(V.tensor_scalar(sel[:, i, :], lg[:, i, :], t4, None, ALU.is_gt))
                link(V.tensor_reduce(rs[:, i, 1:2], sel[:, i, :], AX.X, ALU.add))
                link(V.tensor_scalar(rs[:, i, 1:2], rs[:, i, 1:2], -1.0, float(TOPK), ALU.mult, ALU.add))
                link(V.tensor_scalar(eq[:, i, :], lg[:, i, :], t4, None, ALU.is_equal))
                link(V.tensor_tensor_scan(run[:, i, :], ones[:, 0:EXPERTS], eq[:, i, :], 0.0, ALU.mult, ALU.add))
                link(V.scalar_tensor_tensor(eq[:, i, :], run[:, i, :], rs[:, i, 1:2], eq[:, i, :], ALU.is_le, ALU.mult))
                V.tensor_tensor(sel[:, i, :], sel[:, i, :], eq[:, i, :], ALU.add).then_inc(S["sel_set"], 1)
                dve.wait_ge(S["sel_set"], i + 1)
            dve.wait_ge(S["pos_up"], 1)
            V.scalar_tensor_tensor(pos, ps[:, 7, 0:TT * EXPERTS].rearrange("p (i e) -> p i e", i=TT), 1.0, sel,
                                   ALU.add, ALU.mult).then_inc(S["pos_half"], 1)
            dve.wait_ge(S["pos_half"], 1)
            link(V.tensor_copy(posI[:, :, 0:EXPERTS], pos))
            slots = cst[:, C_SLOT:C_SLOT + CAP]

            def choose(col):
                for t in range(TT):
                    last = V.tensor_scalar(pick[:, t, :], slots, posI[:, t, bass.ds(col, 1)], None, ALU.is_equal)
                    last.then_inc(S["pick_half" if t == 0 else "pick_set"], 1)

            choose(0)
            for i in range(TT):
                dve.wait_ge(S["ex_set"], i + 1)
                link(V.tensor_tensor(ex[:, i, :], ex[:, i, :], sel[:, i, :], ALU.mult))
                link(V.tensor_reduce(rs[:, i, 2:3], ex[:, i, :], AX.X, ALU.add))
                link(V.reciprocal(rs[:, i, 2:3], rs[:, i, 2:3]))
                link(V.tensor_scalar(wgt[:, i, :], ex[:, i, :], rs[:, i, 2:3], None, ALU.mult))
                link(V.tensor_copy(wI[:, i, 0:EXPERTS], wgt[:, i, :]))
            V.tensor_copy(hot[0:EXPERTS, 0, 0:EXPERTS], cst[0:EXPERTS, C_ID32:C_ID32 + EXPERTS]).then_inc(S["pos_sb"], 1)
            dve.wait_ge(S["pos_sb"], 1)

            def expert_of(i):
                V.tensor_copy(hotb, hot[:, 0, bass.ds(i, 1)].to_broadcast([P, CAP])).then_inc(S["hotb_set"], 1)

            def modulated(done):
                dve.wait_ge(S["hg_up"], done)
                V.tensor_tensor(hg, ps[:, 2, :].rearrange("p (f s) -> p f s", f=KD),
                                scale2[:, :].unsqueeze(2).to_broadcast([P, KD, CAP]), ALU.mult).then_inc(S["hg_half"], 1)
                dve.wait_ge(S["hg_half"], done)
                V.tensor_tensor(hg, hg, mod[:, SH2:SH2 + KD].unsqueeze(2).to_broadcast([P, KD, CAP]), ALU.add).then_inc(S["hg_sb"], 1)

            expert_of(0)
            modulated(1)
            link(V.tensor_copy(chunk[:, 0:1], ps[0:EXPERTS, 6, 0:1]))
            link(V.tensor_scalar(chunk[:, 1:2], chunk[:, 0:1], float(CAP), None, ALU.is_gt))
            link(V.tensor_scalar(chunk[:, 2:3], chunk[:, 0:1], float(2 * CAP), chunk[:, 1:2], ALU.is_gt, ALU.add))
            V.tensor_scalar(chunk[:, 3:4], chunk[:, 0:1], float(3 * CAP), chunk[:, 2:3], ALU.is_gt, ALU.add).then_inc(S["extra_set"], 1)
            dve.wait_ge(S["extra_set"], 1)
            dve.wait_ge(S["cum_up"], 1)
            link(V.tensor_copy(chunk[:, 4:5], ps[0:EXPERTS, 6, 1:2]))
            link(V.tensor_tensor(chunk[:, 5:6], chunk[:, 4:5], chunk[:, 3:4], ALU.subtract))
            iq = cst[0:EXPERTS, C_Q:C_Q + OVER]
            oh, base, hs = (hot[0:EXPERTS, j, EXPERTS:ITEMS] for j in range(3))
            link(V.tensor_scalar(oh, iq, chunk[:, 5:6], None, ALU.is_ge))
            link(V.tensor_scalar(hs, iq, chunk[:, 4:5], None, ALU.is_lt))
            link(V.tensor_tensor(oh, oh, hs, ALU.mult))
            link(V.tensor_scalar(base, iq, chunk[:, 5:6], 1.0, ALU.subtract, ALU.add))
            V.scalar_tensor_tensor(base, base, -float(CAP), oh, ALU.mult, ALU.mult).then_inc(S["hot_set"], 1)
            dve.wait_ge(S["item_up"], 1)
            link(V.tensor_copy(posI[:, :, EXPERTS:ITEMS], ps[:, 4, 0:TT * 16].rearrange("p (i n) -> p i n", i=TT)[:, :, 0:OVER]))
            V.tensor_copy(wI[:, :, EXPERTS:ITEMS], ps[:, 5, 0:TT * 16].rearrange("p (i n) -> p i n", i=TT)[:, :, 0:OVER]).then_inc(S["item_sb"], 2)
            V.tensor_copy(itab[:, 0:ITEMS], ps[0:1, 6, 8:8 + ITEMS]).then_inc(S["item_sb"], 1)
            V.tensor_scalar(icnt[:, 0:1], ps[0:1, 6, 2:3], float(EXPERTS), None, ALU.add).then_inc(S["item_sb"], 1)
            dve.wait_ge(S["item_sb"], 4)
            count = dve.value_load(icnt[0:1, 0:1], min_val=EXPERTS, max_val=ITEMS)

            def weights_of(col, i):
                dve.wait_ge(S["pwT_up"], i)
                for t in range(TT):
                    for h in range(2):
                        last = V.tensor_scalar(pickw[:, t, h, CAP * h:CAP * h + CAP], slots, posI[:, t, bass.ds(col, 1)],
                                               wI[:, t, bass.ds(col, 1)], ALU.is_equal, ALU.mult)
                        last.then_inc(S["pickw_set" if t + h == 2 else "pickw_half"], 1)

            def add_item(i):
                for t in range(TT):
                    for h in range(2):
                        dve.wait_ge(S["comb_up"], i * 4 + (2 * t + h + 1))
                        if t + h == 0:
                            dve.wait_ge(S["comb_add"], i * 4)
                        V.tensor_tensor(acc[:, t, 512 * h:512 * h + 512], acc[:, t, 512 * h:512 * h + 512], ps[:, 6 + h, :],
                                        ALU.add).then_inc(S["comb_add"], 1)

            def item(i, first=False):
                dve.wait_ge(S["hg_up"], i + 1)
                choose(i + 1)
                if not first:
                    weights_of(i - 1, i)
                    add_item(i)
                dve.wait_ge(w_used, i * SLOTS + (PRE + GU_PIECES))
                V.tensor_scalar(gate, ps[:, 0, :], LIMIT, None, ALU.min).then_inc(S["gated"], 1)
                V.tensor_scalar(up, ps[:, 1, :], LIMIT, -LIMIT, ALU.min, ALU.max).then_inc(S["up_c"], 1)
                dve.wait_ge(S["sig_set"], i + 1)
                V.tensor_tensor(gate, gate, sig, ALU.mult).then_inc(S["gate_s"], 1)
                dve.wait_ge(S["gate_s"], i + 1)
                dve.wait_ge(S["up_c"], i + 1)
                V.scalar_tensor_tensor(act_, up, 1.0, gate, ALU.add, ALU.mult).then_inc(S["act_set"], 1)
                modulated(i + 2)
                dve.wait_ge(S["actT_up"], i + 1)
                expert_of(i + 1)

            item(0, first=True)
            with dve.Fori(1, EXPERTS) as i:
                item(i)
            with dve.If(count > EXPERTS):
                with dve.Fori(EXPERTS, ITEMS) as i:
                    with dve.If(i < count):
                        item(i)
            weights_of(count - 1, count)
            dve.wait_ge(S["comb_add"], count * 4)
            for t in range(TT):
                V.tensor_tensor(acc[:, t, :], acc[:, t, :], gate_ffn[:, :], ALU.mult).then_inc(S["ffn_gated"], 1)
            for t in range(TT):
                dve.wait_ge(S["ffn_gated"], t + 1)
                V.tensor_tensor(x_tok[:, t, :], x_tok[:, t, :], acc[:, t, :], ALU.add).then_inc(S["x_but_last"], 1)
            dve.wait_ge(S["x_but_last"], TT)
            for t in range(TT):
                for h in range(2):
                    n = 2 * t + h
                    c = slice(512 * h, 512 * h + 512)
                    dve.wait_ge(S["comb_up"], count * 4 + (n + 1))
                    V.tensor_tensor(acc[:, t, c], ps[:, 6 + h, :], gate_ffn[:, c], ALU.mult).then_inc(S["comb_add"], 1)
                    dve.wait_ge(S["comb_add"], count * 4 + (n + 1))
                    V.tensor_tensor(x_tok[:, t, c], x_tok[:, t, c], acc[:, t, c], ALU.add).then_inc(S["fin"], 1)
            for i in range(TT):
                dve.wait_ge(S["sq3"], i + 1)
                link(V.reciprocal(stat[:, 2, i:i + 1], stat[:, 1, i:i + 1]))
                V.scalar_tensor_tensor(x_tok[:, i, :], x_tok[:, i, :], stat[:, 2, i:i + 1], gfin, ALU.mult, ALU.mult).then_inc(S["fin_out"], 1)

    ctx.close()


_INS = ["x", "c", "w_ada", "b_ada", "g_mix", "w_in", "ssm_a_re", "ssm_a_im", "ssm_log_dt", "ssm_b_re", "ssm_b_im",
        "ssm_c_re", "ssm_c_im", "ssm_d", "w_glu", "w_attn_o", "w_out", "g_ffn", "w_router", "b_router", "w_gu", "b_gu",
        "w_down", "b_down", "g_final"]


def kernel(**inputs):
    from concourse import bacc
    from concourse.bass_utils import run_bass_kernel_spmd

    nc = bacc.Bacc("TRN2", target_bir_lowering=False, num_devices=1, dynamic_dma_scratch_size=1024)
    arrays = {f"in_{n}": np.ascontiguousarray(inputs[n]) for n in _INS}
    arrays["in_const"] = constants()
    args = [nc.dram_tensor(n, a.shape, F32, kind="ExternalInput").ap() for n, a in arrays.items()]
    out = nc.dram_tensor("out_0", (1, T, D), F32, kind="ExternalOutput").ap()
    build(nc, *args, out)
    r = run_bass_kernel_spmd(nc, [arrays], core_ids=[0])
    return r.results[0]["out_0"]
```
